# Optimizing a Trainium2 kernel written in Bass

```python
import math
import jax, jax.numpy as jnp
from jax import lax
import numpy as np

D_MODEL = 1024
BATCH = 1
SEQ = 256
DEPTH = 2

GRID_W = 64
CTX_LEN = 256
N_HEADS_A = 4
DH_A = 64
DV_A = 2 * DH_A
WIDTH_A = N_HEADS_A * DV_A
N_HEADS_B = 4
DK_B = 64
DV_B = 64
WIDTH_BK = N_HEADS_B * DK_B
WIDTH_B = N_HEADS_B * DV_B
FN_GROUPS = 4
FN_GROUP_DIM = 64
WIDTH_C = FN_GROUPS * FN_GROUP_DIM
MIX_WIDTH = WIDTH_A + WIDTH_B + WIDTH_C
PROJ_SIZES = (WIDTH_A, WIDTH_A, WIDTH_A, WIDTH_BK, WIDTH_BK, WIDTH_BK, WIDTH_B, WIDTH_B, WIDTH_C)
PROJ_WIDTH = 3 * WIDTH_A + 3 * WIDTH_BK + 2 * WIDTH_B + WIDTH_C
D_FF = 2816
CONV_W = 3
Q_BLOCK = 128
CHUNK = 64
ROPE_BASE = 10000.0
EPS = 1e-6


def rms_norm(x, w):
    xf = x.astype(jnp.float32)
    y = xf * lax.rsqrt(jnp.mean(xf * xf, axis=-1, keepdims=True) + EPS)
    return (y * w.astype(jnp.float32)).astype(x.dtype)

def modulate(h, shift, scale):
    return h * (1 + scale) + shift

def flip(a):
    return jnp.flip(a, axis=1)

def axial_rope(rows):
    pos_r = jnp.repeat(jnp.arange(rows), GRID_W).astype(jnp.float32)
    pos_c = jnp.tile(jnp.arange(GRID_W), rows).astype(jnp.float32)
    half = DH_A // 2
    inv_freq = ROPE_BASE ** (-jnp.arange(0, half, 2, dtype=jnp.float32) / half)
    ang_r = pos_r[:, None] * inv_freq
    ang_c = pos_c[:, None] * inv_freq
    ang = jnp.concatenate([ang_r, ang_r, ang_c, ang_c], axis=-1)
    return jnp.cos(ang), jnp.sin(ang)

def _rotate_half(p):
    h = p.shape[-1] // 2
    return jnp.concatenate([-p[..., h:], p[..., :h]], axis=-1)

def apply_axial_rope(t, cos, sin):
    t_row, t_col = jnp.split(t, 2, axis=-1)
    rot = jnp.concatenate([_rotate_half(t_row), _rotate_half(t_col)], axis=-1)
    cos = cos[None, :, None, None, :]
    sin = sin[None, :, None, None, :]
    return (t * cos + rot * sin).astype(t.dtype)

def diff_attend(q, k, v, lam):
    s = jnp.einsum('bqhcd,bkhcd->bhcqk', q, k).astype(jnp.float32) * (DH_A ** -0.5)
    p = jax.nn.softmax(s, axis=-1)
    a = p[:, :, 0] - lam * p[:, :, 1]
    return jnp.einsum('bhqk,bkhd->bqhd', a, v.astype(jnp.float32))

def diff_attend_blocks(q, k, v, lam):
    b, l = q.shape[:2]
    nb = l // Q_BLOCK
    qb = q.reshape(b, nb, Q_BLOCK, N_HEADS_A, 2, DH_A).transpose(1, 0, 2, 3, 4, 5)
    o = lax.map(lambda blk: diff_attend(blk, k, v, lam), qb)
    return o.transpose(1, 0, 2, 3, 4).reshape(b, l, N_HEADS_A, DV_A)

def diff_head_norm(o, w, lam_init):
    b, l = o.shape[:2]
    return (rms_norm(o, w) * (1.0 - lam_init)).reshape(b, l, WIDTH_A)

def log_forget(z, lb):
    zf = z.astype(jnp.float32)
    return jnp.logaddexp(jnp.log(lb), jnp.log1p(-lb) + jax.nn.log_sigmoid(zf))

def hgrn_scan(q, k, v, logf, s0):
    b, l, h, _ = q.shape
    dv = v.shape[-1]
    nc = l // CHUNK

    def chunks(a):
        return a.reshape(b, nc, CHUNK, h, a.shape[-1]).transpose(1, 0, 3, 2, 4)

    lower = jnp.tril(jnp.ones((CHUNK, CHUNK), dtype=bool))[:, :, None]

    def step(state, blk):
        qc, kc, vc, gc = blk
        cum = jnp.cumsum(gc, axis=2)
        rel = jnp.where(lower, cum[:, :, :, None, :] - cum[:, :, None, :, :], -jnp.inf)
        scores = jnp.einsum('bhtd,bhsd,bhtsd->bhts', qc, kc, jnp.exp(rel))
        o = (jnp.einsum('bhts,bhsv->bhtv', scores, vc)
             + jnp.einsum('bhtd,bhdv->bhtv', qc * jnp.exp(cum), state))
        cum_end = cum[:, :, -1:, :]
        state = (jnp.exp(cum_end)[:, :, 0, :, None] * state
                 + jnp.einsum('bhsd,bhsv->bhdv', kc * jnp.exp(cum_end - cum), vc))
        return state, o

    state, o = lax.scan(step, s0, (chunks(q), chunks(k), chunks(v), chunks(logf)))
    return o.transpose(1, 0, 3, 2, 4).reshape(b, l, h, dv), state

def hgrn_final_state(k, v, logf):
    tail = flip(jnp.cumsum(flip(logf), axis=1)) - logf
    return jnp.einsum('blhk,blhv->bhkv', k * jnp.exp(tail), v)

def hgrn_bidir(m, s_fwd, s_bwd):
    o_f, st_f = hgrn_scan(m['qh'], m['kf'], m['vh'], m['gf'], s_fwd)
    o_b, st_b = hgrn_scan(flip(m['qh']), flip(m['kb']), flip(m['vh']), flip(m['gb']), s_bwd)
    return o_f + flip(o_b), st_f, st_b

def hgrn_out(o, og, w):
    b, l = o.shape[:2]
    return (rms_norm(o, w) * jax.nn.silu(og.astype(jnp.float32))).reshape(b, l, WIDTH_B)

def fourier_mix(u, w):
    b, l, _ = u.shape
    ug = u.astype(jnp.float32).reshape(b, l, FN_GROUPS, FN_GROUP_DIM)
    y = jnp.fft.fft2(ug, axes=(1, 3), norm='ortho').real.reshape(b, l, WIDTH_C)
    return y.astype(u.dtype) @ w

def conv_ffn(h, w_up, conv_w, conv_b, w_down):
    u = h @ w_up
    up = jnp.pad(u, ((0, 0), (1, 1), (0, 0)))
    u = up[:, :-2] * conv_w[0] + up[:, 1:-1] * conv_w[1] + up[:, 2:] * conv_w[2] + conv_b
    gate, val = jnp.split(u, 2, axis=-1)
    return (jax.nn.silu(gate) * val) @ w_down

def unpack(p, lb):
    b, l, _ = p.shape
    idx = np.cumsum(PROJ_SIZES)[:-1].tolist()
    qa, ka, va, qh, zf, zb, ih, gh, uf = jnp.split(p, idx, axis=-1)
    gf = log_forget(zf, lb[0]).reshape(b, l, N_HEADS_B, DK_B)
    gb = log_forget(zb, lb[1]).reshape(b, l, N_HEADS_B, DK_B)
    return {
        'qa': qa.reshape(b, l, N_HEADS_A, 2, DH_A),
        'ka': ka.reshape(b, l, N_HEADS_A, 2, DH_A),
        'va': va.reshape(b, l, N_HEADS_A, DV_A),
        'qh': qh.reshape(b, l, N_HEADS_B, DK_B).astype(jnp.float32),
        'gf': gf, 'gb': gb,
        'kf': -jnp.expm1(gf), 'kb': -jnp.expm1(gb),
        'vh': ih.reshape(b, l, N_HEADS_B, DV_B).astype(jnp.float32),
        'og': gh.reshape(b, l, N_HEADS_B, DV_B),
        'uf': uf,
    }

def merge(att, rec, four, w_out, dt):
    return jnp.concatenate([att.astype(dt), rec.astype(dt), four.astype(dt)], axis=-1) @ w_out

def first_inputs(seed: int = 0) -> dict:
    key = jax.random.key(seed)
    ks = jax.random.split(key, 20)
    f32 = jnp.float32

    def nrm(k, shape, s):
        return s * jax.random.normal(k, shape, f32)

    return {
        'x': nrm(ks[0], (BATCH, SEQ, D_MODEL), 1.0),
        'c': nrm(ks[1], (BATCH, D_MODEL), 1.0),
        'ctx': nrm(ks[2], (BATCH, CTX_LEN, D_MODEL), 1.0),
        'c_ctx': nrm(ks[3], (D_MODEL,), 1.0),
        'w_ada': nrm(ks[4], (DEPTH, D_MODEL, 6 * D_MODEL), 0.5 * D_MODEL ** -0.5),
        'b_ada': nrm(ks[5], (DEPTH, 6 * D_MODEL), 0.02),
        'norm1_w': 1.0 + nrm(ks[6], (DEPTH, D_MODEL), 0.05),
        'norm2_w': 1.0 + nrm(ks[7], (DEPTH, D_MODEL), 0.05),
        'w_in': nrm(ks[8], (DEPTH, D_MODEL, PROJ_WIDTH), D_MODEL ** -0.5),
        'lam_qk': nrm(ks[9], (DEPTH, 4, DH_A), 0.1),
        'subln_w': 1.0 + nrm(ks[10], (DEPTH, DV_A), 0.05),
        'lb_param': nrm(ks[11], (DEPTH, 2, WIDTH_BK), 0.5),
        'hgrn_norm_w': 1.0 + nrm(ks[12], (DEPTH, DV_B), 0.05),
        'w_fnet': nrm(ks[13], (DEPTH, WIDTH_C, WIDTH_C), WIDTH_C ** -0.5),
        'w_out': nrm(ks[14], (DEPTH, MIX_WIDTH, D_MODEL), MIX_WIDTH ** -0.5),
        'w_up': nrm(ks[15], (DEPTH, D_MODEL, 2 * D_FF), D_MODEL ** -0.5),
        'conv_w': jnp.array([0.0, 1.0, 0.0], f32)[None, :, None] + nrm(ks[16], (DEPTH, CONV_W, 2 * D_FF), 0.2),
        'conv_b': nrm(ks[17], (DEPTH, 2 * D_FF), 0.02),
        'w_down': nrm(ks[18], (DEPTH, D_FF, D_MODEL), D_FF ** -0.5),
        'final_norm_w': 1.0 + nrm(ks[19], (D_MODEL,), 0.05),
    }

def first_block(x, c, ctx, c_ctx, w_ada, b_ada, norm1_w, norm2_w, w_in, lam_qk, subln_w,
              lb_param, hgrn_norm_w, w_fnet, w_out, w_up, conv_w, conv_b, w_down, final_norm_w):
    b, l, _ = x.shape
    rows = l // GRID_W
    cos, sin = axial_rope(rows)
    lb_all = jnp.cumsum(jax.nn.softmax(lb_param.astype(jnp.float32), axis=0), axis=0)
    lb_all = lb_all - lb_all[0:1]
    c_act = jax.nn.silu(c)
    cc_act = jax.nn.silu(c_ctx)
    xc = ctx
    for li in range(DEPTH):
        last = li == DEPTH - 1
        dt = x.dtype
        mod = c_act @ w_ada[li] + b_ada[li]
        sh1, sc1, g1, sh2, sc2, g2 = jnp.split(mod[:, None, :], 6, axis=-1)
        mod_c = cc_act @ w_ada[li] + b_ada[li]
        sh1c, sc1c, g1c, sh2c, sc2c, g2c = jnp.split(mod_c[None, None, :], 6, axis=-1)
        lam_init = 0.8 - 0.6 * math.exp(-0.3 * li)
        lq1, lk1, lq2, lk2 = lam_qk[li].astype(jnp.float32)
        lam = jnp.exp(jnp.sum(lq1 * lk1)) - jnp.exp(jnp.sum(lq2 * lk2)) + lam_init

        m = unpack(modulate(rms_norm(x, norm1_w[li]), sh1, sc1) @ w_in[li], lb_all[li])
        mc = unpack(modulate(rms_norm(xc, norm1_w[li]), sh1c, sc1c) @ w_in[li], lb_all[li])

        k_all = jnp.concatenate([mc['ka'], apply_axial_rope(m['ka'], cos, sin)], axis=1)
        v_all = jnp.concatenate([mc['va'], m['va']], axis=1)
        att = diff_head_norm(diff_attend_blocks(apply_axial_rope(m['qa'], cos, sin), k_all, v_all, lam),
                             subln_w[li], lam_init)

        if last:
            s_f = hgrn_final_state(mc['kf'], mc['vh'], mc['gf'])
            s_b = hgrn_final_state(flip(mc['kb']), flip(mc['vh']), flip(mc['gb']))
        else:
            zeros = jnp.zeros((xc.shape[0], N_HEADS_B, DK_B, DV_B), jnp.float32)
            o_c, s_f, s_b = hgrn_bidir(mc, zeros, zeros)
        o_l, _, _ = hgrn_bidir(m, s_f, s_b)
        rec = hgrn_out(o_l, m['og'], hgrn_norm_w[li])

        four = fourier_mix(m['uf'], w_fnet[li])

        x = x + g1 * merge(att, rec, four, w_out[li], dt)
        x = x + g2 * conv_ffn(modulate(rms_norm(x, norm2_w[li]), sh2, sc2),
                              w_up[li], conv_w[li], conv_b[li], w_down[li])

        if not last:
            att_c = diff_head_norm(diff_attend(mc['qa'], mc['ka'], mc['va'], lam), subln_w[li], lam_init)
            rec_c = hgrn_out(o_c, mc['og'], hgrn_norm_w[li])
            four_c = fourier_mix(mc['uf'], w_fnet[li])
            xc = xc + g1c * merge(att_c, rec_c, four_c, w_out[li], dt)
            xc = xc + g2c * conv_ffn(modulate(rms_norm(xc, norm2_w[li]), sh2c, sc2c),
                                     w_up[li], conv_w[li], conv_b[li], w_down[li])
    return rms_norm(x, final_norm_w)


N_MIXERS = 2
CONV_EXPAND = 2
CONV_WIDTH = D_MODEL * CONV_EXPAND
CONV_K = 3
HEAD_DIM = 64
HEADS_PER_GROUP = D_MODEL // HEAD_DIM
DILATED_GROUPS = ((128, 1), (512, 4), (2048, 16))
N_GROUPS = len(DILATED_GROUPS)
ATTN_WIDTH = HEADS_PER_GROUP * HEAD_DIM
QKV_COLS = N_GROUPS * 3 * ATTN_WIDTH
BLOCK = 128
N_BUCKETS = 32
MAX_DISTANCE = 2048
N_CONV_LAYERS = (DEPTH + 1) // 2
N_ATTN_LAYERS = DEPTH // 2


def rms_norm_2(x, g):
    xf = x.astype(jnp.float32)
    y = xf * lax.rsqrt(jnp.mean(xf * xf, axis=-1, keepdims=True) + EPS)
    return (y * g.astype(jnp.float32)).astype(x.dtype)

def t5_bucket(dist):
    max_exact = N_BUCKETS // 2
    d = jnp.maximum(dist, 1).astype(jnp.float32)
    large = max_exact + (jnp.log(d / max_exact) / math.log(MAX_DISTANCE / max_exact)
                         * (N_BUCKETS - max_exact)).astype(jnp.int32)
    large = jnp.minimum(large, N_BUCKETS - 1)
    return jnp.where(dist < max_exact, dist, large)

def short_conv_mixer(h, w_in, w_conv, w_out):
    S = h.shape[1]
    proj = h @ w_in
    b_gate, c_gate, u, z = jnp.split(proj, 4, axis=-1)
    v = c_gate * u
    vp = jnp.pad(v, ((0, 0), (CONV_K - 1, 0), (0, 0)))
    conv = sum(w_conv[k] * vp[:, k:k + S] for k in range(CONV_K))
    y = b_gate * conv * jax.nn.silu(z)
    return y @ w_out

def dilated_group_attention(q, k, v, bias_tab, window, dilation):
    B, S, H, Dh = q.shape
    L = S // dilation
    nb = -(-L // BLOCK)
    Lp = nb * BLOCK
    span = window // dilation

    def to_sub(t):
        t = t.reshape(B, L, dilation, H, Dh).transpose(0, 2, 3, 1, 4)
        t = jnp.pad(t, ((0, 0), (0, 0), (0, 0), (0, Lp - L), (0, 0)))
        return t.reshape(B, dilation, H, nb, BLOCK, Dh)

    def band(t):
        prev = jnp.pad(t, ((0, 0), (0, 0), (0, 0), (1, 0), (0, 0), (0, 0)))[:, :, :, :-1]
        return jnp.concatenate([prev, t], axis=4)

    qs = to_sub(q)
    kb = band(to_sub(k))
    vb = band(to_sub(v))
    logits = jnp.einsum('brhnqd,brhnkd->brhnqk', qs, kb).astype(jnp.float32) * (HEAD_DIM ** -0.5)

    a = jnp.arange(BLOCK)[:, None]
    kk = jnp.arange(2 * BLOCK)[None, :]
    step = BLOCK + a - kk
    blk = jnp.arange(nb)[:, None, None]
    key_pos = (blk - 1) * BLOCK + kk[None]
    valid = (step >= 0) & (step <= span) & (key_pos >= 0)
    bucket = t5_bucket(jnp.clip(step, 0, span) * dilation)
    bias = bias_tab.astype(jnp.float32)[bucket].transpose(2, 0, 1)[:, None]

    logits = jnp.where(valid, logits + bias, -jnp.inf)
    lse = jax.nn.logsumexp(logits, axis=-1)
    probs = jnp.exp(logits - lse[..., None])
    out = jnp.einsum('brhnqk,brhnkd->brhnqd', probs.astype(v.dtype), vb)

    out = out.reshape(B, dilation, H, Lp, Dh)[:, :, :, :L]
    out = out.transpose(0, 3, 1, 2, 4).reshape(B, S, H, Dh)
    lse = lse.reshape(B, dilation, H, Lp)[:, :, :, :L]
    lse = lse.transpose(0, 3, 1, 2).reshape(B, S, H)
    return out, lse

def dilated_attention_mixer(h, w_in, q_gain, k_gain, w_out, rel_bias):
    B, S, _ = h.shape
    proj = h @ w_in
    qkv = proj[..., :QKV_COLS].reshape(B, S, N_GROUPS, 3, HEADS_PER_GROUP, HEAD_DIM)
    z = proj[..., QKV_COLS:]
    outs, lses = [], []
    for g, (window, dilation) in enumerate(DILATED_GROUPS):
        q = rms_norm_2(qkv[:, :, g, 0], q_gain[g])
        k = rms_norm_2(qkv[:, :, g, 1], k_gain[g])
        bias_g = rel_bias[:, g * HEADS_PER_GROUP:(g + 1) * HEADS_PER_GROUP]
        o, l = dilated_group_attention(q, k, qkv[:, :, g, 2], bias_g, window, dilation)
        outs.append(o)
        lses.append(l)
    alpha = jax.nn.softmax(jnp.stack(lses, axis=0), axis=0)
    o = jnp.sum(alpha[..., None] * jnp.stack(outs, axis=0).astype(jnp.float32), axis=0)
    y = o.reshape(B, S, ATTN_WIDTH).astype(h.dtype) * jax.nn.silu(z)
    return y @ w_out

def second_inputs(seed: int = 0) -> dict:
    key = jax.random.key(seed)
    ks = jax.random.split(key, 12)
    f32 = jnp.float32
    nc, na = N_CONV_LAYERS, N_ATTN_LAYERS
    x = jax.random.normal(ks[0], (BATCH, SEQ, D_MODEL), f32)
    conv_norm = 1.0 + 0.1 * jax.random.normal(ks[1], (nc, D_MODEL), f32)
    conv_w_in = jax.random.normal(ks[2], (nc, D_MODEL, 4 * CONV_WIDTH), f32) * D_MODEL ** -0.5
    conv_w = jax.random.normal(ks[3], (nc, CONV_K, CONV_WIDTH), f32) * CONV_K ** -0.5
    conv_w_out = jax.random.normal(ks[4], (nc, CONV_WIDTH, D_MODEL), f32) * CONV_WIDTH ** -0.5
    attn_norm = 1.0 + 0.1 * jax.random.normal(ks[5], (na, D_MODEL), f32)
    attn_w_in = jax.random.normal(ks[6], (na, D_MODEL, QKV_COLS + ATTN_WIDTH), f32) * D_MODEL ** -0.5
    attn_q_gain = 1.0 + 0.1 * jax.random.normal(ks[7], (na, N_GROUPS, HEAD_DIM), f32)
    attn_k_gain = 1.0 + 0.1 * jax.random.normal(ks[8], (na, N_GROUPS, HEAD_DIM), f32)
    attn_w_out = jax.random.normal(ks[9], (na, ATTN_WIDTH, D_MODEL), f32) * ATTN_WIDTH ** -0.5
    rel_bias = 0.5 * jax.random.normal(ks[10], (N_BUCKETS, N_GROUPS * HEADS_PER_GROUP), f32)
    return {"x": x, "conv_norm": conv_norm, "conv_w_in": conv_w_in, "conv_w": conv_w,
            "conv_w_out": conv_w_out, "attn_norm": attn_norm, "attn_w_in": attn_w_in,
            "attn_q_gain": attn_q_gain, "attn_k_gain": attn_k_gain, "attn_w_out": attn_w_out,
            "rel_bias": rel_bias}

def second_block(x, conv_norm, conv_w_in, conv_w, conv_w_out, attn_norm, attn_w_in,
              attn_q_gain, attn_k_gain, attn_w_out, rel_bias):
    for i in range(DEPTH):
        j = i // N_MIXERS
        if i % N_MIXERS == 0:
            h = rms_norm_2(x, conv_norm[j])
            x = x + short_conv_mixer(h, conv_w_in[j], conv_w[j], conv_w_out[j])
        else:
            h = rms_norm_2(x, attn_norm[j])
            x = x + dilated_attention_mixer(h, attn_w_in[j], attn_q_gain[j], attn_k_gain[j],
                                            attn_w_out[j], rel_bias)
    return x


def setup_inputs(seed=0):
    out = dict(first_inputs(seed))
    for name, value in second_inputs(seed + 1).items():
        if name != "x":
            out[name + "_2"] = value
    return out


def reference(
    x, c, ctx, c_ctx, w_ada, b_ada, norm1_w, norm2_w, w_in, lam_qk, subln_w, lb_param,
    hgrn_norm_w, w_fnet, w_out, w_up, conv_w, conv_b, w_down, final_norm_w, conv_norm_2,
    conv_w_in_2, conv_w_2, conv_w_out_2, attn_norm_2, attn_w_in_2, attn_q_gain_2, attn_k_gain_2,
    attn_w_out_2, rel_bias_2,
):
    x = first_block(
        x, c, ctx, c_ctx, w_ada, b_ada, norm1_w, norm2_w, w_in, lam_qk, subln_w, lb_param,
        hgrn_norm_w, w_fnet, w_out, w_up, conv_w, conv_b, w_down, final_norm_w,
    )
    return second_block(
        x, conv_norm_2, conv_w_in_2, conv_w_2, conv_w_out_2, attn_norm_2, attn_w_in_2,
        attn_q_gain_2, attn_k_gain_2, attn_w_out_2, rel_bias_2,
    )


_drawn_inputs = setup_inputs


def setup_inputs(seed=0):
    import zlib

    import numpy as np

    out = dict(_drawn_inputs(seed))
    spreads = {}
    factors = {'lam_qk': 4.407,
     'subln_w': 3.04,
     'hgrn_norm_w': 6.316,
     'conv_b': 4.745,
     'attn_norm_2': 2.802,
     'attn_q_gain_2': 6.793,
     'attn_k_gain_2': 6.529}
    for name, (base, spread) in spreads.items():
        noise = np.random.default_rng([zlib.crc32(name.encode()), seed]).standard_normal(out[name].shape)
        drawn = base * np.exp(spread * noise) if base else spread * noise
        out[name] = __import__('jax').numpy.asarray(drawn.astype(out[name].dtype))
    for name, factor in factors.items():
        out[name] = (out[name] * factor).astype(out[name].dtype)
    return out
```

```python
import math
from contextlib import ExitStack

import numpy as np

import concourse.bass as bass
from concourse import mybir

F32 = mybir.dt.float32
U8 = mybir.dt.uint8
ALU = mybir.AluOpType
ACT = mybir.ActivationFunctionType
AX = mybir.AxisListType

P = 128
DM = 1024
KT = DM // P
SEQ = 256
NT = 4
DEPTH = 2
EPS = 1e-6
NH_A = 4
DFF = 2816
FT = DFF // P
CEXP = 2048
ET = CEXP // P
NG = 3
NH = 16
LEVELS = 8
BANKS = 8
SLOTS = 3
SLOT = KT * 512
NEG = -1.0e30


def level_block(level):
    return 2 ** (level - 1)


def scan_matrices():
    u, tau = np.arange(P)[:, None], np.arange(P)[None, :]
    out = np.zeros((P, 2, 9, P), np.float32)
    for level in range(1, LEVELS):
        b = level_block(level)
        mid = tau // (2 * b) * 2 * b + b
        out[:, 0, level - 1] = np.where(tau >= mid, (u >= mid) & (u <= tau), (u > tau) & (u < mid))
        out[:, 1, level - 1] = np.where(tau < mid, (u >= tau) & (u < mid), (u >= mid) & (u < tau))
    out[:, 0, 7], out[:, 1, 7] = u <= tau, u >= tau
    out[:, 0, 8], out[:, 1, 8] = u > tau, u < tau
    return out.reshape(P, -1)


def level_masks():
    s, t = np.arange(P)[:, None], np.arange(P)[None, :]
    out = np.zeros((P, 2, LEVELS, P), np.float32)
    out[:, 0, 0] = out[:, 1, 0] = s == t
    for level in range(1, LEVELS):
        b = level_block(level)
        same = s // (2 * b) == t // (2 * b)
        out[:, 0, level] = same & (s // b % 2 == 0) & (t // b % 2 == 1)
        out[:, 1, level] = same & (s // b % 2 == 1) & (t // b % 2 == 0)
    return out.reshape(P, -1)


def rope_tables():
    pos = np.arange(SEQ)
    half = 32
    inv = (np.float32(10000.0) ** (-np.arange(0, half, 2, dtype=np.float32) / half)).astype(np.float32)
    ar = (pos // 64).astype(np.float32)[:, None] * inv
    ac = (pos % 64).astype(np.float32)[:, None] * inv
    ang = np.concatenate([ar, ar, ac, ac], axis=-1).T
    ang = np.concatenate([ang, ang], axis=0)
    return np.cos(ang).astype(np.float32), np.sin(ang).astype(np.float32)


def rotate_matrix():
    r = np.zeros((P, P), np.float32)
    for base in range(0, P, 32):
        for m in range(16):
            r[base + m + 16, base + m] = -1.0
            r[base + m, base + m + 16] = 1.0
    return r


def t5_bucket(dist):
    d = np.maximum(dist, 1).astype(np.float32)
    large = 16 + (np.log(d / np.float32(16)) / np.float32(math.log(2048 / 16)) * np.float32(16)).astype(np.int32)
    return np.where(dist < 16, dist, np.minimum(large, 31))


def constants():
    ident = np.eye(P, dtype=np.float32)
    k = np.arange(SEQ, dtype=np.float64)
    ang = 2 * np.pi * (np.outer(k, k) % SEQ) / SEQ
    scale = 1.0 / math.sqrt(SEQ * 64)
    both = np.concatenate([np.cos(ang), np.sin(ang)], axis=1) * scale
    dft_seq = both.reshape(2, P, 512).transpose(1, 0, 2).reshape(P, -1).astype(np.float32)
    d = np.arange(64, dtype=np.float64)
    ang = 2 * np.pi * (np.outer(d, d) % 64) / 64
    two = np.eye(2)
    dft_cos = np.kron(two, np.cos(ang)).astype(np.float32)
    dft_sin = np.kron(two, -np.sin(ang)).astype(np.float32)
    cos, sin = rope_tables()
    sel = np.zeros((P, 2, P), np.float32)
    sel[0, 0], sel[1, 1] = 1.0, 1.0
    means = np.kron(two, np.ones((64, 64))).astype(np.float32)
    wide = np.concatenate([ident, ident[::-1], sel.reshape(P, -1), means, dft_seq, dft_cos, dft_sin, rotate_matrix(), cos, sin,
                           scan_matrices()], axis=1)
    dist = 255 - np.arange(384)
    hot = np.zeros((32 + NG, 384), np.float32)
    tab = np.zeros((NG, NG * NH), np.float32)
    bucket = t5_bucket(np.maximum(dist, 0))
    for m in range(384):
        hot[bucket[m], m] = 1.0
    for g, dil in enumerate((1, 4, 16)):
        hot[32 + g] = ~((dist >= 0) & (dist % dil == 0) & (dist // dil <= 128))
        tab[g, g * NH:(g + 1) * NH] = NEG
    return np.ascontiguousarray(wide), level_masks(), hot, tab


class Signal:

    def __init__(self, sem, keys):
        self.sem = sem
        self.count = {k: i + 1 for i, k in enumerate(keys)}

    def after(self, key):
        return self.count[key]


class Line:

    def __init__(self):
        self.n = 0

    def one(self):
        self.n += 1
        return 1


def program(nc, A, wide_c, mask_c, hot_c, tab_c, out):
    ctx = ExitStack()

    def sb(name, cols, dt=F32, rows=P):
        return ctx.enter_context(nc.sbuf_tensor(name, [rows, cols], dt))

    def sem(name):
        return ctx.enter_context(nc.semaphore(name))

    with ctx:
        ring = sb("weight_ring", SLOTS * SLOT)
        res = sb("residual", NT * DM)
        ht_r = sb("normed_t", KT * 512)
        arena = sb("arena", 12288)
        mg = sb("merge_and_gates", 8192)
        scr = sb("scratch", 3840)
        wide = sb("wide_consts", 128 * 4 + 128 + 1024 + 256 + 128 + 512 + 2304)
        masks = sb("level_masks_sb", 2 * LEVELS * P, U8)
        cols = sb("param_columns", 640)
        lbs = sb("log_bounds", 1024)
        small = sb("small", 600)
        grow = sb("gate_row", 512, rows=2)
        ps = ctx.enter_context(nc.psum_tensor("acc", [P, BANKS, 512], F32))

        RES = res[:, :].rearrange("p (t n) -> p t n", t=NT)
        HT = ht_r[:, :].rearrange("p (k n) -> p k n", k=KT)
        HT2 = ht_r[:, 0:KT * SEQ].rearrange("p (k n) -> p k n", k=KT)
        MT = mg[:, 0:4096].rearrange("p (k n) -> p k n", k=8)
        XS = mg[:, 0:4096].rearrange("p (t n) -> p t n", t=NT)
        GB = mg[:, 4096:8192].rearrange("p (g s n) -> p g s n", g=2, s=2)
        KTOK = mg[:, 6144:8192].rearrange("p (t n) -> p t n", t=NT)
        OREC = mg[:, 2048:3072].rearrange("p (t n) -> p t n", t=NT)
        V2 = mg[:, 0:6144].rearrange("p (g t n) -> p g t n", g=NG, t=2)
        ZS = mg[:, 6144:8192].rearrange("p (k n) -> p k n", k=KT)
        VA = arena[:, 0:2048].rearrange("p (t n) -> p t n", t=NT)
        GL = arena[:, 2048:4096].rearrange("p (t n) -> p t n", t=NT)
        IH = arena[:, 4096:5120].rearrange("p (t n) -> p t n", t=NT)
        GH = arena[:, 5120:6144].rearrange("p (t n) -> p t n", t=NT)
        UF = arena[:, 6144:7168].rearrange("p (t n) -> p t n", t=NT)
        QA = arena[:, 7168:9216].rearrange("p (h n) -> p h n", h=NH_A)
        KA = arena[:, 9216:11264].rearrange("p (h n) -> p h n", h=NH_A)
        QH = arena[:, 11264:12288].rearrange("p (k n) -> p k n", k=2)
        HF = arena[:, 0:FT * 512].rearrange("p (f n) -> p f n", f=FT)
        YC = arena[:, 0:ET * SEQ].rearrange("p (f n) -> p f n", f=ET)
        QK2 = arena[:, :].rearrange("p (g a h n) -> p g a h n", g=NG, a=2, h=8)
        at = [0]

        def part(t, n, pos=at):
            pos[0] += n
            return t[:, pos[0] - n:pos[0]]

        ident = part(wide, 128)
        flip = part(wide, 128)
        sel = part(wide, 256).rearrange("p (s n) -> p s n", s=2)
        means = part(wide, 128)
        dft_seq = part(wide, 1024).rearrange("p (k n) -> p k n", k=2)
        dft_cos, dft_sin, rot = part(wide, 128), part(wide, 128), part(wide, 128)
        cosT, sinT = part(wide, 256), part(wide, 256)
        m0 = at[0]
        SM = part(wide, 2304).rearrange("p (d l n) -> p d l n", d=2, l=9)
        BIAS = wide[:, m0:m0 + 2304].rearrange("p (b g n) -> p b g n", b=3, g=NG)
        MASK = masks[:, :].rearrange("p (d l n) -> p d l n", d=2, l=LEVELS)
        pos = [0]

        def sm(n):
            return part(small, n, pos)

        ssq, rstd, EPS_COL = sm(4), sm(4), sm(1)
        modt = sm(128).rearrange("p (l m k s) -> p l m k s", l=2, m=4, k=KT)
        csil = sm(16).rearrange("p (s k) -> p s k", s=2)
        nscale = sm(16).rearrange("p (k s) -> p k s", k=KT)
        hw = sm(128).rearrange("p (l n) -> p l n", l=2)
        lam2 = sm(4).rearrange("p (l a) -> p l a", l=2)
        neglam = sm(2)
        amax = sm(4).rearrange("p (b c) -> p b c", b=2)
        asum = sm(4).rearrange("p (b c) -> p b c", b=2)
        arec = sm(4).rearrange("p (b c) -> p b c", b=2)
        ossq, orstd = sm(2), sm(2)
        hssq, hrstd = sm(16).rearrange("p (t h) -> p t h", t=4), sm(16).rearrange("p (t h) -> p t h", t=4)
        bred, bmax, bsum, brec = sm(2), sm(2), sm(2), sm(2)
        rows = scr[:, 0:640].rearrange("p (c n) -> p c n", c=5)
        lam_rows = scr[:, 640:1152].rearrange("p (l a n) -> p l a n", l=2, a=4)
        lam_tmp = scr[:, 1152:1216]
        lb_rows = scr[:, 1280:2304].rearrange("p (l n) -> p l n", l=2)
        lb_t = scr[:, 2304:3328].rearrange("p (l n) -> p l n", l=2)
        XE = [scr[:, 0:2048].rearrange("p (q l n) -> p q l n", q=2, l=8),
              ht_r[:, 0:2048].rearrange("p (q l n) -> p q l n", q=2, l=8)]
        KTT = scr[:, 2048:2560].rearrange("p (b q n) -> p b q n", b=2, q=2)
        ACC = scr[:, 2560:3584].rearrange("p (d a h n) -> p d a h n", d=2, a=2, h=2)
        ST = scr[:, 3584:3840].rearrange("p (d q n) -> p d q n", d=2, q=2)
        SE = ht_r[:, 2048:2568].rearrange("p (b n) -> p b n", b=2)
        KD = ht_r[:, 2568:3080].rearrange("p (b n) -> p b n", b=2)
        gate_t = scr[:, 0:1536].rearrange("p (a n) -> p a n", a=3)
        rope_t = scr[:, 1536:2048].rearrange("p (b n) -> p b n", b=2)
        FS = ht_r[:, 0:1024].rearrange("p (f n) -> p f n", f=2)
        YT4 = ht_r[:, 1024:1536].rearrange("p (f n) -> p f n", f=2)
        wf = ht_r[:, 3584:4096].rearrange("p (f n) -> p f n", f=2)
        E2 = ht_r[:, 0:2048].rearrange("p (b c n) -> p b c n", b=2, c=2)
        AT = ht_r[:, 2048:3072].rearrange("p (b n) -> p b n", b=2)
        ON = ht_r[:, 3072:3328].rearrange("p (b n) -> p b n", b=2)
        wo_t = scr[:, 0:1024].rearrange("p (b n) -> p b n", b=2)
        FC = scr[:, 0:3072].rearrange("p (b a n) -> p b a n", b=2, a=3)
        CC = scr[:, 0:2048].rearrange("p (b a n) -> p b a n", b=2, a=4)
        SQ = scr[:, 0:1024].rearrange("p (b n) -> p b n", b=2)
        RQ = scr[:, 1024:2048].rearrange("p (b n) -> p b n", b=2)
        LG = scr[:, 0:1536].rearrange("p (b g n) -> p b g n", b=2, g=NG)
        E3 = scr[:, 1536:3072].rearrange("p (b n) -> p b n", b=2)
        Y2 = ht_r[:, 0:2048].rearrange("p (t n) -> p t n", t=2)
        YT2 = ht_r[:, 2048:4096].rearrange("p (k n) -> p k n", k=KT)
        hot = res[0:32 + NG, 0:384]
        tabx = res[0:32 + NG, 384:384 + NG * NH]
        vec = res[0:NG * NH, 512:512 + 384]
        vec_d = nc.dram_tensor("bias_rows", [NG * NH, 384], F32, kind="Internal").ap()

        slot_in = [sem(f"slot_in{i}") for i in range(SLOTS)]
        slot_part = sem("slot_read_part_way")
        read_at, parts_read = [], [0]
        full = sem("psum_full")
        taken = [sem(f"psum_taken{i}") for i in range(BANKS)]
        s_in, s_const = sem("residual_in"), sem("constants_in")
        s_small, s_eps, s_mask = sem("small_in"), sem("eps_ready"), sem("masks_ready")
        s_lb = sem("bounds_in")
        s_wf = sem("fnet_in")
        s_gb = sem("gate_bias_in")
        s_fw = sem("final_weight_in")
        s_vec = sem("bias_rows_out")
        s_hot = sem("hot_in")
        s_bias = [sem(f"bias_in{i}") for i in range(3)]
        s_out = sem("result_out")
        vector_step, scalar_step = sem("vector_step"), sem("scalar_step")

        def S(name, keys):
            return Signal(sem(name), keys)

        NORMS = [("n1", 0), ("n2", 0), ("n1", 1), ("n2", 1), ("fn", 0), ("cn", 0), ("an", 0)]

        def norm_tiles(N):
            return range(NT) if N in (("n1", 0), ("n2", 0), ("n1", 1)) else range(2, NT)

        nk = [(N, t) for N in NORMS for t in norm_tiles(N)]
        squared = S("row_scale", nk)
        scaled = S("scaled", [k for k in nk if k[0] != ("fn", 0)])
        res_new = S("residual_new", [("w_out", 0), ("w_down", 0), ("w_out", 1), ("w_down", 1), ("final", 0)])
        c_ready = sem("c_ready")
        lam_sum, lam_exp = sem("lam_sum"), sem("lam_exp")
        lb_abs, lb_exp = sem("lb_difference"), sem("lb_logs")
        gate_keys = [(li, t) for li in range(DEPTH) for t in range(NT)]
        z_soft = S("z_softplus", gate_keys)
        b_gap = S("bound_gap", [k for k in gate_keys if k[0]])
        b_soft = S("bound_softplus", [k for k in gate_keys if k[0]])
        g_ready = S("g_ready", gate_keys)
        k_ready = S("k_ready", gate_keys)

        def units(li):
            out_ = []
            for f, b in ((0, 1), (1, 0), (2, 3), (3, 2)):
                out_ += [(0, f), (1, b)]
            return out_

        UN = [(li, i) for li in range(DEPTH) for i in range(8)]

        def is_full(li, i):
            return li == 0 or i >= 4

        z_ready = S("z_ready", [u for u in UN if is_full(*u)])
        kd_ready = S("kd_ready", [u for u in UN if u[1] < 6])
        rec_keys = [(li, t) for li in range(DEPTH) for t in (range(NT) if li == 0 else range(2, NT))]
        rec_sum = S("rec_sum", rec_keys)
        og_exp = S("og_exp", rec_keys)
        rec_ready = S("rec_ready", rec_keys)

        def att_units(li):
            return [(t, h) for t in (range(NT) if li == 0 else range(2, NT)) for h in range(NH_A)]

        AU = [(li, u) for li in range(DEPTH) for u in range(len(att_units(li)))]
        a_max = S("a_max", AU)
        a_exp = S("a_exp", AU)
        a_ready = S("a_ready", AU)
        o_sq = S("o_scale", AU)
        FK = [(li, f) for li in range(DEPTH) for f in range(FT)]
        f_mid = S("ff_centre", FK)
        f_exp = S("ff_silu", FK)
        f_out = S("ff_product", FK)
        CK = list(range(ET))
        c_copy = S("conv_gate_copied", CK)
        c_z = S("conv_z_silu", CK)
        c_out = S("conv_product", CK)
        QKEYS = [(g, a, j) for g in range(NG) for a in range(2) for j in range(4)]
        q_sq = S("qk_squared", QKEYS)
        q_rs = S("qk_scale", QKEYS)
        zk = [(c, t) for c in range(2) for t in range(2)]
        BU = [(h, t) for h in range(NH) for t in range(2)]
        b_max = S("b_max", BU)
        b_exp = S("b_exp", BU)

        col_loads = []
        ncol = [0]

        def column(rows_ap, n, halves=False):
            c0 = ncol[0]
            ncol[0] += n
            done = 0
            while done < n:
                c, r = divmod(c0 + done, P)
                m = min(n - done, P - r)
                col_loads.append((rows_ap[done:done + m, :], c, r, m, halves))
                done += m
            return c0

        def as_rows(ap):
            return ap.rearrange("(r n) -> r n", n=P)

        col = {"c": column(as_rows(A["c"].rearrange("a n -> (a n)")), 8), "cc": column(as_rows(A["c_ctx"]), 8)}
        for li in range(DEPTH):
            col["b_ada", li] = column(as_rows(A["b_ada"][li, :]), 48)
            col["n1", li] = column(as_rows(A["norm1_w"][li, :]), 8)
            col["n2", li] = column(as_rows(A["norm2_w"][li, :]), 8)
            col["subln", li] = column(A["subln_w"][li:li + 1, :], 1)
            for j in range(3):
                col["cw", li, j] = column(as_rows(A["conv_w"][li, j, :]), 2 * FT)
            col["cb", li] = column(as_rows(A["conv_b"][li, :]), 2 * FT)
        col["cn", 0] = column(as_rows(A["conv_norm_2"][0, :]), 8)
        col["an", 0] = column(as_rows(A["attn_norm_2"][0, :]), 8)
        for j in range(3):
            col["cw2", j] = column(as_rows(A["conv_w_2"][0, j, :]), ET)
        col["gain", 0] = column(A["attn_q_gain_2"][0, :, :], NG, True)
        col["gain", 1] = column(A["attn_k_gain_2"][0, :, :], NG, True)
        NCOL = ncol[0]
        assert NCOL <= 640
        small_ins = [(lam_rows.rearrange("p l a n -> p (l a n)"), A["lam_qk"].rearrange("l a n -> (l a n)").partition_broadcast(P)),
                     (hw.rearrange("p l n -> p (l n)"), A["hgrn_norm_w"].rearrange("l n -> (l n)").partition_broadcast(P))]
        for src, c, r, m, halves in col_loads:
            if halves:
                small_ins += [(rows[r:r + m, c, 0:64], src), (rows[r:r + m, c, 64:128], src)]
            else:
                small_ins.append((rows[r:r + m, c, :], src))

        def pcol(key, j=0):
            return cols[:, col[key] + j:col[key] + j + 1]

        def kview(w, c0, n=512):
            return w[:, c0:c0 + n].rearrange("(k p) n -> p k n", p=P)

        def slot(n):
            return ring[:, (n % SLOTS) * SLOT:(n % SLOTS + 1) * SLOT]

        plan = []

        def plan_square(key, w, c0):
            src = kview(w, c0)
            plan.append((key, [(lambda s: s.rearrange("p (k n) -> p k n", k=KT)[:, 0:4, :], src[:, 0:4, :]),
                               (lambda s: s.rearrange("p (k n) -> p k n", k=KT)[:, 4:8, :], src[:, 4:8, :])]))

        def plan_pair(key, a, b):
            plan.append((key, [(lambda s: s.rearrange("p (k h n) -> p k h n", k=KT, h=2)[:, :, 0, :], a),
                               (lambda s: s.rearrange("p (k h n) -> p k h n", k=KT, h=2)[:, :, 1, :], b)]))

        def plan_rows(key, w, r0, nrow, c0):
            src = w[r0:r0 + nrow * P, c0:c0 + 512].rearrange("(k p) n -> p k n", p=P)
            h = nrow // 2
            plan.append((key, [(lambda s: s.rearrange("p (k n) -> p k n", k=KT)[:, 0:h, :], src[:, 0:h, :]),
                               (lambda s: s.rearrange("p (k n) -> p k n", k=KT)[:, h:nrow, :], src[:, h:nrow, :])]))

        w_in_cols = {"qa": 0, "ka": 512, "va": 1024, "zz": 1792, "ihgh": 2304}
        DOWN = [(0, 8), (8, 8), (16, 6)]
        fill = {}

        def plan_ada(li, j):
            plan_square(("ada", li, j), A["w_ada"][li, :, :], 512 * j)

        FILL = {(0, "fourier"): [(0, 4), (0, 5)],
                (0, "hgrn"): [(0, 6), (0, 7), (0, 8), (0, 9)],
                (0, "att"): [(0, 10), (0, 11), (1, 0), (1, 1), (1, 2), (1, 3)],
                (1, "fourier"): [(1, 4), (1, 5)],
                (1, "hgrn"): [(1, 6), (1, 7), (1, 8), (1, 9)],
                (1, "att"): [(1, 10), (1, 11)]}
        for j in range(4):
            plan_ada(0, j)
        for li in range(DEPTH):
            W = A["w_in"][li, :, :]
            for name, c0 in w_in_cols.items():
                plan_square(("w_in", li, name), W, c0)
            plan_pair(("w_in", li, "qhuf"), kview(W, 1536, 256), kview(W, 2816, 256))
            for stage in ("fourier", "hgrn", "att"):
                for lj in FILL[li, stage]:
                    plan_ada(*lj)
            for c in range(2):
                plan_square(("w_out", li, c), A["w_out"][li, :, :], 512 * c)
            for s in range(FT // 2):
                W = A["w_up"][li, :, :]
                plan_pair(("w_up", li, s), kview(W, 256 * s, 256), kview(W, DFF + 256 * s, 256))
            for c in range(2):
                for r0, nrow in DOWN:
                    plan_rows(("w_down", li, c, r0), A["w_down"][li, :, :], P * r0, nrow, 512 * c)
        W = A["conv_w_in_2"][0, :, :]
        for e in range(ET // 2):
            plan_pair(("c_in", e, 0), kview(W, 256 * e, 256), kview(W, CEXP + 256 * e, 256))
            plan_pair(("c_in", e, 1), kview(W, 2 * CEXP + 256 * e, 256), kview(W, 3 * CEXP + 256 * e, 256))
        for c in range(2):
            for r0 in (0, 8):
                plan_rows(("c_out", c, r0), A["conv_w_out_2"][0, :, :], P * r0, 8, 512 * c)
        W = A["attn_w_in_2"][0, :, :]
        for g in range(NG):
            for a in range(3):
                for c in range(2):
                    plan_square(("a_in", g, a, c), W, g * 3072 + a * 1024 + c * 512)
        for c in range(2):
            plan_square(("a_in", "z", c), W, NG * 3072 + 512 * c)
        for c in range(2):
            plan_square(("a_out", c), A["attn_w_out_2"][0, :, :], 512 * c)

        group = {}

        def bank(key, n=512):
            return ps[:, group[key] % BANKS, 0:n]

        def full_after(key):
            return group[key] + 1

        def taken_of(key):
            return taken[group[key] % BANKS]

        def taken_after(key):
            return taken_of(key), group[key] // BANKS + 1

        def backwards(ap):
            *dims, (step, count) = ap.ap
            return bass.AP(tensor=ap.tensor, offset=ap.offset + step * (count - 1), ap=[*[list(d) for d in dims], [-step, count]])

        def cols_of(t):
            return slice(t * P, (t + 1) * P)

        def stream_of(t):
            return 0 if t >= 2 else 1

        block = ctx.enter_context(nc.Block())

        @block.tensor
        def _(pe):
            read = [0]

            def open_group(key):
                n = len(group)
                group[key] = n
                if n >= BANKS:
                    pe.wait_ge(taken[n % BANKS], n // BANKS)
                return ps[:, n % BANKS, :]

            def weights(key):
                n = read[0]
                assert plan[n][0] == key, (plan[n][0], key)
                pe.wait_ge(slot_in[n % SLOTS], 32 * (n // SLOTS + 1))
                read[0] += 1
                return slot(n).rearrange("p (k n) -> p k n", k=KT)

            def release(part_way=None):
                if part_way is None:
                    read_at.append((full, len(group)))
                else:
                    part_way.then_inc(slot_part, 1)
                    parts_read[0] += 1
                    read_at.append((slot_part, parts_read[0]))

            def norm(N):
                first = True
                for k in range(KT):
                    o = open_group((N, k))
                    for t in norm_tiles(N):
                        if first:
                            pe.wait_ge(scaled.sem, scaled.after((N, t)))
                        last = pe.transpose(o[:, cols_of(t)], XS[:, t, k * P:(k + 1) * P], ident)
                    first = False
                    last.then_inc(full, 1)

            def wait_normed(N):
                for k in range(KT):
                    pe.wait_ge(*taken_after((N, k)))

            def ada(li, j):
                w = weights(("ada", li, j))
                o = open_group(("ada", li, j))
                if j in (4, 5, 10, 11):
                    for k in range(KT):
                        last = pe.matmul(o[0:2, :], csil[:, :, k], w[:, k, :], start=(k == 0), stop=(k == KT - 1))
                else:
                    for n in range(4):
                        for k in range(KT):
                            last = pe.matmul(o[:, 2 * n:2 * n + 2], w[:, k, n * P:(n + 1) * P], csil[:, :, k],
                                             start=(k == 0), stop=(k == KT - 1))
                last.then_inc(full, 1)
                release()

            def gate_rows(li, j):
                pe.wait_ge(*taken_after(("ada", li, j)))
                for s in range(2 if li == 0 else 1):
                    o = open_group(("gb", li, j, s))
                    pe.matmul(o[:, :], sel[0:2, s, :], grow[:, :], start=True, stop=True).then_inc(full, 1)

            def filler(li, stage):
                todo = list(FILL[li, stage])

                def one():
                    if todo:
                        lj = todo.pop(0)
                        ada(*lj)
                        if lj[1] in (4, 5, 10, 11):
                            gate_rows(*lj)
                return one, todo

            def t_out(li, w, key, dst_cols, lhs):
                o = open_group(key)
                for k in range(KT):
                    last = pe.matmul(o[:, 0:dst_cols.stop - dst_cols.start], lhs(k), HT[:, k, dst_cols],
                                     start=(k == 0), stop=(k == KT - 1))
                last.then_inc(full, 1)

            def w_in(li):
                live = range(NT) if li == 0 else range(2, NT)
                xcols = slice(0, 512) if li == 0 else slice(256, 512)
                w = weights(("w_in", li, "qa"))
                wait_normed(("n1", li))
                for h in range(NH_A):
                    t_out(li, w, ("qa", li, h), xcols, lambda k: w[:, k, h * P:(h + 1) * P])
                release()
                w = weights(("w_in", li, "ka"))
                for h in range(NH_A):
                    t_out(li, w, ("ka", li, h), slice(0, 512), lambda k: w[:, k, h * P:(h + 1) * P])
                release()
                for name, X in (("qa", QA), ("ka", KA)):
                    for h in range(NH_A):
                        pe.wait_ge(*taken_after((name, li, h)))
                        o = open_group(("rot", name, li, h))
                        pe.matmul(o[:, 0:256], rot, X[:, h, 256:512], start=True, stop=True).then_inc(full, 1)
                for name, tiles in (("va", range(NT)), ("zz", range(NT)), ("ihgh", range(NT))):
                    w = weights(("w_in", li, name))
                    for t in tiles:
                        n = 256 if name == "ihgh" and t not in live else 512
                        o = open_group((name, li, t))
                        for k in range(KT):
                            last = pe.matmul(o[:, 0:n], HT[:, k, cols_of(t)], w[:, k, 0:n],
                                             start=(k == 0), stop=(k == KT - 1))
                        last.then_inc(full, 1)
                    release()
                w = weights(("w_in", li, "qhuf"))
                for p in range(2):
                    t_out(li, w, ("qh", li, p), xcols, lambda k: w[:, k, p * P:(p + 1) * P])
                for t in live:
                    o = open_group(("uf", li, t))
                    for k in range(KT):
                        last = pe.matmul(o[:, 0:256], HT[:, k, cols_of(t)], w[:, k, 256:512],
                                         start=(k == 0), stop=(k == KT - 1))
                    last.then_inc(full, 1)
                release()

            def fourier(li):
                one, todo = filler(li, "fourier")
                streams = (0, 1) if li == 0 else (1,)
                pe.wait_ge(s_wf, 16 * (li + 1))
                for s in streams:
                    for f in range(2):
                        o = open_group(("f1", li, s, f))
                        for k in range(2):
                            t = 2 * s + k
                            pe.wait_ge(*taken_after(("uf", li, t)))
                            last = pe.matmul(o[:, :], UF[:, t, f * P:(f + 1) * P], dft_seq[:, k, :],
                                             start=(k == 0), stop=(k == 1))
                        last.then_inc(full, 1)
                    one()
                    o = open_group(("f2", li, s))
                    for f in range(2):
                        pe.wait_ge(*taken_after(("f1", li, s, f)))
                        pe.matmul(o[:, f * 256:(f + 1) * 256], dft_cos, FS[:, f, 0:256], start=True, stop=False)
                        last = pe.matmul(o[:, f * 256:(f + 1) * 256], dft_sin, FS[:, f, 256:512], start=False, stop=True)
                    last.then_inc(full, 1)
                    pe.wait_ge(*taken_after(("f2", li, s)))
                    o = open_group(("f3", li, s))
                    for c in range(2):
                        for f in range(2):
                            last = pe.matmul(o[:, c * 256:(c + 1) * 256], wf[:, f, c * P:(c + 1) * P], YT4[:, f, :],
                                             start=(f == 0), stop=(f == 1))
                    last.then_inc(full, 1)
                while todo:
                    one()

            def hgrn(li):
                one, todo = filler(li, "hgrn")
                un = units(li)

                def gates(i):
                    d, t = un[i]
                    pe.wait_ge(g_ready.sem, g_ready.after((li, t)))
                    pe.wait_ge(k_ready.sem, k_ready.after((li, t)))
                    if is_full(li, i):
                        o = open_group(("kT", li, i))
                        for p in range(2):
                            last = pe.transpose(o[:, p * P:(p + 1) * P], KTOK[:, t, d * 256 + p * P:d * 256 + (p + 1) * P], ident)
                        last.then_inc(full, 1)
                        for p in range(2):
                            for hf in range(2):
                                o = open_group(("E", li, i, p, hf))
                                pe.matmul(o[:, :], GL[:, t, d * 256 + p * P:d * 256 + (p + 1) * P],
                                                SM[:, d, 4 * hf:4 * hf + 4, :], start=True, stop=True).then_inc(full, 1)
                    if i < 6:
                        o = open_group(("suf", li, i))
                        pe.matmul(o[:, 0:256], SM[:, d, 8, :], GL[:, t, d * 256:(d + 1) * 256], start=True, stop=True)
                        end = (P - 1) * (1 - d)
                        for p in range(2):
                            last = pe.matmul(o[:, 256 + p:257 + p], GL[:, t, d * 256 + p * P:d * 256 + (p + 1) * P],
                                             SM[:, d, 7, end:end + 1], start=True, stop=True)
                        last.then_inc(full, 1)

                def apply(i):
                    d, t = un[i]
                    b = i % 2
                    if is_full(li, i):
                        pe.wait_ge(z_ready.sem, z_ready.after((li, i)))
                        pe.wait_ge(*taken_after(("kT", li, i)))
                        if i == (0 if li == 0 else 4):
                            for p in range(2):
                                pe.wait_ge(*taken_after(("qh", li, p)))
                        for lp in range(4):
                            for par in range(2):
                                o = open_group(("S", li, i, lp, par))
                                r = slice(64 * par, 64 * par + 64)
                                for lv in range(2):
                                    level = 2 * lp + lv
                                    for p in range(2):
                                        c = (lv * 2 + p) * P
                                        if level == 0:
                                            zk_, zq_ = KTT[r, b, p, :], QH[r, p, cols_of(t)]
                                        else:
                                            zk_ = zq_ = XE[b][r, p, level - 1, :]
                                        last = pe.matmul(o[:, c:c + P], zk_, zq_, start=True, stop=True)
                                last.then_inc(full, 1)
                        for par in range(2):
                            o = open_group(("O", li, i, par))
                            r = slice(64 * par, 64 * par + 64)
                            pe.wait_ge(*taken_after(("S", li, i, 3, par)))
                            if i >= 2:
                                pe.wait_ge(*taken_after(("SU", li, i - 2)))
                            for p in range(2):
                                h = 2 * p + par
                                last = pe.matmul(o[:, p * 64:(p + 1) * 64], ACC[:, d, par, p, :], IH[:, t, h * 64:(h + 1) * 64],
                                                 start=True, stop=(i < 2))
                                if i >= 2:
                                    last = pe.matmul(o[:, p * 64:(p + 1) * 64], XE[b][r, p, 7, :], ST[r, d, p, :],
                                                     start=False, stop=True)
                            last.then_inc(full, 1)
                    if i < 6:
                        pe.wait_ge(kd_ready.sem, kd_ready.after((li, i)))
                        o = open_group(("SU", li, i))
                        for p in range(2):
                            last = pe.matmul(o[:, p * P:(p + 1) * P], KD[:, b, p * P:(p + 1) * P], IH[:, t, p * P:(p + 1) * P],
                                             start=True, stop=True)
                        last.then_inc(full, 1)

                for t in range(NT):
                    pe.wait_ge(*taken_after(("ihgh", li, t)))
                gates(0)
                for i in range(8):
                    if i + 1 < 8:
                        gates(i + 1)
                    apply(i)
                    one()
                assert not todo
                for p in range(2):
                    o = open_group(("rec", li, p))
                    for t in (range(NT) if li == 0 else range(2, NT)):
                        pe.wait_ge(rec_ready.sem, rec_ready.after((li, t)))
                        last = pe.transpose(o[:, cols_of(t)], OREC[:, t, p * P:(p + 1) * P], ident)
                    last.then_inc(full, 1)

            def attention(li):
                one, todo = filler(li, "att")
                au = att_units(li)
                for name in ("qa", "ka"):
                    for h in range(NH_A):
                        pe.wait_ge(*taken_after(("rot", name, li, h)))
                for t in range(NT):
                    pe.wait_ge(*taken_after(("va", li, t)))
                U = len(au)
                for st in range(U + 3):
                    if st < U:
                        t, h = au[st]
                        nk_ = 256 if t < 2 else 512
                        for c in range(2):
                            o = open_group(("s", li, st, c))
                            r = slice(64 * c, 64 * c + 64)
                            pe.matmul(o[:, 0:nk_], QA[r, h, cols_of(t)], KA[r, h, 0:nk_], start=True, stop=True).then_inc(full, 1)
                    if 0 <= st - 1 < U:
                        u = st - 1
                        t, h = au[u]
                        o = open_group(("aT", li, u))
                        pe.wait_ge(a_ready.sem, a_ready.after((li, u)))
                        for j in range(2 if t < 2 else 4):
                            last = pe.transpose(o[:, j * P:(j + 1) * P], E2[:, u % 2, 0, j * P:(j + 1) * P], ident)
                        last.then_inc(full, 1)
                    if 0 <= st - 2 < U:
                        u = st - 2
                        t, h = au[u]
                        o = open_group(("av", li, u))
                        pe.wait_ge(*taken_after(("aT", li, u)))
                        nj = 2 if t < 2 else 4
                        for j in range(nj):
                            last = pe.matmul(o[:, 0:P], AT[:, u % 2, j * P:(j + 1) * P], VA[:, j, h * P:(h + 1) * P],
                                             start=(j == 0), stop=(j == nj - 1))
                        last.then_inc(full, 1)
                    if 0 <= st - 3 < U:
                        u = st - 3
                        pe.wait_ge(*taken_after(("av", li, u)))
                        o = open_group(("oT", li, u))
                        pe.transpose(o[:, 0:P], ON[:, u % 2, :], ident).then_inc(full, 1)
                    if st % 2 == 1:
                        one()
                while todo:
                    one()

            def w_out(li):
                live = range(NT) if li == 0 else range(2, NT)
                for u in range(len(att_units(li))):
                    pe.wait_ge(*taken_after(("oT", li, u)))
                for p in range(2):
                    pe.wait_ge(*taken_after(("rec", li, p)))
                for s in ((0, 1) if li == 0 else (1,)):
                    pe.wait_ge(*taken_after(("f3", li, s)))
                for c in range(2):
                    w = weights(("w_out", li, c))
                    for t in live:
                        o = open_group(("w_out", li, c, t))
                        for k in range(8):
                            last = pe.matmul(o[:, :], MT[:, k, cols_of(t)], w[:, k, :], start=(k == 0), stop=(k == 7))
                        last.then_inc(full, 1)
                    release()

            def ffn(li):
                xcols = slice(0, 512) if li == 0 else slice(256, 512)
                live = range(NT) if li == 0 else range(2, NT)
                norm(("n2", li))
                for s in range(FT // 2):
                    w = weights(("w_up", li, s))
                    if s == 0:
                        wait_normed(("n2", li))
                    for j in range(2):
                        for a in range(2):
                            t_out(li, w, ("u", li, 2 * s + j, a), xcols,
                                  lambda k: w[:, k, a * 256 + j * P:a * 256 + (j + 1) * P])
                    release()
                for c in range(2):
                    outs = [open_group(("w_down", li, c, t)) for t in live]
                    for r0, nrow in DOWN:
                        w = weights(("w_down", li, c, r0))
                        for k in range(nrow):
                            if c == 0:
                                pe.wait_ge(f_out.sem, f_out.after((li, r0 + k)))
                            for t, o in zip(live, outs):
                                f = r0 + k
                                last = pe.matmul(o[:, :], HF[:, f, cols_of(t)], w[:, k, :], start=(f == 0), stop=(f == FT - 1))
                                if f == FT - 1:
                                    last.then_inc(full, 1)
                        release(last if r0 + nrow < FT else None)

            pe.wait_ge(s_const, 32)
            pe.wait_ge(s_small, 16 * len(small_ins))
            for c in range((NCOL + P - 1) // P):
                n = min(P, NCOL - c * P)
                o = open_group(("cols", c))
                pe.transpose(o[:, 0:n], rows[0:n, c, :], ident[0:n, 0:n]).then_inc(full, 1)
            pe.wait_ge(c_ready, 1)
            for j in range(4):
                ada(0, j)
            for li in range(DEPTH):
                norm(("n1", li))
                w_in(li)
                fourier(li)
                hgrn(li)
                attention(li)
                w_out(li)
                ffn(li)

            norm(("cn", 0))
            for e in range(ET // 2):
                pair = {}
                for s in range(2):
                    w = weights(("c_in", e, s))
                    if e == 0 and s == 0:
                        wait_normed(("cn", 0))
                    for j in range(2):
                        o = open_group(("c", 2 * e + j, s))
                        for a in range(2):
                            for k in range(KT):
                                last = pe.matmul(o[:, a * 256:(a + 1) * 256], w[:, k, a * 256 + j * P:a * 256 + (j + 1) * P],
                                                 HT[:, k, 256:512], start=(k == 0), stop=(k == KT - 1))
                        last.then_inc(full, 1)
                    release()
            for c in range(2):
                outs = [open_group(("c_out", c, t)) for t in (2, 3)]
                for r0 in (0, 8):
                    w = weights(("c_out", c, r0))
                    for k in range(8):
                        f = r0 + k
                        if c == 0:
                            pe.wait_ge(c_out.sem, c_out.after(f))
                        for o, tk in zip(outs, range(2)):
                            last = pe.matmul(o[:, :], YC[:, f, tk * P:(tk + 1) * P], w[:, k, :], start=(f == 0), stop=(f == ET - 1))
                            if f == ET - 1:
                                last.then_inc(full, 1)
                    release(last if r0 == 0 else None)
            o = open_group("vec")
            pe.wait_ge(s_hot, 48)
            pe.matmul(o[0:NG * NH, 0:384], tabx, hot, start=True, stop=True).then_inc(full, 1)
            norm(("an", 0))
            first = True
            pend = []

            def mean_of(key):
                pe.wait_ge(q_sq.sem, q_sq.after(key))
                o = open_group(("ms", key))
                pe.matmul(o[:, :], means, SQ[:, QKEYS.index(key) % 2, :], start=True, stop=True).then_inc(full, 1)

            for g in range(NG):
                for a in range(3):
                    for c in range(2):
                        w = weights(("a_in", g, a, c))
                        if first:
                            wait_normed(("an", 0))
                            first = False
                        if a < 2:
                            for jj in range(2):
                                key = (g, a, 2 * c + jj)
                                o = open_group(("qk", key))
                                for m in range(2):
                                    for k in range(KT):
                                        last = pe.matmul(o[:, m * 256:(m + 1) * 256],
                                                         w[:, k, (2 * jj + m) * P:(2 * jj + m + 1) * P],
                                                         HT[:, k, 256:512], start=(k == 0), stop=(k == KT - 1))
                                last.then_inc(full, 1)
                                pend.append(key)
                                if len(pend) > 1:
                                    mean_of(pend.pop(0))
                        else:
                            for t in range(2):
                                o = open_group(("v2", g, c, t))
                                for k in range(KT):
                                    last = pe.matmul(o[:, :], HT[:, k, 256 + t * P:256 + (t + 1) * P], w[:, k, :],
                                                     start=(k == 0), stop=(k == KT - 1))
                                last.then_inc(full, 1)
                                if pend:
                                    mean_of(pend.pop(0))
                        release()
            for c in range(2):
                w = weights(("a_in", "z", c))
                for j in range(2):
                    o = open_group(("z2", c, j))
                    for m in range(2):
                        for k in range(KT):
                            last = pe.matmul(o[:, m * 256:(m + 1) * 256], w[:, k, (2 * j + m) * P:(2 * j + m + 1) * P],
                                             HT[:, k, 256:512], start=(k == 0), stop=(k == KT - 1))
                    last.then_inc(full, 1)
                release()
            for key in QKEYS:
                pe.wait_ge(*taken_after(("qk", key)))
            for g in range(NG):
                for c in range(2):
                    for t in range(2):
                        pe.wait_ge(*taken_after(("v2", g, c, t)))
            U = len(BU)
            for st in range(U + 2):
                if st < U:
                    h, t = BU[st]
                    r = slice(64 * (h % 2), 64 * (h % 2) + 64)
                    n = (t + 1) * P
                    for part_, gs in enumerate(((0, 1), (2,))):
                        o = open_group(("s2", st, part_))
                        for g in gs:
                            last = pe.matmul(o[:, g % 2 * 256:g % 2 * 256 + n], QK2[r, g, 0, h // 2, cols_of(t)],
                                             QK2[r, g, 1, h // 2, 0:n], start=True, stop=True)
                        last.then_inc(full, 1)
                if 0 <= st - 1 < U:
                    u = st - 1
                    h, t = BU[u]
                    pe.wait_ge(b_exp.sem, b_exp.after(BU[u]))
                    for part_, gs in enumerate(((0, 1), (2,))):
                        o = open_group(("eT", u, part_))
                        for g in gs:
                            for kt in range(t + 1):
                                c = (g % 2 * 2 + kt) * P
                                last = pe.transpose(o[:, c:c + P], LG[:, u % 2, g, kt * P:(kt + 1) * P], ident)
                        last.then_inc(full, 1)
                if 0 <= st - 2 < U:
                    u = st - 2
                    h, t = BU[u]
                    o = open_group(("o2", u))
                    for part_ in range(2):
                        pe.wait_ge(*taken_after(("eT", u, part_)))
                    blocks = [(g, kt) for g in range(NG) for kt in range(t + 1)]
                    for j, (g, kt) in enumerate(blocks):
                        c = (g * 2 + kt) * P
                        last = pe.matmul(o[:, 0:64], E3[:, u % 2, c:c + P], V2[:, g, kt, h * 64:(h + 1) * 64],
                                         start=(j == 0), stop=(j == len(blocks) - 1))
                    last.then_inc(full, 1)
            for u in range(U - 8, U):
                pe.wait_ge(*taken_after(("o2", u)))
            for k in range(KT):
                o = open_group(("yT", k))
                for t in range(2):
                    last = pe.matmul(o[:, t * P:(t + 1) * P], Y2[:, t, k * P:(k + 1) * P], flip, start=True, stop=True)
                last.then_inc(full, 1)
            for k in range(KT):
                pe.wait_ge(*taken_after(("yT", k)))
            for c in range(2):
                w = weights(("a_out", c))
                for t in range(2):
                    o = open_group(("a_out", c, t))
                    for k in range(KT):
                        last = pe.matmul(o[:, :], YT2[:, k, t * P:(t + 1) * P], w[:, k, :], start=(k == 0), stop=(k == KT - 1))
                    last.then_inc(full, 1)
            assert read[0] == len(plan)

        @block.sync
        def _(sp):
            sp.dma_start(wide[:, :], wide_c).then_inc(s_const, 16)
            sp.dma_start(arena[:, 0:2 * LEVELS * P], mask_c).then_inc(s_const, 16)
            for dst, src in small_ins:
                sp.dma_start(dst, src).then_inc(s_small, 16)
            sp.dma_start(RES[:, 0:2, :], A["ctx"].rearrange("a (t p) n -> p (a t) n", p=P)).then_inc(s_in, 16)
            sp.dma_start(RES[:, 2:4, :], A["x"].rearrange("a (t p) n -> p (a t) n", p=P)).then_inc(s_in, 16)
            for n, (key, parts) in enumerate(plan):
                if n >= SLOTS:
                    sp.wait_ge(*read_at[n - SLOTS])
                for dst, src in parts:
                    sp.dma_start(dst(slot(n)), src).then_inc(slot_in[n % SLOTS], 16)
            for c in range(2):
                for t in range(2):
                    sp.wait_ge(*taken_after(("a_out", c, t)))
                    sp.dma_start(out[0, t * P:(t + 1) * P, c * 512:(c + 1) * 512],
                                 RES[:, 2 + t, c * 512:(c + 1) * 512]).then_inc(s_out, 16)
            sp.wait_ge(s_out, 64)

        @block.gpsimd
        def _(pool):

            def gate_bias(li, g):
                row = A["b_ada"][li, (2 + 3 * g) * DM:(3 + 3 * g) * DM]
                for s in range(2 if li == 0 else 1):
                    pool.dma_start(GB[:, g, s, :], row.partition_broadcast(P)).then_inc(s_gb, 16)

            pool.dma_start(lb_rows, A["lb_param"].rearrange("l d n -> l (d n)").partition_broadcast(P)).then_inc(s_lb, 16)
            gate_bias(0, 0)
            pool.wait_ge(*taken_after(("uf", 0, 3)))
            pool.wait_ge(full, full_after(("uf", 0, 3)))
            pool.dma_start(wf, A["w_fnet"][0, :, :].rearrange("(f p) n -> p f n", p=P)).then_inc(s_wf, 16)
            pool.wait_ge(kd_ready.sem, kd_ready.after((0, 5)))
            pool.wait_ge(full, full_after(("kT", 0, 7)))
            gate_bias(0, 1)
            pool.wait_ge(res_new.sem, res_new.after(("w_out", 0)))
            gate_bias(1, 0)
            pool.wait_ge(full, full_after(("uf", 1, 3)))
            pool.dma_start(wf, A["w_fnet"][1, :, :].rearrange("(f p) n -> p f n", p=P)).then_inc(s_wf, 16)
            pool.wait_ge(kd_ready.sem, kd_ready.after((1, 5)))
            pool.wait_ge(full, full_after(("kT", 1, 7)))
            gate_bias(1, 1)
            pool.wait_ge(res_new.sem, res_new.after(("w_down", 1)))
            pool.dma_start(GB[:, 0, 0, :], A["final_norm_w"].partition_broadcast(P)).then_inc(s_fw, 16)
            pool.wait_ge(res_new.sem, res_new.after(("w_down", 0)))
            pool.dma_start(hot, hot_c).then_inc(s_hot, 16)
            pool.dma_start(tabx[0:32, :], A["rel_bias_2"]).then_inc(s_hot, 16)
            pool.dma_start(tabx[32:32 + NG, :], tab_c).then_inc(s_hot, 16)
            pool.wait_ge(*taken_after("vec"))
            pool.dma_start(vec_d, vec).then_inc(s_vec, 16)
            pool.wait_ge(s_vec, 16)
            for h in range(NH):
                if h >= 3:
                    pool.wait_ge(b_max.sem, b_max.after((h - 3, 1)))
                src = bass.AP(tensor=vec_d.tensor, offset=h * 384, ap=[[1, P], [NH * 384, NG], [1, 256]])
                pool.dma_start(BIAS[:, h % 3, :, :], src).then_inc(s_bias[h % 3], 16)
            for b in range(3):
                pool.wait_ge(s_bias[b], 16 * len(range(b, NH, 3)))

        @block.scalar
        def _(act):
            line = Line()
            act.wait_ge(s_eps, 1)

            def evict(key, dst, n):
                act.wait_ge(full, full_after(key))
                act.activation(dst, bank(key, n), ACT.Copy).then_inc(taken_of(key), 1)

            def root(signal, key, dst, mean):
                act.activation(dst, mean, ACT.Ln, bias=EPS_COL).then_inc(scalar_step, line.one())
                act.wait_ge(scalar_step, line.n)
                act.activation(dst, dst, ACT.Exp, scale=-0.5).then_inc(signal.sem, 1)

            def norm(N):
                for t in norm_tiles(N):
                    if N == ("n1", 0):
                        if t == 0:
                            act.wait_ge(s_in, 32)
                    elif N == ("an", 0):
                        act.wait_ge(*taken_after(("c_out", 1, 3)))
                        act.wait_ge(*taken_after(("c_out", 0, 3)))
                    elif t == norm_tiles(N)[0]:
                        act.wait_ge(res_new.sem, res_new.after({("n2", 0): ("w_out", 0), ("n1", 1): ("w_down", 0), ("n2", 1): ("w_out", 1),
                                           ("fn", 0): ("w_down", 1), ("cn", 0): ("final", 0)}[N]))
                    act.activation(XS[:, t, :], RES[:, t, :], ACT.Square, scale=1.0 / 32.0, accum_out=ssq[:, t:t + 1]).then_inc(scalar_step, line.one())
                    act.wait_ge(scalar_step, line.n)
                    root(squared, (N, t), rstd[:, t:t + 1], ssq[:, t:t + 1])
                if N == ("fn", 0):
                    return
                for k in range(1, KT, 2):
                    act.wait_ge(full, full_after((N, k)))
                    if N[0] in ("n1", "n2"):
                        m = 0 if N[0] == "n1" else 2
                        if 0 in norm_tiles(N):
                            act.activation(HT[:, k, 0:256], bank((N, k))[:, 0:256], ACT.Identity,
                                                scale=nscale[:, k, 1:2], bias=modt[:, N[1], m, k, 1:2]).then_inc(scalar_step, line.one())
                        act.activation(HT[:, k, 256:512], bank((N, k))[:, 256:512], ACT.Identity,
                                                    scale=nscale[:, k, 0:1], bias=modt[:, N[1], m, k, 0:1]).then_inc(taken_of((N, k)), 1)
                    else:
                        act.activation(HT[:, k, 256:512], bank((N, k))[:, 256:512], ACT.Copy,
                                                    scale=pcol(N, k)).then_inc(taken_of((N, k)), 1)

            def ada(li, j):
                if j in (4, 5, 10, 11):
                    key = ("ada", li, j)
                    act.wait_ge(full, full_after(key))
                    act.activation(grow[:, :], bank(key)[0:2, :], ACT.Copy).then_inc(taken_of(key), 1)

            def filler(li, stage):
                todo = list(FILL[li, stage])

                def one():
                    if todo:
                        ada(*todo.pop(0))
                return one, todo

            def w_in(li):
                lo = 0 if li == 0 else 256
                for name, X in (("qa", QA), ("ka", KA)):
                    for h in range(NH_A):
                        l0 = lo if name == "qa" else 0
                        evict((name, li, h), X[:, h, l0:512], 512 - l0)
                for t in range(NT):
                    evict(("va", li, t), VA[:, t, :], 512)
                for t in range(NT):
                    key = ("zz", li, t)
                    act.wait_ge(full, full_after(key))
                    if t:
                        act.wait_ge(*taken_after(("zz", li, t - 1)))
                    act.activation(gate_t[:, 0, :], bank(key), ACT.Abs).then_inc(scalar_step, line.one())
                    act.wait_ge(scalar_step, line.n)
                    act.activation(gate_t[:, 0, :], gate_t[:, 0, :], ACT.Exp, scale=-1.0).then_inc(scalar_step, line.one())
                    act.wait_ge(scalar_step, line.n)
                    act.activation(gate_t[:, 0, :], gate_t[:, 0, :], ACT.Ln, bias=1.0).then_inc(z_soft.sem, 1)
                    if li:
                        act.wait_ge(b_gap.sem, b_gap.after((li, t)))
                        act.activation(gate_t[:, 1, :], gate_t[:, 1, :], ACT.Abs).then_inc(scalar_step, line.one())
                        act.wait_ge(scalar_step, line.n)
                        act.activation(gate_t[:, 1, :], gate_t[:, 1, :], ACT.Exp, scale=-1.0).then_inc(scalar_step, line.one())
                        act.wait_ge(scalar_step, line.n)
                        act.activation(gate_t[:, 1, :], gate_t[:, 1, :], ACT.Ln, bias=1.0).then_inc(b_soft.sem, 1)
                    act.wait_ge(*taken_after(key))
                    act.activation(KTOK[:, t, :], KTOK[:, t, :], ACT.Exp).then_inc(k_ready.sem, 1)
                for t in range(NT):
                    key = ("ihgh", li, t)
                    act.wait_ge(full, full_after(key))
                    if li == 0 or t >= 2:
                        act.activation(GH[:, t, :], bank(key)[:, 256:512], ACT.Silu).then_inc(scalar_step, line.one())
                    act.activation(IH[:, t, :], bank(key)[:, 0:256], ACT.Copy).then_inc(taken_of(key), 1)
                for p in range(2):
                    evict(("qh", li, p), QH[:, p, lo:512], 512 - lo)
                for t in (range(NT) if li == 0 else range(2, NT)):
                    evict(("uf", li, t), UF[:, t, :], 256)

            def fourier(li):
                one, todo = filler(li, "fourier")
                for s in ((0, 1) if li == 0 else (1,)):
                    for f in range(2):
                        evict(("f1", li, s, f), FS[:, f, :], 512)
                    one()
                    evict(("f2", li, s), YT4, 512)
                    key = ("f3", li, s)
                    act.wait_ge(full, full_after(key))
                    act.activation(MT[:, 6:8, s * 256:(s + 1) * 256],
                                             bank(key).rearrange("p (c n) -> p c n", c=2), ACT.Copy).then_inc(taken_of(key), 1)
                while todo:
                    one()

            def hgrn(li):
                one, todo = filler(li, "hgrn")

                def gates(i):
                    b = i % 2
                    if is_full(li, i):
                        for p in range(2):
                            for hf in range(2):
                                key = ("E", li, i, p, hf)
                                act.wait_ge(full, full_after(key))
                                if i >= 2 and is_full(li, i - 2):
                                    act.wait_ge(full, full_after(("O", li, i - 2, 1)))
                                act.activation(XE[b][:, p, 4 * hf:4 * hf + 4, :],
                                                         bank(key).rearrange("p (l n) -> p l n", l=4), ACT.Exp).then_inc(taken_of(key), 1)
                    if i < 6:
                        key = ("suf", li, i)
                        act.wait_ge(full, full_after(key))
                        if i >= 2:
                            act.wait_ge(*taken_after(("SU", li, i - 2)))
                        act.activation(SE[:, b, 0:258], bank(key, 258), ACT.Exp).then_inc(taken_of(key), 1)

                gates(0)
                for i in range(8):
                    if i + 1 < 8:
                        gates(i + 1)
                    one()
                for t in (range(NT) if li == 0 else range(2, NT)):
                    act.wait_ge(rec_sum.sem, rec_sum.after((li, t)))
                    act.activation(hrstd[:, t, :], hssq[:, t, :], ACT.Ln, scale=1.0 / 64.0, bias=EPS_COL).then_inc(scalar_step, line.one())
                    act.wait_ge(scalar_step, line.n)
                    act.activation(hrstd[:, t, :], hrstd[:, t, :], ACT.Exp, scale=-0.5).then_inc(og_exp.sem, 1)
                for p in range(2):
                    key = ("rec", li, p)
                    lo = 0 if li == 0 else 256
                    act.wait_ge(full, full_after(("rec", li, 1)))
                    act.activation(MT[:, 4 + p, lo:512], bank(key)[:, lo:512], ACT.Copy).then_inc(taken_of(key), 1)

            def attention(li):
                one, todo = filler(li, "att")
                au = att_units(li)
                U = len(au)
                lam_init = 0.8 - 0.6 * math.exp(-0.3 * li)
                for st in range(U + 3):
                    if st < U:
                        u = st
                        t, h = au[u]
                        n = 256 if t < 2 else 512
                        act.wait_ge(a_max.sem, a_max.after((li, u)))
                        if u >= 2:
                            act.wait_ge(full, full_after(("aT", li, u - 2)))
                        if u >= 2:
                            act.wait_ge(a_ready.sem, a_ready.after((li, u - 2)))
                        for c in range(2):
                            ins = act.activation(E2[:, u % 2, c, 0:n], bank(("s", li, u, c), n), ACT.Exp, scale=0.125,
                                                 bias=amax[:, u % 2, c:c + 1], accum_out=asum[:, u % 2, c:c + 1])
                            ins.then_inc(taken_of(("s", li, u, c)), 1)
                    if 0 <= st - 1 < U:
                        u = st - 1
                        t, h = au[u]
                        n = 256 if t < 2 else 512
                        if u >= 2:
                            act.wait_ge(full, full_after(("av", li, u - 2)))
                        evict(("aT", li, u), AT[:, u % 2, 0:n], n)
                    if 0 <= st - 2 < U:
                        u = st - 2
                        act.wait_ge(full, full_after(("av", li, u)))
                        if u >= 2:
                            act.wait_ge(full, full_after(("oT", li, u - 2)))
                        b = slice(u % 2, u % 2 + 1)
                        act.activation(ON[:, u % 2, :], bank(("av", li, u), P), ACT.Square,
                                            scale=1.0 / math.sqrt(128.0), accum_out=ossq[:, b]).then_inc(scalar_step, line.one())
                        act.wait_ge(scalar_step, line.n)
                        root(o_sq, (li, u), orstd[:, b], ossq[:, b])
                    if 0 <= st - 3 < U:
                        u = st - 3
                        t, h = au[u]
                        act.wait_ge(full, full_after(("oT", li, u)))
                        act.activation(MT[:, h, cols_of(t)], bank(("oT", li, u), P), ACT.Copy,
                                                           scale=pcol(("subln", li))).then_inc(taken_of(("oT", li, u)), 1)
                    if st % 2 == 1:
                        one()
                while todo:
                    one()

            def ffn(li):
                norm(("n2", li))
                lo = 0 if li == 0 else 256
                w = 512 - lo

                def centre(f):
                    b = f % 2
                    if f >= 2:
                        act.wait_ge(f_out.sem, f_out.after((li, f - 2)))
                    for a in range(2):
                        key = ("u", li, f, a)
                        act.wait_ge(full, full_after(key))
                        ins = act.activation(FC[:, b, a, 0:w], bank(key, w), ACT.Identity,
                                             scale=pcol(("cw", li, 1), a * FT + f), bias=pcol(("cb", li), a * FT + f))
                        if a:
                            ins.then_inc(f_mid.sem, 1)
                        else:
                            ins.then_inc(scalar_step, line.one())

                centre(0)
                for f in range(FT):
                    if f + 1 < FT:
                        centre(f + 1)
                    act.wait_ge(*taken_after(("u", li, f, 0)))
                    act.activation(FC[:, f % 2, 2, 0:w], FC[:, f % 2, 0, 0:w], ACT.Silu).then_inc(f_exp.sem, 1)

            for c in range((NCOL + P - 1) // P):
                n = min(P, NCOL - c * P)
                evict(("cols", c), cols[:, c * P:c * P + n], n)
            act.wait_ge(*taken_after(("cols", 0)))
            act.activation(csil.rearrange("p s k -> p (s k)"), cols[:, 0:16], ACT.Silu).then_inc(c_ready, 1)
            act.wait_ge(lam_sum, 2 * DEPTH)
            act.activation(lam2, lam2, ACT.Exp).then_inc(lam_exp, 1)
            act.wait_ge(lb_abs, 1)
            act.activation(lb_t[:, 0, :], lb_rows[:, 0, :], ACT.Abs).then_inc(scalar_step, line.one())
            act.wait_ge(scalar_step, line.n)
            act.activation(lb_t[:, 0, :], lb_t[:, 0, :], ACT.Exp, scale=-1.0).then_inc(scalar_step, line.one())
            act.wait_ge(scalar_step, line.n)
            act.activation(lb_t[:, 0, :], lb_t[:, 0, :], ACT.Ln, bias=1.0).then_inc(lb_exp, 1)
            for li in range(DEPTH):
                norm(("n1", li))
                w_in(li)
                fourier(li)
                hgrn(li)
                attention(li)
                ffn(li)
            norm(("fn", 0))
            norm(("cn", 0))
            for e in range(ET):
                b = e % 2
                if e >= 2:
                    act.wait_ge(c_out.sem, c_out.after(e - 2))
                act.wait_ge(full, full_after(("c", e, 0)))
                act.activation(CC[:, b, 0, :], bank(("c", e, 0))[:, 256:512], ACT.Copy).then_inc(c_copy.sem, 1)
                act.wait_ge(full, full_after(("c", e, 1)))
                act.activation(CC[:, b, 1, :], bank(("c", e, 1))[:, 256:512], ACT.Silu).then_inc(c_z.sem, 1)
            norm(("an", 0))
            pend = []

            def scale_of(key):
                n = QKEYS.index(key)
                act.wait_ge(full, full_after(("ms", key)))
                if n >= 2:
                    act.wait_ge(*taken_after(("qk", QKEYS[n - 2])))
                act.activation(RQ[:, n % 2, :], bank(("ms", key)), ACT.Ln, bias=EPS_COL).then_inc(taken_of(("ms", key)), 1)
                act.wait_ge(*taken_after(("ms", key)))
                act.activation(RQ[:, n % 2, :], RQ[:, n % 2, :], ACT.Exp, scale=-0.5).then_inc(q_rs.sem, 1)

            for g in range(NG):
                for a in range(2):
                    for j in range(4):
                        key = (g, a, j)
                        n = QKEYS.index(key)
                        act.wait_ge(full, full_after(("qk", key)))
                        if n >= 2:
                            act.wait_ge(full, full_after(("ms", QKEYS[n - 2])))
                        act.activation(SQ[:, n % 2, :], bank(("qk", key)), ACT.Square, scale=0.125).then_inc(q_sq.sem, 1)
                        pend.append(key)
                        if len(pend) > 1:
                            scale_of(pend.pop(0))
                for c in range(2):
                    for t in range(2):
                        evict(("v2", g, c, t), V2[:, g, t, c * 512:(c + 1) * 512], 512)
                        if pend:
                            scale_of(pend.pop(0))
            for c, j in zk:
                key, k0 = ("z2", c, j), 4 * c + 2 * j
                act.wait_ge(full, full_after(key))
                act.activation(ZS[:, k0:k0 + 2, :], bank(key).rearrange("p (m n) -> p m n", m=2), ACT.Silu).then_inc(taken_of(key), 1)
            for st in range(len(BU) + 1):
                if st < len(BU):
                    u = st
                    h, t = BU[u]
                    n = (t + 1) * P
                    act.wait_ge(b_max.sem, b_max.after(BU[u]))
                    act.activation(LG[:, u % 2, :, 0:n], LG[:, u % 2, :, 0:n], ACT.Exp,
                                                     bias=bmax[:, u % 2:u % 2 + 1], accum_out=bsum[:, u % 2:u % 2 + 1]).then_inc(b_exp.sem, 1)
                if 0 <= st - 1:
                    u = st - 1
                    h, t = BU[u]
                    n = (t + 1) * P
                    key = ("eT", u, 0)
                    act.wait_ge(full, full_after(key))
                    if u >= 2:
                        act.wait_ge(full, full_after(("o2", u - 2)))
                    act.activation(E3[:, u % 2, 0:512].rearrange("p (g n) -> p g n", g=2)[:, :, 0:n],
                                             bank(key).rearrange("p (g n) -> p g n", g=2)[:, :, 0:n], ACT.Copy).then_inc(taken_of(key), 1)

        @block.vector
        def _(dve):
            line = Line()

            def norm(N):
                m = {"n1": 0, "n2": 2}.get(N[0])
                if m is not None:
                    dve.tensor_scalar(nscale, modt[:, N[1], m + 1, :, :], 1.0, None, ALU.add).then_inc(vector_step, line.one())
                    dve.wait_ge(vector_step, line.n)
                    w8 = cols[:, col[N]:col[N] + 8].unsqueeze(2).to_broadcast([P, KT, 2])
                    dve.tensor_tensor(nscale, nscale, w8, ALU.mult).then_inc(vector_step, line.one())
                    dve.wait_ge(vector_step, line.n)
                for t in norm_tiles(N):
                    dve.wait_ge(squared.sem, squared.after((N, t)))
                    if N == ("fn", 0):
                        if t == 2:
                            dve.wait_ge(s_fw, 16)
                        ins = dve.scalar_tensor_tensor(RES[:, t, :], RES[:, t, :], rstd[:, t:t + 1], GB[:, 0, 0, :],
                                                       ALU.mult, ALU.mult)
                        if t == 2:
                            ins.then_inc(vector_step, line.one())
                        else:
                            ins.then_inc(res_new.sem, 1)
                    else:
                        dve.tensor_scalar(XS[:, t, :], RES[:, t, :], rstd[:, t:t + 1], None, ALU.mult).then_inc(scaled.sem, 1)
                if N == ("fn", 0):
                    return
                for k in range(0, KT, 2):
                    dve.wait_ge(full, full_after((N, k)))
                    b = bank((N, k))
                    if m is not None:
                        if 0 in norm_tiles(N):
                            dve.tensor_scalar(HT[:, k, 0:256], b[:, 0:256], nscale[:, k, 1:2],
                                                   modt[:, N[1], m, k, 1:2], ALU.mult, ALU.add).then_inc(vector_step, line.one())
                        dve.tensor_scalar(HT[:, k, 256:512], b[:, 256:512], nscale[:, k, 0:1],
                                                       modt[:, N[1], m, k, 0:1], ALU.mult, ALU.add).then_inc(taken_of((N, k)), 1)
                    else:
                        dve.tensor_scalar(HT[:, k, 256:512], b[:, 256:512], pcol(N, k), None, ALU.mult).then_inc(taken_of((N, k)), 1)

            seen_gb = [0]

            def ada(li, j):
                key = ("ada", li, j)
                if j in (4, 5, 10, 11):
                    g, c = (0 if j < 6 else 1), j % 2
                    if c == 0:
                        seen_gb[0] += 32 if li == 0 else 16
                        dve.wait_ge(s_gb, seen_gb[0])
                    for s in range(2 if li == 0 else 1):
                        k2 = ("gb", li, j, s)
                        dve.wait_ge(full, full_after(k2))
                        d = GB[:, g, s, c * 512:(c + 1) * 512]
                        dve.tensor_tensor(d, bank(k2), d, ALU.add).then_inc(taken_of(k2), 1)
                else:
                    m = {0: 0, 1: 0, 2: 1, 3: 1, 6: 2, 7: 2, 8: 3, 9: 3}[j]
                    dve.wait_ge(full, full_after(key))
                    c0 = col["b_ada", li] + 4 * j
                    bb = cols[:, c0:c0 + 4].unsqueeze(2).to_broadcast([P, 4, 2])
                    k0 = 4 * (j % 2)
                    dve.tensor_tensor(modt[:, li, m, k0:k0 + 4, :],
                                                bank(key, 8).rearrange("p (k s) -> p k s", s=2), bb, ALU.add).then_inc(taken_of(key), 1)
                    dve.wait_ge(*taken_after(key))

            def filler(li, stage):
                todo = list(FILL[li, stage])

                def one():
                    if todo:
                        ada(*todo.pop(0))
                return one, todo

            def w_in(li):
                n = 0
                for name, X in (("qa", QA), ("ka", KA)):
                    for h in range(NH_A):
                        key = ("rot", name, li, h)
                        dve.wait_ge(full, full_after(key))
                        b = n % 2
                        dve.tensor_tensor(rope_t[:, b, :], bank(key, 256), sinT, ALU.mult).then_inc(vector_step, line.one())
                        dve.tensor_tensor(X[:, h, 256:512], X[:, h, 256:512], cosT, ALU.mult).then_inc(vector_step, line.one())
                        dve.wait_ge(vector_step, line.n)
                        dve.tensor_tensor(X[:, h, 256:512], X[:, h, 256:512], rope_t[:, b, :], ALU.add).then_inc(taken_of(key), 1)
                        n += 1
                for t in range(NT):
                    key = ("zz", li, t)
                    z = bank(key)
                    dve.wait_ge(z_soft.sem, z_soft.after((li, t)))
                    if li == 0:
                        dve.scalar_tensor_tensor(GL[:, t, :], z, 0.0, gate_t[:, 0, :], ALU.min, ALU.subtract).then_inc(g_ready.sem, 1)
                        dve.wait_ge(g_ready.sem, g_ready.after((li, t)))
                        dve.tensor_tensor(KTOK[:, t, :], GL[:, t, :], z, ALU.subtract).then_inc(taken_of(key), 1)
                    else:
                        dve.scalar_tensor_tensor(GL[:, t, :], z, 0.0, gate_t[:, 0, :], ALU.min, ALU.subtract).then_inc(vector_step, line.one())
                        dve.wait_ge(vector_step, line.n)
                        dve.tensor_tensor(GL[:, t, :], GL[:, t, :], lbs[:, 512:1024], ALU.add).then_inc(vector_step, line.one())
                        dve.wait_ge(vector_step, line.n)
                        dve.tensor_tensor(gate_t[:, 1, :], GL[:, t, :], lbs[:, 0:512], ALU.subtract).then_inc(b_gap.sem, 1)
                        dve.tensor_tensor(KTOK[:, t, :], GL[:, t, :], z, ALU.subtract).then_inc(taken_of(key), 1)
                        dve.tensor_tensor(GL[:, t, :], GL[:, t, :], lbs[:, 0:512], ALU.max).then_inc(vector_step, line.one())
                        dve.wait_ge(vector_step, line.n)
                        dve.wait_ge(b_soft.sem, b_soft.after((li, t)))
                        dve.tensor_tensor(GL[:, t, :], GL[:, t, :], gate_t[:, 1, :], ALU.add).then_inc(g_ready.sem, 1)

            def hgrn(li):
                one, todo = filler(li, "hgrn")
                un = units(li)

                def gates(i):
                    d, t = un[i]
                    b = i % 2
                    if is_full(li, i):
                        key = ("kT", li, i)
                        dve.wait_ge(full, full_after(key))
                        dve.tensor_copy(KTT[:, b, :, :], bank(key, 256).rearrange("p (q n) -> p q n", q=2)).then_inc(taken_of(key), 1)
                        dve.wait_ge(*taken_after(key))
                        for p in range(2):
                            for hf in range(2):
                                dve.wait_ge(*taken_after(("E", li, i, p, hf)))
                        if i == (0 if li == 0 else 4):
                            for p in range(2):
                                dve.wait_ge(*taken_after(("qh", li, p)))
                        q = QH[:, :, cols_of(t)]
                        for level in range(1, LEVELS):
                            B = level_block(level)
                            for hf in range(2):
                                src = q if hf == 1 - d else KTT[:, b, :, :]
                                for p in range(2):
                                    x = XE[b][:, p, level - 1, :].rearrange("p (m h n) -> p m h n", h=2, n=B)[:, :, hf, :]
                                    y = src[:, p, :].rearrange("p (m h n) -> p m h n", h=2, n=B)[:, :, hf, :]
                                    dve.tensor_tensor(x, x, y, ALU.mult).then_inc(vector_step, line.one())
                        dve.tensor_tensor(XE[b][:, :, 7, :], XE[b][:, :, 7, :], q, ALU.mult).then_inc(z_ready.sem, 1)
                    if i < 6:
                        dve.wait_ge(*taken_after(("suf", li, i)))
                        if i >= 2:
                            dve.wait_ge(full, full_after(("SU", li, i - 2)))
                        dve.tensor_tensor(KD[:, b, :], KTOK[:, t, d * 256:(d + 1) * 256], SE[:, b, 0:256], ALU.mult).then_inc(kd_ready.sem, 1)

                def apply(i):
                    d, t = un[i]
                    b = i % 2
                    if is_full(li, i):
                        for lp in range(4):
                            dve.wait_ge(full, full_after(("S", li, i, lp, 1)))
                            for lv in range(2):
                                m = MASK[:, d, 2 * lp + lv, :].unsqueeze(1).to_broadcast([P, 2, P])
                                for par in range(2):
                                    key = ("S", li, i, lp, par)
                                    ins = dve.copy_predicated(ACC[:, d, par, :, :], m,
                                                              bank(key)[:, lv * 256:(lv + 1) * 256].rearrange("p (h n) -> p h n", h=2))
                                    if lv:
                                        ins.then_inc(taken_of(key), 1)
                                    else:
                                        ins.then_inc(vector_step, line.one())
                                dve.wait_ge(vector_step, line.n)
                            for par in range(2):
                                dve.wait_ge(*taken_after(("S", li, i, lp, par)))
                        for par in range(2):
                            key = ("O", li, i, par)
                            dve.wait_ge(full, full_after(key))
                            o = OREC[:, t, :].rearrange("p (q a n) -> p q a n", q=2, a=2)[:, :, par, :]
                            src = bank(key, P).rearrange("p (q n) -> p q n", q=2)
                            if (d, t) in ((0, 0), (1, 1), (0, 2), (1, 3)):
                                dve.tensor_copy(o, src).then_inc(taken_of(key), 1)
                            else:
                                dve.tensor_tensor(o, src, o, ALU.add).then_inc(taken_of(key), 1)
                    if i < 6:
                        key = ("SU", li, i)
                        dve.wait_ge(full, full_after(key))
                        for p in range(2):
                            for hh in range(2):
                                r = slice(64 * hh, 64 * hh + 64)
                                dst = ST[r, d, p, :]
                                new = bank(key)[r, p * P + hh * 64:p * P + hh * 64 + 64]
                                if i < 2:
                                    ins = dve.tensor_copy(dst, new)
                                else:
                                    ins = dve.scalar_tensor_tensor(dst, dst, SE[r, b, 256 + p:257 + p], new, ALU.mult, ALU.add)
                                if p == 1 and hh == 1:
                                    ins.then_inc(taken_of(key), 1)
                                else:
                                    ins.then_inc(vector_step, line.one())
                        dve.wait_ge(*taken_after(key))

                dve.wait_ge(s_mask, 1)
                dve.memset(scr[:, 2560:3584], 0.0).then_inc(vector_step, line.one())
                dve.wait_ge(vector_step, line.n)
                gates(0)
                for i in range(8):
                    if i + 1 < 8:
                        gates(i + 1)
                    apply(i)
                    one()
                live = range(NT) if li == 0 else range(2, NT)
                for par in range(2):
                    dve.wait_ge(*taken_after(("O", li, 7, par)))
                for t in live:
                    o = OREC[:, t, :]
                    o4 = o.rearrange("p (h n) -> p h n", h=4)
                    tf = scr[:, 0:256]
                    dve.tensor_tensor(tf, o, o, ALU.mult).then_inc(vector_step, line.one())
                    dve.wait_ge(vector_step, line.n)
                    dve.tensor_reduce(hssq[:, t, :], tf.rearrange("p (h n) -> p h n", h=4), AX.X, ALU.add).then_inc(rec_sum.sem, 1)
                    dve.wait_ge(rec_sum.sem, rec_sum.after((li, t)))
                for t in live:
                    o = OREC[:, t, :]
                    o4 = o.rearrange("p (h n) -> p h n", h=4)
                    dve.wait_ge(og_exp.sem, og_exp.after((li, t)))
                    dve.tensor_tensor(o4, o4, hrstd[:, t, :].unsqueeze(2).to_broadcast([P, 4, 64]), ALU.mult).then_inc(vector_step, line.one())
                    dve.wait_ge(vector_step, line.n)
                    dve.tensor_tensor(o4, o4, hw[:, li, :].unsqueeze(1).to_broadcast([P, 4, 64]), ALU.mult).then_inc(vector_step, line.one())
                    dve.wait_ge(vector_step, line.n)
                    dve.tensor_tensor(o, o, GH[:, t, :], ALU.mult).then_inc(rec_ready.sem, 1)

            def attention(li):
                one, todo = filler(li, "att")
                au = att_units(li)
                U = len(au)
                lam_init = 0.8 - 0.6 * math.exp(-0.3 * li)
                for st in range(U + 3):
                    if st < U:
                        u = st
                        t, h = au[u]
                        n = 256 if t < 2 else 512
                        b = u % 2
                        for c in range(2):
                            dve.wait_ge(full, full_after(("s", li, u, c)))
                            dve.tensor_reduce(arec[:, b, c:c + 1], bank(("s", li, u, c), n), AX.X, ALU.max).then_inc(vector_step, line.one())
                        dve.wait_ge(vector_step, line.n)
                        dve.tensor_scalar(amax[:, b, :], arec[:, b, :], -0.125, None, ALU.mult).then_inc(a_max.sem, 1)
                        dve.wait_ge(a_max.sem, a_max.after((li, u)))
                        for c in range(2):
                            dve.wait_ge(*taken_after(("s", li, u, c)))
                        dve.reciprocal(arec[:, b, :], asum[:, b, :]).then_inc(vector_step, line.one())
                        dve.wait_ge(vector_step, line.n)
                        dve.tensor_tensor(arec[:, b, 1:2], arec[:, b, 1:2], neglam[:, li:li + 1], ALU.mult).then_inc(vector_step, line.one())
                        dve.tensor_scalar(E2[:, b, 0, 0:n], E2[:, b, 0, 0:n], arec[:, b, 0:1], None, ALU.mult).then_inc(vector_step, line.one())
                        dve.wait_ge(vector_step, line.n)
                        dve.scalar_tensor_tensor(E2[:, b, 0, 0:n], E2[:, b, 1, 0:n], arec[:, b, 1:2],
                                                                       E2[:, b, 0, 0:n], ALU.mult, ALU.add).then_inc(a_ready.sem, 1)
                    if 0 <= st - 2 < U:
                        u = st - 2
                        b = u % 2
                        dve.wait_ge(o_sq.sem, o_sq.after((li, u)))
                        dve.tensor_scalar(ON[:, b, :], bank(("av", li, u), P), orstd[:, b:b + 1],
                                                              1.0 - lam_init, ALU.mult, ALU.mult).then_inc(taken_of(("av", li, u)), 1)
                    if st % 2 == 1:
                        one()
                while todo:
                    one()

            def add_out(name, li, gate, last_key):
                live = range(NT) if li == 0 and name in ("w_out", "w_down") else range(2, NT)
                n = 0
                for c in range(2):
                    for t in live:
                        key = (name, li, c, t) if name in ("w_out", "w_down") else (name, c, t)
                        dve.wait_ge(full, full_after(key))
                        r = RES[:, t, c * 512:(c + 1) * 512]
                        end = c == 1 and t == NT - 1
                        if gate is None:
                            dve.tensor_tensor(r, bank(key), r, ALU.add).then_inc(taken_of(key), 1)
                        else:
                            s = stream_of(t)
                            dve.tensor_tensor(wo_t[:, n % 2, :], bank(key), GB[:, gate, s, c * 512:(c + 1) * 512], ALU.mult).then_inc(taken_of(key), 1)
                            dve.wait_ge(*taken_after(key))
                            ins = dve.tensor_tensor(r, r, wo_t[:, n % 2, :], ALU.add)
                            if end:
                                ins.then_inc(res_new.sem, 1)
                            else:
                                ins.then_inc(vector_step, line.one())
                        n += 1

            def ffn(li):
                norm(("n2", li))
                lo = 0 if li == 0 else 256
                w = 512 - lo
                ns = w // 256

                def conv(f):
                    b = f % 2
                    dve.wait_ge(f_mid.sem, f_mid.after((li, f)))
                    for a in range(2):
                        key = ("u", li, f, a)
                        u3 = bank(key, w).rearrange("p (s n) -> p s n", s=ns)
                        o3 = FC[:, b, a, 0:w].rearrange("p (s n) -> p s n", s=ns)
                        dve.scalar_tensor_tensor(o3[:, :, 1:256], u3[:, :, 0:255], pcol(("cw", li, 0), a * FT + f),
                                                      o3[:, :, 1:256], ALU.mult, ALU.add).then_inc(vector_step, line.one())
                        dve.wait_ge(vector_step, line.n)
                        dve.scalar_tensor_tensor(o3[:, :, 0:255], u3[:, :, 1:256], pcol(("cw", li, 2), a * FT + f),
                                                           o3[:, :, 0:255], ALU.mult, ALU.add).then_inc(taken_of(key), 1)
                        dve.wait_ge(*taken_after(key))

                def product(f):
                    b = f % 2
                    dve.wait_ge(f_exp.sem, f_exp.after((li, f)))
                    e, vl = FC[:, b, 2, 0:w], FC[:, b, 1, 0:w]
                    dve.tensor_tensor(HF[:, f, lo:512], e, vl, ALU.mult).then_inc(f_out.sem, 1)

                conv(0)
                for f in range(FT):
                    if f + 1 < FT:
                        conv(f + 1)
                    product(f)
                add_out("w_down", li, 1, ("w_down", li))

            dve.wait_ge(s_const, 32)
            dve.tensor_copy(masks[:, :], arena[:, 0:2 * LEVELS * P]).then_inc(s_mask, 1)
            dve.memset(EPS_COL, EPS).then_inc(s_eps, 1)
            dve.wait_ge(s_small, 16 * len(small_ins))
            for li in range(DEPTH):
                for a in range(2):
                    dve.tensor_tensor_reduce(out=lam_tmp, in0=lam_rows[:, li, 2 * a, :], in1=lam_rows[:, li, 2 * a + 1, :],
                                             scale=1.0, scalar=0.0, op0=ALU.mult, op1=ALU.add,
                                             accum_out=lam2[:, li, a:a + 1]).then_inc(lam_sum, 1)
                    dve.wait_ge(lam_sum, 2 * li + a + 1)
            dve.wait_ge(lam_exp, 1)
            for li in range(DEPTH):
                dve.tensor_tensor(neglam[:, li:li + 1], lam2[:, li, 1:2], lam2[:, li, 0:1], ALU.subtract).then_inc(vector_step, line.one())
                dve.wait_ge(vector_step, line.n)
                dve.tensor_scalar(neglam[:, li:li + 1], neglam[:, li:li + 1], -(0.8 - 0.6 * math.exp(-0.3 * li)), None, ALU.add).then_inc(vector_step, line.one())
            dve.wait_ge(s_lb, 16)
            dve.tensor_tensor(lb_rows[:, 0, :], lb_rows[:, 1, :], lb_rows[:, 0, :], ALU.subtract).then_inc(lb_abs, 1)
            dve.wait_ge(lb_exp, 1)
            dve.scalar_tensor_tensor(lbs[:, 0:512], lb_rows[:, 0, :], 0.0, lb_t[:, 0, :], ALU.min, ALU.subtract).then_inc(vector_step, line.one())
            dve.wait_ge(vector_step, line.n)
            dve.tensor_tensor(lbs[:, 512:1024], lbs[:, 0:512], lb_rows[:, 0, :], ALU.subtract).then_inc(vector_step, line.one())
            for c in range((NCOL + P - 1) // P):
                dve.wait_ge(*taken_after(("cols", c)))
            for j in range(4):
                ada(0, j)
            for li in range(DEPTH):
                norm(("n1", li))
                w_in(li)
                one, todo = filler(li, "fourier")
                while todo:
                    one()
                hgrn(li)
                attention(li)
                add_out("w_out", li, 0, ("w_out", li))
                ffn(li)
            norm(("fn", 0))
            norm(("cn", 0))
            for e in range(ET):
                b = e % 2
                p0 = bank(("c", e, 0))
                v, s_, cv = CC[:, b, 0, :], CC[:, b, 1, :], CC[:, b, 2, :]
                dve.wait_ge(c_copy.sem, c_copy.after(e))
                dve.wait_ge(full, full_after(("c", e, 1)))
                p1 = bank(("c", e, 1))
                dve.wait_ge(c_z.sem, c_z.after(e))
                dve.tensor_tensor(v, p1[:, 0:256], v, ALU.mult).then_inc(taken_of(("c", e, 1)), 1)
                dve.wait_ge(*taken_after(("c", e, 1)))
                dve.wait_ge(vector_step, line.n)
                dve.tensor_scalar(cv, v, pcol(("cw2", 2), e), None, ALU.mult).then_inc(vector_step, line.one())
                dve.wait_ge(vector_step, line.n)
                dve.scalar_tensor_tensor(cv[:, 1:256], v[:, 0:255], pcol(("cw2", 1), e), cv[:, 1:256], ALU.mult, ALU.add).then_inc(vector_step, line.one())
                dve.wait_ge(vector_step, line.n)
                dve.scalar_tensor_tensor(cv[:, 2:256], v[:, 0:254], pcol(("cw2", 0), e), cv[:, 2:256], ALU.mult, ALU.add).then_inc(vector_step, line.one())
                dve.tensor_tensor(s_, p0[:, 0:256], s_, ALU.mult).then_inc(taken_of(("c", e, 0)), 1)
                dve.wait_ge(*taken_after(("c", e, 0)))
                dve.tensor_tensor(YC[:, e, :], s_, cv, ALU.mult).then_inc(c_out.sem, 1)
            add_out("c_out", 0, None, None)
            dve.wait_ge(full, full_after("vec"))
            dve.tensor_copy(vec, bank("vec")[0:NG * NH, 0:384]).then_inc(taken_of("vec"), 1)
            norm(("an", 0))
            for n, key in enumerate(QKEYS):
                g, a, j = key
                b = n % 2
                dve.wait_ge(q_rs.sem, q_rs.after(key))
                d = QK2[:, g, a, 2 * j:2 * j + 2, :].rearrange("p m (t n) -> p (m t) n", t=2)
                if a == 0:
                    d = backwards(d)
                ins = dve.scalar_tensor_tensor(d, bank(("qk", key)).rearrange("p (m n) -> p m n", m=4), pcol(("gain", a), g),
                                               RQ[:, b, :].rearrange("p (m n) -> p m n", m=4), ALU.mult, ALU.mult)
                ins.then_inc(taken_of(("qk", key)), 1)
            for st in range(len(BU) + 2):
                if st < len(BU):
                    u = st
                    h, t = BU[u]
                    b = u % 2
                    n = (t + 1) * P
                    if t == 0:
                        dve.wait_ge(s_bias[h % 3], 16 * (h // 3 + 1))
                    if u >= 2:
                        dve.wait_ge(full, full_after(("eT", u - 2, 1)))
                    for part_, gs in enumerate(((0, 1), (2,))):
                        key = ("s2", u, part_)
                        dve.wait_ge(full, full_after(key))
                        g0, ng = gs[0], len(gs)
                        src = bank(key).rearrange("p (g n) -> p g n", g=2)[:, 0:ng, 0:n]
                        dve.scalar_tensor_tensor(LG[:, b, g0:g0 + ng, 0:n], src, 0.125,
                                                           BIAS[:, h % 3, g0:g0 + ng, 256 - n:256], ALU.mult, ALU.add).then_inc(taken_of(key), 1)
                        dve.wait_ge(*taken_after(key))
                    dve.tensor_reduce(bred[:, b:b + 1], LG[:, b, :, 0:n], AX.XY, ALU.max).then_inc(vector_step, line.one())
                    dve.wait_ge(vector_step, line.n)
                    dve.tensor_scalar(bmax[:, b:b + 1], bred[:, b:b + 1], -1.0, None, ALU.mult).then_inc(b_max.sem, 1)
                if 0 <= st - 1 < len(BU):
                    u = st - 1
                    h, t = BU[u]
                    n = (t + 1) * P
                    key = ("eT", u, 1)
                    dve.wait_ge(full, full_after(key))
                    if u >= 2:
                        dve.wait_ge(full, full_after(("o2", u - 2)))
                    dve.tensor_copy(E3[:, u % 2, 512:512 + n], bank(key, n)).then_inc(taken_of(key), 1)
                    b = u % 2
                    dve.wait_ge(b_exp.sem, b_exp.after(BU[u]))
                    if u >= 2:
                        dve.wait_ge(*taken_after(("o2", u - 2)))
                    dve.reciprocal(brec[:, b:b + 1], bsum[:, b:b + 1]).then_inc(vector_step, line.one())
                    dve.wait_ge(vector_step, line.n)
                if 0 <= st - 2:
                    u = st - 2
                    h, t = BU[u]
                    b = u % 2
                    dve.wait_ge(full, full_after(("o2", u)))
                    dve.tensor_scalar(Y2[:, t, h * 64:(h + 1) * 64], bank(("o2", u), 64), brec[:, b:b + 1], None,
                                                      ALU.mult).then_inc(taken_of(("o2", u)), 1)
            for k in range(KT):
                dve.wait_ge(full, full_after(("yT", k)))
                dve.tensor_tensor(YT2[:, k, :], bank(("yT", k), 256), ZS[:, k, :], ALU.mult).then_inc(taken_of(("yT", k)), 1)
            for c in range(2):
                for t in range(2):
                    key = ("a_out", c, t)
                    dve.wait_ge(full, full_after(key))
                    r = RES[:, 2 + t, c * 512:(c + 1) * 512]
                    dve.tensor_tensor(r, bank(key), r, ALU.add).then_inc(taken_of(key), 1)


_INS = ["x", "c", "ctx", "c_ctx", "w_ada", "b_ada", "norm1_w", "norm2_w", "w_in", "lam_qk", "subln_w", "lb_param",
        "hgrn_norm_w", "w_fnet", "w_out", "w_up", "conv_w", "conv_b", "w_down", "final_norm_w", "conv_norm_2",
        "conv_w_in_2", "conv_w_2", "conv_w_out_2", "attn_norm_2", "attn_w_in_2", "attn_q_gain_2", "attn_k_gain_2",
        "attn_w_out_2", "rel_bias_2"]


def kernel(**inputs):
    import numpy as _np
    import concourse.bacc as _bacc
    from concourse import mybir as _mybir
    from concourse.bass_utils import run_bass_kernel_spmd as _run

    nc = _bacc.Bacc("TRN2", target_bir_lowering=False, num_devices=1)
    arrays, args = {}, {}
    for name in _INS:
        a = _np.ascontiguousarray(inputs[name])
        arrays[f"in_{name}_dram"] = a
        args[name] = nc.dram_tensor(f"in_{name}_dram", a.shape, _mybir.dt.from_np(a.dtype), kind="ExternalInput").ap()
    consts = []
    for name, a in zip(("wide", "masks", "hot", "tab"), constants()):
        arrays[f"const_{name}_dram"] = a
        consts.append(nc.dram_tensor(f"const_{name}_dram", a.shape, _mybir.dt.from_np(a.dtype), kind="ExternalInput").ap())
    out = nc.dram_tensor("out_0_dram", (1, SEQ, DM), F32, kind="ExternalOutput").ap()
    program(nc, args, *consts, out)
    r = _run(nc, [arrays], core_ids=[0])
    return r.results[0]["out_0_dram"]
```

```python
import math
from contextlib import ExitStack

import numpy as np

import concourse.bass as bass
from concourse import mybir

F32 = mybir.dt.float32
F32R = mybir.dt.float32r
U8 = mybir.dt.uint8
ALU = mybir.AluOpType
ACT = mybir.ActivationFunctionType
AX = mybir.AxisListType

P = 128
DM = 1024
KT = DM // P
SEQ = 256
NT = 4
DEPTH = 2
EPS = 1e-6
NH_A = 4
DFF = 2816
FT = DFF // P
CEXP = 2048
ET = CEXP // P
NG = 3
NH = 16
LEVELS = 8
BANKS = 8
SLOTS = 4
SLOT = KT * 256
HIGH = 2
NEG = -1.0e30


def level_block(level):
    return 2 ** (level - 1)


def scan_matrices():
    u, tau = np.arange(P)[:, None], np.arange(P)[None, :]
    out = np.zeros((P, 2, 9, P), np.float32)
    for level in range(1, LEVELS):
        b = level_block(level)
        mid = tau // (2 * b) * 2 * b + b
        out[:, 0, level - 1] = np.where(tau >= mid, (u >= mid) & (u <= tau), (u > tau) & (u < mid))
        out[:, 1, level - 1] = np.where(tau < mid, (u >= tau) & (u < mid), (u >= mid) & (u < tau))
    out[:, 0, 7], out[:, 1, 7] = u <= tau, u >= tau
    out[:, 0, 8], out[:, 1, 8] = u > tau, u < tau
    return out.reshape(P, -1)


def level_masks():
    s, t = np.arange(P)[:, None], np.arange(P)[None, :]
    out = np.zeros((P, 2, LEVELS, P), np.float32)
    out[:, 0, 0] = out[:, 1, 0] = s == t
    for level in range(1, LEVELS):
        b = level_block(level)
        same = s // (2 * b) == t // (2 * b)
        out[:, 0, level] = same & (s // b % 2 == 0) & (t // b % 2 == 1)
        out[:, 1, level] = same & (s // b % 2 == 1) & (t // b % 2 == 0)
    return out.reshape(P, -1)


def rope_tables():
    pos = np.arange(SEQ)
    half = 32
    inv = (np.float32(10000.0) ** (-np.arange(0, half, 2, dtype=np.float32) / half)).astype(np.float32)
    ar = (pos // 64).astype(np.float32)[:, None] * inv
    ac = (pos % 64).astype(np.float32)[:, None] * inv
    ang = np.concatenate([ar, ar, ac, ac], axis=-1).T
    ang = np.concatenate([ang, ang], axis=0)
    return np.cos(ang).astype(np.float32), np.sin(ang).astype(np.float32)


def rotate_matrix():
    r = np.zeros((P, P), np.float32)
    for base in range(0, P, 32):
        for m in range(16):
            r[base + m + 16, base + m] = -1.0
            r[base + m, base + m + 16] = 1.0
    return r


def t5_bucket(dist):
    d = np.maximum(dist, 1).astype(np.float32)
    large = 16 + (np.log(d / np.float32(16)) / np.float32(math.log(2048 / 16)) * np.float32(16)).astype(np.int32)
    return np.where(dist < 16, dist, np.minimum(large, 31))


def constants():
    ident = np.eye(P, dtype=np.float32)
    k = np.arange(SEQ, dtype=np.float64)
    ang = 2 * np.pi * (np.outer(k, k) % SEQ) / SEQ
    scale = 1.0 / math.sqrt(SEQ * 64)
    both = np.concatenate([np.cos(ang), np.sin(ang)], axis=1) * scale
    dft_seq = both.reshape(2, P, 512).transpose(1, 0, 2).reshape(P, -1).astype(np.float32)
    d = np.arange(64, dtype=np.float64)
    ang = 2 * np.pi * (np.outer(d, d) % 64) / 64
    two = np.eye(2)
    dft_cos = np.kron(two, np.cos(ang)).astype(np.float32)
    dft_sin = np.kron(two, -np.sin(ang)).astype(np.float32)
    cos, sin = rope_tables()
    sel = np.zeros((P, 2, P), np.float32)
    sel[0, 0], sel[1, 1] = 1.0, 1.0
    means = np.kron(two, np.ones((64, 64))).astype(np.float32)
    wide = np.concatenate([ident, ident[::-1], sel.reshape(P, -1), means, dft_seq, dft_cos, dft_sin, rotate_matrix(), cos, sin,
                           scan_matrices()], axis=1)
    dist = 255 - np.arange(384)
    hot = np.zeros((32 + NG, 384), np.float32)
    tab = np.zeros((NG, NG * NH), np.float32)
    bucket = t5_bucket(np.maximum(dist, 0))
    for m in range(384):
        hot[bucket[m], m] = 1.0
    for g, dil in enumerate((1, 4, 16)):
        hot[32 + g] = ~((dist >= 0) & (dist % dil == 0) & (dist // dil <= 128))
        tab[g, g * NH:(g + 1) * NH] = NEG
    return np.ascontiguousarray(wide), level_masks(), hot, tab


class Signal:

    def __init__(self, sem, keys):
        self.sem = sem
        self.count = {k: i + 1 for i, k in enumerate(keys)}

    def after(self, key):
        return self.count[key]


class Line:

    def __init__(self):
        self.n = 0

    def one(self):
        self.n += 1
        return 1


def program(nc, A, wide_c, mask_c, hot_c, tab_c, out):
    ctx = ExitStack()

    def sb(name, cols, dt=F32, rows=P):
        return ctx.enter_context(nc.sbuf_tensor(name, [rows, cols], dt))

    def sem(name):
        return ctx.enter_context(nc.semaphore(name))

    with ctx:
        def at_top(name, cols, dt, above):
            return nc.alloc_sbuf_tensor_at(name, [P, cols], dt, offset=top + 4 * above)

        top = (nc.sbuf_top - 4 * (SLOTS * SLOT + 2 * KT * 512)) // 32 * 32
        ring = at_top("weights", SLOTS * SLOT, F32, 0)
        ring_lo = at_top("weights_low", SLOTS * SLOT, F32R, 0)
        ht_hi = at_top("normed_t_high", KT * 512, F32R, SLOTS * SLOT)
        ht_lo = at_top("normed_t_low", KT * 512, F32R, SLOTS * SLOT + KT * 512)
        ht_r = at_top("mixer_scratch", KT * 512, F32, SLOTS * SLOT)
        ht_b = at_top("mixer_scratch_2", KT * 512, F32, SLOTS * SLOT + KT * 512)
        ring_hi = sb("weights_high", HIGH * SLOT, F32R)
        res = sb("residual", NT * DM)
        arena = sb("arena", 12288)
        mg = sb("merge_and_gates", 6144)
        scr = sb("scratch", 3840)
        wide = sb("wide_consts", 128 * 4 + 128 + 1024 + 256 + 128 + 512 + 2304)
        masks = sb("level_masks_sb", 2 * LEVELS * P, U8)
        cols = sb("param_columns", 600)
        small = sb("small", 376)
        assert nc.sbuf_base <= top
        ps = ctx.enter_context(nc.psum_tensor("acc", [P, BANKS, 512], F32))

        RES = res[:, :].rearrange("p (t n) -> p t n", t=NT)
        HH = ht_hi[:, :].rearrange("p (k n) -> p k n", k=KT)
        HL = ht_lo[:, :].rearrange("p (k n) -> p k n", k=KT)
        MT = mg[:, 0:4096].rearrange("p (k n) -> p k n", k=8)
        XS = mg[:, 0:4096].rearrange("p (t n) -> p t n", t=NT)
        GB = mg[:, 4096:6144].rearrange("p (s n) -> p s n", s=2)
        SP = mg[:, 0:2048].rearrange("p (t n) -> p t n", t=NT)
        BG = mg[:, 2048:4096].rearrange("p (t n) -> p t n", t=NT)
        KTOK = ht_b[:, 0:2048].rearrange("p (t n) -> p t n", t=NT)
        OREC = mg[:, 2048:3072].rearrange("p (t n) -> p t n", t=NT)
        V2 = mg[:, 0:6144].rearrange("p (g t n) -> p g t n", g=NG, t=2)
        ZS = res[:, 0:2048].rearrange("p (k n) -> p k n", k=KT)
        VA = arena[:, 0:2048].rearrange("p (t n) -> p t n", t=NT)
        GL = arena[:, 2048:4096].rearrange("p (t n) -> p t n", t=NT)
        IH = arena[:, 4096:5120].rearrange("p (t n) -> p t n", t=NT)
        GH = arena[:, 5120:6144].rearrange("p (t n) -> p t n", t=NT)
        UF = arena[:, 6144:7168].rearrange("p (t n) -> p t n", t=NT)
        QA = arena[:, 7168:9216].rearrange("p (h n) -> p h n", h=NH_A)
        KA = arena[:, 9216:11264].rearrange("p (h n) -> p h n", h=NH_A)
        QH = arena[:, 11264:12288].rearrange("p (k n) -> p k n", k=2)
        HF = arena[:, 0:FT * 512].rearrange("p (f n) -> p f n", f=FT)
        YC = arena[:, 0:ET * SEQ].rearrange("p (f n) -> p f n", f=ET)
        QK2 = arena[:, :].rearrange("p (g a h n) -> p g a h n", g=NG, a=2, h=8)
        at = [0]

        def part(t, n, pos=at):
            pos[0] += n
            return t[:, pos[0] - n:pos[0]]

        ident = part(wide, 128)
        flip = part(wide, 128)
        sel = part(wide, 256).rearrange("p (s n) -> p s n", s=2)
        means = part(wide, 128)
        dft_seq = part(wide, 1024).rearrange("p (k n) -> p k n", k=2)
        dft_cos, dft_sin, rot = part(wide, 128), part(wide, 128), part(wide, 128)
        cosT, sinT = part(wide, 256), part(wide, 256)
        m0 = at[0]
        SM = part(wide, 2304).rearrange("p (d l n) -> p d l n", d=2, l=9)
        BIAS = wide[:, m0:m0 + 2304].rearrange("p (b g n) -> p b g n", b=3, g=NG)
        MASK = masks[:, :].rearrange("p (d l n) -> p d l n", d=2, l=LEVELS)
        pos = [0]

        def sm(n):
            return part(small, n, pos)

        ssq, rstd, EPS_COL = sm(4), sm(4), sm(1)
        modt = sm(128).rearrange("p (l m k s) -> p l m k s", l=2, m=4, k=KT)
        csil = sm(16).rearrange("p (s k) -> p s k", s=2)
        nscale = sm(16).rearrange("p (k s) -> p k s", k=KT)
        hw = sm(128).rearrange("p (l n) -> p l n", l=2)
        lam2 = sm(4).rearrange("p (l a) -> p l a", l=2)
        neglam = sm(2)
        amax = sm(4).rearrange("p (b c) -> p b c", b=2)
        asum = sm(4).rearrange("p (b c) -> p b c", b=2)
        arec = sm(4).rearrange("p (b c) -> p b c", b=2)
        ossq, orstd = sm(2), sm(2)
        hssq, hrstd = sm(16).rearrange("p (t h) -> p t h", t=4), sm(16).rearrange("p (t h) -> p t h", t=4)
        minus_half = sm(4)
        bred, bmax, bsum, brec = sm(2), sm(2), sm(2), sm(2)
        rows = scr[:, 0:640].rearrange("p (c n) -> p c n", c=5)
        lam_rows = scr[:, 640:1152].rearrange("p (l a n) -> p l a n", l=2, a=4)
        lam_tmp = scr[:, 1152:1216]
        lb_rows = scr[:, 2048:3072].rearrange("p (l n) -> p l n", l=2)
        XE = [scr[:, 0:2048].rearrange("p (q l n) -> p q l n", q=2, l=8),
              ht_r[:, 0:2048].rearrange("p (q l n) -> p q l n", q=2, l=8)]
        KTT = scr[:, 2048:2560].rearrange("p (b q n) -> p b q n", b=2, q=2)
        ACC = scr[:, 2560:3584].rearrange("p (d a h n) -> p d a h n", d=2, a=2, h=2)
        ST = scr[:, 3584:3840].rearrange("p (d q n) -> p d q n", d=2, q=2)
        SE = ht_r[:, 2048:2568].rearrange("p (b n) -> p b n", b=2)
        KD = ht_r[:, 2568:3080].rearrange("p (b n) -> p b n", b=2)
        rope_t = scr[:, 1536:2048].rearrange("p (b n) -> p b n", b=2)
        FS = ht_r[:, 0:1024].rearrange("p (f n) -> p f n", f=2)
        YT4 = ht_r[:, 1024:1536].rearrange("p (f n) -> p f n", f=2)
        wf = scr[:, 3072:3584].rearrange("p (f n) -> p f n", f=2)
        E2 = ht_r[:, 0:2048].rearrange("p (b c n) -> p b c n", b=2, c=2)
        AT = ht_r[:, 2048:3072].rearrange("p (b n) -> p b n", b=2)
        ON = ht_r[:, 3072:3328].rearrange("p (b n) -> p b n", b=2)
        wo_t = scr[:, 0:1024].rearrange("p (b n) -> p b n", b=2)
        grow = scr[0:2, 3584:3840]
        n_t = scr[:, 1024:2048].rearrange("p (b n) -> p b n", b=2)
        FC = scr[:, 0:3072].rearrange("p (b a n) -> p b a n", b=2, a=3)
        CC = scr[:, 0:2048].rearrange("p (b a n) -> p b a n", b=2, a=4)
        SQ = scr[:, 0:1024].rearrange("p (b n) -> p b n", b=2)
        RQ = scr[:, 1024:3072].rearrange("p (b n) -> p b n", b=4)
        LG = scr[:, 0:1536].rearrange("p (b g n) -> p b g n", b=2, g=NG)
        E3 = scr[:, 1536:3072].rearrange("p (b n) -> p b n", b=2)
        Y2 = ht_r[:, 0:2048].rearrange("p (t n) -> p t n", t=2)
        YT2 = ht_r[:, 2048:4096].rearrange("p (k n) -> p k n", k=KT)
        hot = res[0:32 + NG, 0:384]
        tabx = res[0:32 + NG, 384:384 + NG * NH]
        vec = res[0:NG * NH, 512:512 + 384]
        vec_d = nc.dram_tensor("bias_rows", [NG * NH, 384], F32, kind="Internal").ap()

        slot_in = [sem(f"slot_in{i}") for i in range(SLOTS)]
        slot_part = sem("slot_read_part_way")
        read_at, parts_read = [], [0]
        full = sem("psum_full")
        taken = [sem(f"psum_taken{i}") for i in range(BANKS)]
        s_in, s_const = sem("residual_in"), sem("constants_in")
        s_small, s_eps, s_mask = sem("small_in"), sem("eps_ready"), sem("masks_ready")
        s_half = sem("minus_half_ready")
        s_lb = sem("bounds_in")
        s_wf = sem("fnet_in")
        s_gb = sem("gate_bias_in")
        s_fw = sem("final_weight_in")
        s_vec = sem("bias_rows_out")
        s_hot = sem("hot_in")
        s_bias = [sem(f"bias_in{i}") for i in range(3)]
        s_out = sem("result_out")
        vector_step, scalar_step, pool_step = sem("vector_step"), sem("scalar_step"), sem("pool_step")

        def S(name, keys):
            return Signal(sem(name), keys)

        NORMS = [("n1", 0), ("n2", 0), ("n1", 1), ("n2", 1), ("fn", 0), ("cn", 0), ("an", 0)]

        def norm_tiles(N):
            return range(NT) if N in (("n1", 0), ("n2", 0), ("n1", 1)) else range(2, NT)

        nk = [(N, t) for N in NORMS for t in norm_tiles(N)]
        squared = S("row_squares", nk)
        row_scale = S("row_scale", nk)
        scaled = S("scaled", [k for k in nk if k[0] != ("fn", 0)])
        res_new = S("residual_new", [("w_out", 0), ("w_down", 0), ("w_out", 1), ("w_down", 1), ("final", 0)])
        c_ready = sem("c_ready")
        lam_sum, lam_exp = sem("lam_sum"), sem("lam_exp")
        lb_abs, lb_exp = sem("lb_difference"), sem("lb_logs")
        gate_keys = [(li, t) for li in range(DEPTH) for t in range(NT)]
        z_soft = S("z_softplus", gate_keys)
        b_gap = S("bound_gap", [k for k in gate_keys if k[0]])
        b_soft = S("bound_softplus", [k for k in gate_keys if k[0]])
        g_ready = S("g_ready", gate_keys)
        k_ready = S("k_ready", gate_keys)

        def units(li):
            out_ = []
            for f, b in ((0, 1), (1, 0), (2, 3), (3, 2)):
                out_ += [(0, f), (1, b)]
            return out_

        UN = [(li, i) for li in range(DEPTH) for i in range(8)]

        def is_full(li, i):
            return li == 0 or i >= 4

        z_ready = S("z_ready", [u for u in UN if is_full(*u)])
        kd_ready = S("kd_ready", [u for u in UN if u[1] < 6])
        rec_keys = [(li, t) for li in range(DEPTH) for t in (range(NT) if li == 0 else range(2, NT))]
        rec_sum = S("rec_sum", rec_keys)
        og_exp = S("og_exp", rec_keys)
        rec_ready = S("rec_ready", rec_keys)

        def att_units(li):
            return [(t, h) for t in (range(NT) if li == 0 else range(2, NT)) for h in range(NH_A)]

        AU = [(li, u) for li in range(DEPTH) for u in range(len(att_units(li)))]
        a_max = S("a_max", AU)
        a_exp = S("a_exp", AU)
        a_ready = S("a_ready", AU)
        o_sq = S("o_squared", AU)
        o_rs = S("o_scale", AU)
        FK = [(li, f) for li in range(DEPTH) for f in range(FT)]
        f_mid = S("ff_centre", [(li, 2 * f2 + j, a) for li in range(DEPTH) for f2 in range(FT // 2) for a in range(2) for j in range(2)])
        f_exp = S("ff_silu", FK)
        f_out = S("ff_product", FK)
        CK = list(range(ET))
        c_out = S("conv_product", CK)
        QKEYS = [(g, a, j) for g in range(NG) for a in range(2) for j in range(4)]
        q_sq = S("qk_squared", QKEYS)
        q_rs = S("qk_scale", QKEYS)
        q_done = S("qk_scaled", QKEYS)
        zk = [(c, t) for c in range(2) for t in range(2)]
        BU = [(h, t) for h in range(NH) for t in range(2)]
        b_max = S("b_max", BU)
        b_exp = S("b_exp", BU)

        CONV_J = [(e, j) for e in range(ET // 2) for j in range(2)]
        col_loads = []
        ncol = [0]

        def column(rows_ap, n, halves=False):
            c0 = ncol[0]
            ncol[0] += n
            done = 0
            while done < n:
                c, r = divmod(c0 + done, P)
                m = min(n - done, P - r)
                col_loads.append((rows_ap[done:done + m, :], c, r, m, halves))
                done += m
            return c0

        def as_rows(ap):
            return ap.rearrange("(r n) -> r n", n=P)

        col = {"c": column(as_rows(A["c"].rearrange("a n -> (a n)")), 8), "cc": column(as_rows(A["c_ctx"]), 8)}
        for li in range(DEPTH):
            col["b_ada", li] = column(as_rows(A["b_ada"][li, :]), 48)
            col["n1", li] = column(as_rows(A["norm1_w"][li, :]), 8)
            col["n2", li] = column(as_rows(A["norm2_w"][li, :]), 8)
            col["subln", li] = column(A["subln_w"][li:li + 1, :], 1)
            for j in range(3):
                col["cw", li, j] = column(as_rows(A["conv_w"][li, j, :]), 2 * FT)
            col["cb", li] = column(as_rows(A["conv_b"][li, :]), 2 * FT)
        col["cn", 0] = column(as_rows(A["conv_norm_2"][0, :]), 8)
        col["an", 0] = column(as_rows(A["attn_norm_2"][0, :]), 8)
        for j in range(3):
            col["cw2", j] = column(as_rows(A["conv_w_2"][0, j, :]), ET)
        col["gain", 0] = column(A["attn_q_gain_2"][0, :, :], NG, True)
        col["gain", 1] = column(A["attn_k_gain_2"][0, :, :], NG, True)
        NCOL = ncol[0]
        assert NCOL <= 640
        small_ins = [(lam_rows.rearrange("p l a n -> p (l a n)"), A["lam_qk"].rearrange("l a n -> (l a n)").partition_broadcast(P)),
                     (hw.rearrange("p l n -> p (l n)"), A["hgrn_norm_w"].rearrange("l n -> (l n)").partition_broadcast(P))]
        for src, c, r, m, halves in col_loads:
            if halves:
                small_ins += [(rows[r:r + m, c, 0:64], src), (rows[r:r + m, c, 64:128], src)]
            else:
                small_ins.append((rows[r:r + m, c, :], src))

        def pcol(key, j=0):
            return cols[:, col[key] + j:col[key] + j + 1]

        def slot(n, t=None):
            return (ring if t is None else t)[:, (n % SLOTS) * SLOT:(n % SLOTS + 1) * SLOT]

        plan = []
        split_no = {}

        def plan_slot(key, split, src):
            if split:
                split_no[key] = len(split_no)
            plan.append((key, split, src))

        def by_columns(key, split, w, c0):
            plan_slot(key, split, w[:, c0:c0 + 256].rearrange("(k p) n -> p k n", p=P))

        def by_rows(key, split, w, r0, nrow, c0):
            plan_slot(key, split, w[r0:r0 + nrow * P, c0:c0 + 512].rearrange("(k p) n -> p k n", p=P))

        GATES = {2: 0, 5: 1}
        FILL = {("w_in", 0): [(0, n) for n in range(8, 20)],
                ("w_up", 0): [(0, n) for n in range(20, 24)] + [(1, n) for n in range(8)],
                ("w_in", 1): [(1, n) for n in range(8, 20)],
                ("w_up", 1): [(1, n) for n in range(20, 24)]}

        def fill(stage, n):
            return FILL[stage][n:n + 1]

        def plan_ada(li, n):
            by_columns(("ada", li, n), False, A["w_ada"][li, :, :], 256 * n)

        W_IN = [("qa", 0, 0), ("qa", 1, 256), ("ka", 0, 512), ("ka", 1, 768), ("va", 0, 1024), ("va", 1, 1024),
                ("ihgh", 0, 2304), ("ihgh", 1, 2304), ("qh", 0, 1536), ("uf", 0, 2816), ("zz", 0, 1792), ("zz", 1, 1792)]
        DOWN = [(4 * i, min(4, FT - 4 * i)) for i in range((FT + 3) // 4)]
        for n in range(8):
            plan_ada(0, n)
        for li in range(DEPTH):
            W = A["w_in"][li, :, :]
            for n, (name, h, c0) in enumerate(W_IN):
                if name in ("va", "ihgh", "zz"):
                    by_rows(("w_in", li, name, h), True, W, 512 * h, 4, c0)
                else:
                    by_columns(("w_in", li, name, h), True, W, c0)
                for lj in fill(("w_in", li), n):
                    plan_ada(*lj)
            for c in range(2):
                for h in range(2):
                    by_rows(("w_out", li, c, h), False, A["w_out"][li, :, :], 512 * h, 4, 512 * c)
            for f2 in range(FT // 2):
                for a in range(2):
                    by_columns(("w_up", li, f2, a), True, A["w_up"][li, :, :], DFF * a + 256 * f2)
                    for lj in fill(("w_up", li), 2 * f2 + a):
                        plan_ada(*lj)
            for c in range(2):
                for r0, nrow in DOWN:
                    by_rows(("w_down", li, c, r0), True, A["w_down"][li, :, :], P * r0, nrow, 512 * c)
        C_IN = (1, 2, 3, 0)
        for e in range(ET // 2):
            for q in C_IN:
                by_columns(("c_in", e, q), True, A["conv_w_in_2"][0, :, :], CEXP * q + 256 * e)
        C_OUT = [(4 * i, 4) for i in range(ET // 4)]
        for c in range(2):
            for r0, nrow in C_OUT:
                by_rows(("c_out", c, r0), True, A["conv_w_out_2"][0, :, :], P * r0, nrow, 512 * c)
        W = A["attn_w_in_2"][0, :, :]
        A_IN = []
        for g in range(NG):
            A_IN += [(g, a, j) for a in range(2) for j in range(4)] + [(g, 2, j) for j in range(4)]
        A_IN += [("z", 0, j) for j in range(4)]
        for g, a, j in A_IN:
            if a == 2:
                by_rows(("a_in", g, a, j), True, W, 512 * (j % 2), 4, g * 3072 + 2048 + 512 * (j // 2))
            else:
                by_columns(("a_in", g, a, j), True, W, (NG * 3072 if g == "z" else g * 3072 + a * 1024) + 256 * j)
        for c in range(2):
            for h in range(2):
                by_rows(("a_out", c, h), False, A["attn_w_out_2"][0, :, :], 512 * h, 4, 512 * c)
        item = {key: n for n, (key, _, _) in enumerate(plan)}
        split_keys = list(split_no)
        hi_in = S("weights_high_ready", split_keys)
        lo_in = S("weights_split", split_keys)
        FS_KEYS = [("w_down", 0, c, r) for c in range(2) for r, _ in DOWN] + [("w_down", 1, c, r) for c in range(2) for r, _ in DOWN]
        FS_KEYS += [("c_out", c, r) for c in range(2) for r, _ in C_OUT]
        part_hi = S("products_high_ready", FS_KEYS)
        part_lo = S("products_split", FS_KEYS)
        ht_done = S("normed_split", [(N, k) for N in NORMS if N[0] != "fn" for k in range(KT)])

        def stage_keys(stage):
            return [k for k in split_keys if k[:len(stage)] == stage]

        def hi_slot(key):
            m = split_no[key] % HIGH
            return ring_hi[:, m * SLOT:(m + 1) * SLOT]

        group = {}
        finished = {}

        def bank(key, n=512):
            return ps[:, group[key] % BANKS, 0:n]

        def full_after(key):
            return finished[key]

        def taken_of(key):
            return taken[group[key] % BANKS]

        def taken_after(key):
            return taken_of(key), group[key] // BANKS + 1

        def backwards(ap):
            *dims, (step, count) = ap.ap
            return bass.AP(tensor=ap.tensor, offset=ap.offset + step * (count - 1), ap=[*[list(d) for d in dims], [-step, count]])

        def cols_of(t):
            return slice(t * P, (t + 1) * P)

        def stream_of(t):
            return 0 if t >= 2 else 1

        block = ctx.enter_context(nc.Block())

        @block.tensor
        def _(pe):
            read = [0]

            def closed(key):
                finished[key] = len(finished) + 1
                return 1

            def open_group(key, closes_next=True):
                n = len(group)
                group[key] = n
                if closes_next:
                    closed(key)
                if n >= BANKS:
                    pe.wait_ge(taken[n % BANKS], n // BANKS)
                return ps[:, n % BANKS, :]

            def weights(key):
                n = read[0]
                assert plan[n][0] == key, (plan[n][0], key)
                read[0] += 1
                if not plan[n][1]:
                    pe.wait_ge(slot_in[n % SLOTS], 16 * (n // SLOTS + 1))
                    return slot(n)
                pe.wait_ge(lo_in.sem, lo_in.after(key))
                return hi_slot(key), slot(n, ring_lo)

            def halves(w, k):
                return [x.rearrange("p (k n) -> p k n", k=k) for x in w]

            def product(o, a, b, start, stop):
                (ah, al), (bh, bl) = a, b
                pe.matmul(o, ah, bh, start=start, stop=False)
                pe.matmul(o, ah, bl, start=False, stop=False)
                return pe.matmul(o, al, bh, start=False, stop=stop)

            def release(part_way=None):
                if part_way is None:
                    read_at.append((full, len(finished)))
                else:
                    part_way.then_inc(slot_part, 1)
                    parts_read[0] += 1
                    read_at.append((slot_part, parts_read[0]))

            def norm(N):
                first = True
                for k in range(KT):
                    o = open_group((N, k))
                    for t in norm_tiles(N):
                        if first:
                            pe.wait_ge(scaled.sem, scaled.after((N, t)))
                        last = pe.transpose(o[:, cols_of(t)], XS[:, t, k * P:(k + 1) * P], ident)
                    first = False
                    last.then_inc(full, 1)

            def wait_normed(N):
                pe.wait_ge(ht_done.sem, ht_done.after((N, KT - 1)))

            def ada(li, n):
                w = weights(("ada", li, n)).rearrange("p (k n) -> p k n", k=KT)
                o = open_group(("ada", li, n))
                if n // 4 in GATES:
                    for k in range(KT):
                        last = pe.matmul(o[0:2, 0:256], csil[:, :, k], w[:, k, :], start=(k == 0), stop=(k == KT - 1))
                else:
                    for m in range(2):
                        for k in range(KT):
                            last = pe.matmul(o[:, 2 * m:2 * m + 2], w[:, k, m * P:(m + 1) * P], csil[:, :, k],
                                             start=(k == 0), stop=(k == KT - 1))
                last.then_inc(full, 1)
                release()
                if n // 4 in GATES:
                    pe.wait_ge(*taken_after(("ada", li, n)))
                    for s in range(2 if li == 0 else 1):
                        o = open_group(("gb", li, n, s))
                        pe.matmul(o[:, 0:256], sel[0:2, s, :], grow, start=True, stop=True).then_inc(full, 1)

            def t_out(key, w, m, cs, c0=0, open_=True, close_=True):
                o = open_group(key) if open_ else ps[:, group[key] % BANKS, :]
                wh, wl = halves(w, KT)
                for k in range(KT):
                    last = product(o[:, c0:c0 + cs.stop - cs.start], (wh[:, k, m * P:(m + 1) * P], wl[:, k, m * P:(m + 1) * P]),
                                   (HH[:, k, cs], HL[:, k, cs]), k == 0, k == KT - 1)
                if close_:
                    last.then_inc(full, 1)

            def tok_out(key_of, name, tiles, n_of, c_of=cols_of):
                outs = {}
                for h in range(2):
                    wh, wl = halves(weights((*name, h)), 4)
                    for t in tiles:
                        if h == 0:
                            outs[t] = open_group(key_of(t), closes_next=False)
                        n = n_of(t)
                        for k in range(4):
                            last = product(outs[t][:, 0:n], (HH[:, 4 * h + k, c_of(t)], HL[:, 4 * h + k, c_of(t)]),
                                           (wh[:, k, 0:n], wl[:, k, 0:n]), h == 0 and k == 0, h == 1 and k == 3)
                        if h == 1:
                            last.then_inc(full, closed(key_of(t)))
                    release(last if h == 0 else None)
                    yield

            def w_in(li):
                live = range(NT) if li == 0 else range(2, NT)
                xcols = slice(0, 512) if li == 0 else slice(256, 512)
                wait_normed(("n1", li))
                n = 0

                def after():
                    for lj in fill(("w_in", li), n):
                        ada(*lj)

                for name, cs in (("qa", xcols), ("ka", slice(0, 512))):
                    for h in range(2):
                        w = weights(("w_in", li, name, h))
                        for m in range(2):
                            t_out((name, li, 2 * h + m), w, m, cs)
                        release()
                        after()
                        n += 1
                for name, X in (("qa", QA), ("ka", KA)):
                    for h in range(NH_A):
                        pe.wait_ge(*taken_after((name, li, h)))
                        o = open_group(("rot", name, li, h))
                        pe.matmul(o[:, 0:256], rot, X[:, h, 256:512], start=True, stop=True).then_inc(full, 1)
                for name in ("va", "ihgh"):
                    for _ in tok_out(lambda t: (name, li, t), ("w_in", li, name), range(NT),
                                     lambda t: 256 if name == "ihgh" and t not in live else 512):
                        after()
                        n += 1
                w = weights(("w_in", li, "qh", 0))
                for p in range(2):
                    t_out(("qh", li, p), w, p, xcols)
                release()
                after()
                n += 1
                wh, wl = halves(weights(("w_in", li, "uf", 0)), KT)
                for t in live:
                    o = open_group(("uf", li, t))
                    for k in range(KT):
                        last = product(o[:, 0:256], (HH[:, k, cols_of(t)], HL[:, k, cols_of(t)]), (wh[:, k, :], wl[:, k, :]),
                                       k == 0, k == KT - 1)
                    last.then_inc(full, 1)
                release()
                after()
                n += 1
                for _ in tok_out(lambda t: ("zz", li, t), ("w_in", li, "zz"), range(NT), lambda t: 512):
                    after()
                    n += 1

            def fourier(li):
                streams = (0, 1) if li == 0 else (1,)
                pe.wait_ge(s_wf, 16 * (li + 1))
                for s in streams:
                    for f in range(2):
                        o = open_group(("f1", li, s, f))
                        for k in range(2):
                            t = 2 * s + k
                            pe.wait_ge(*taken_after(("uf", li, t)))
                            last = pe.matmul(o[:, :], UF[:, t, f * P:(f + 1) * P], dft_seq[:, k, :],
                                             start=(k == 0), stop=(k == 1))
                        last.then_inc(full, 1)
                    o = open_group(("f2", li, s))
                    for f in range(2):
                        pe.wait_ge(*taken_after(("f1", li, s, f)))
                        pe.matmul(o[:, f * 256:(f + 1) * 256], dft_cos, FS[:, f, 0:256], start=True, stop=False)
                        last = pe.matmul(o[:, f * 256:(f + 1) * 256], dft_sin, FS[:, f, 256:512], start=False, stop=True)
                    last.then_inc(full, 1)
                    pe.wait_ge(*taken_after(("f2", li, s)))
                    o = open_group(("f3", li, s))
                    for c in range(2):
                        for f in range(2):
                            last = pe.matmul(o[:, c * 256:(c + 1) * 256], wf[:, f, c * P:(c + 1) * P], YT4[:, f, :],
                                             start=(f == 0), stop=(f == 1))
                    last.then_inc(full, 1)

            def hgrn(li):
                un = units(li)

                def gates(i):
                    d, t = un[i]
                    pe.wait_ge(g_ready.sem, g_ready.after((li, t)))
                    pe.wait_ge(k_ready.sem, k_ready.after((li, t)))
                    if is_full(li, i):
                        o = open_group(("kT", li, i))
                        for p in range(2):
                            last = pe.transpose(o[:, p * P:(p + 1) * P], KTOK[:, t, d * 256 + p * P:d * 256 + (p + 1) * P], ident)
                        last.then_inc(full, 1)
                        for p in range(2):
                            for hf in range(2):
                                o = open_group(("E", li, i, p, hf))
                                pe.matmul(o[:, :], GL[:, t, d * 256 + p * P:d * 256 + (p + 1) * P],
                                                SM[:, d, 4 * hf:4 * hf + 4, :], start=True, stop=True).then_inc(full, 1)
                    if i < 6:
                        o = open_group(("suf", li, i))
                        pe.matmul(o[:, 0:256], SM[:, d, 8, :], GL[:, t, d * 256:(d + 1) * 256], start=True, stop=True)
                        end = (P - 1) * (1 - d)
                        for p in range(2):
                            last = pe.matmul(o[:, 256 + p:257 + p], GL[:, t, d * 256 + p * P:d * 256 + (p + 1) * P],
                                             SM[:, d, 7, end:end + 1], start=True, stop=True)
                        last.then_inc(full, 1)

                def apply(i):
                    d, t = un[i]
                    b = i % 2
                    if is_full(li, i):
                        pe.wait_ge(z_ready.sem, z_ready.after((li, i)))
                        pe.wait_ge(*taken_after(("kT", li, i)))
                        if i == (0 if li == 0 else 4):
                            for p in range(2):
                                pe.wait_ge(*taken_after(("qh", li, p)))
                        for lp in range(4):
                            for par in range(2):
                                o = open_group(("S", li, i, lp, par))
                                r = slice(64 * par, 64 * par + 64)
                                for lv in range(2):
                                    level = 2 * lp + lv
                                    for p in range(2):
                                        c = (lv * 2 + p) * P
                                        if level == 0:
                                            zk_, zq_ = KTT[r, b, p, :], QH[r, p, cols_of(t)]
                                        else:
                                            zk_ = zq_ = XE[b][r, p, level - 1, :]
                                        last = pe.matmul(o[:, c:c + P], zk_, zq_, start=True, stop=True)
                                last.then_inc(full, 1)
                        for par in range(2):
                            o = open_group(("O", li, i, par))
                            r = slice(64 * par, 64 * par + 64)
                            pe.wait_ge(*taken_after(("S", li, i, 3, par)))
                            if i >= 2:
                                pe.wait_ge(*taken_after(("SU", li, i - 2)))
                            for p in range(2):
                                h = 2 * p + par
                                last = pe.matmul(o[:, p * 64:(p + 1) * 64], ACC[:, d, par, p, :], IH[:, t, h * 64:(h + 1) * 64],
                                                 start=True, stop=(i < 2))
                                if i >= 2:
                                    last = pe.matmul(o[:, p * 64:(p + 1) * 64], XE[b][r, p, 7, :], ST[r, d, p, :],
                                                     start=False, stop=True)
                            last.then_inc(full, 1)
                    if i < 6:
                        pe.wait_ge(kd_ready.sem, kd_ready.after((li, i)))
                        o = open_group(("SU", li, i))
                        for p in range(2):
                            last = pe.matmul(o[:, p * P:(p + 1) * P], KD[:, b, p * P:(p + 1) * P], IH[:, t, p * P:(p + 1) * P],
                                             start=True, stop=True)
                        last.then_inc(full, 1)

                for t in range(NT):
                    pe.wait_ge(*taken_after(("ihgh", li, t)))
                gates(0)
                for i in range(8):
                    if i + 1 < 8:
                        gates(i + 1)
                    apply(i)
                for p in range(2):
                    o = open_group(("rec", li, p))
                    for t in (range(NT) if li == 0 else range(2, NT)):
                        pe.wait_ge(rec_ready.sem, rec_ready.after((li, t)))
                        last = pe.transpose(o[:, cols_of(t)], OREC[:, t, p * P:(p + 1) * P], ident)
                    last.then_inc(full, 1)

            def attention(li):
                au = att_units(li)
                for name in ("qa", "ka"):
                    for h in range(NH_A):
                        pe.wait_ge(*taken_after(("rot", name, li, h)))
                for t in range(NT):
                    pe.wait_ge(*taken_after(("va", li, t)))
                U = len(au)
                for st in range(U + 3):
                    if st < U:
                        t, h = au[st]
                        nk_ = 256 if t < 2 else 512
                        for c in range(2):
                            o = open_group(("s", li, st, c))
                            r = slice(64 * c, 64 * c + 64)
                            pe.matmul(o[:, 0:nk_], QA[r, h, cols_of(t)], KA[r, h, 0:nk_], start=True, stop=True).then_inc(full, 1)
                    if 0 <= st - 1 < U:
                        u = st - 1
                        t, h = au[u]
                        o = open_group(("aT", li, u))
                        pe.wait_ge(a_ready.sem, a_ready.after((li, u)))
                        for j in range(2 if t < 2 else 4):
                            last = pe.transpose(o[:, j * P:(j + 1) * P], E2[:, u % 2, 0, j * P:(j + 1) * P], ident)
                        last.then_inc(full, 1)
                    if 0 <= st - 2 < U:
                        u = st - 2
                        t, h = au[u]
                        o = open_group(("av", li, u))
                        pe.wait_ge(*taken_after(("aT", li, u)))
                        nj = 2 if t < 2 else 4
                        for j in range(nj):
                            last = pe.matmul(o[:, 0:P], AT[:, u % 2, j * P:(j + 1) * P], VA[:, j, h * P:(h + 1) * P],
                                             start=(j == 0), stop=(j == nj - 1))
                        last.then_inc(full, 1)
                    if 0 <= st - 3 < U:
                        u = st - 3
                        pe.wait_ge(*taken_after(("av", li, u)))
                        o = open_group(("oT", li, u))
                        pe.transpose(o[:, 0:P], ON[:, u % 2, :], ident).then_inc(full, 1)

            def w_out(li):
                live = range(NT) if li == 0 else range(2, NT)
                for u in range(len(att_units(li))):
                    pe.wait_ge(*taken_after(("oT", li, u)))
                for p in range(2):
                    pe.wait_ge(*taken_after(("rec", li, p)))
                for s in ((0, 1) if li == 0 else (1,)):
                    pe.wait_ge(*taken_after(("f3", li, s)))
                for c in range(2):
                    outs = [open_group(("w_out", li, c, t)) for t in live]
                    for h in range(2):
                        w = weights(("w_out", li, c, h)).rearrange("p (k n) -> p k n", k=4)
                        for t, o in zip(live, outs):
                            for k in range(4):
                                last = pe.matmul(o[:, :], MT[:, 4 * h + k, cols_of(t)], w[:, k, :],
                                                 start=(h == 0 and k == 0), stop=(h == 1 and k == 3))
                            if h == 1:
                                last.then_inc(full, 1)
                        release(last if h == 0 else None)

            def rows_out(name, parts, live, c_of, total):
                for c in range(2):
                    outs = [open_group((*name, c, t)) for t in live]
                    for r0, nrow in parts:
                        key = (*name, c, r0)
                        wh, wl = halves(weights(key), 4)
                        pe.wait_ge(part_lo.sem, part_lo.after(key))
                        b = 4 * (FS_KEYS.index(key) % 2)
                        for k in range(nrow):
                            f = r0 + k
                            for t, o in zip(live, outs):
                                last = product(o[:, :], (HH[:, b + k, c_of(t)], HL[:, b + k, c_of(t)]),
                                               (wh[:, k, :], wl[:, k, :]), f == 0, f == total - 1)
                                if f == total - 1:
                                    last.then_inc(full, 1)
                        release(last if r0 + nrow < total else None)

            def ffn(li):
                xcols = slice(0, 512) if li == 0 else slice(256, 512)
                live = range(NT) if li == 0 else range(2, NT)
                norm(("n2", li))
                wait_normed(("n2", li))
                for f2 in range(FT // 2):
                    for a in range(2):
                        w = weights(("w_up", li, f2, a))
                        for j in range(2):
                            t_out(("u", li, 2 * f2 + j, a), w, j, xcols)
                        release()
                        for lj in fill(("w_up", li), 2 * f2 + a):
                            ada(*lj)
                rows_out(("w_down", li), DOWN, live, cols_of, FT)

            pe.wait_ge(s_const, 32)
            pe.wait_ge(s_small, 16 * len(small_ins))
            for c in range((NCOL + P - 1) // P):
                n = min(P, NCOL - c * P)
                o = open_group(("cols", c))
                pe.transpose(o[:, 0:n], rows[0:n, c, :], ident[0:n, 0:n]).then_inc(full, 1)
            pe.wait_ge(c_ready, 1)
            for n in range(8):
                ada(0, n)
            for li in range(DEPTH):
                norm(("n1", li))
                w_in(li)
                fourier(li)
                hgrn(li)
                attention(li)
                w_out(li)
                ffn(li)

            norm(("cn", 0))
            wait_normed(("cn", 0))
            for e in range(ET // 2):
                for q in C_IN:
                    w = weights(("c_in", e, q))
                    for j in range(2):
                        t_out(("c", 2 * e + j, q), w, j, slice(256, 512))
                    release()
            rows_out(("c_out",), C_OUT, (2, 3), lambda t: slice(t * P, (t + 1) * P), ET)
            o = open_group("vec")
            pe.wait_ge(s_hot, 48)
            pe.matmul(o[0:NG * NH, 0:384], tabx, hot, start=True, stop=True).then_inc(full, 1)
            norm(("an", 0))
            pend = []

            def mean_of(key):
                pe.wait_ge(q_sq.sem, q_sq.after(key))
                o = open_group(("ms", key))
                pe.matmul(o[:, :], means, SQ[:, QKEYS.index(key) % 2, :], start=True, stop=True).then_inc(full, 1)

            wait_normed(("an", 0))
            for g in range(NG):
                for key in [(g, a, j) for a in range(2) for j in range(4)]:
                    w = weights(("a_in", *key))
                    t_out(("qk", key), w, 0, slice(256, 512), close_=False)
                    t_out(("qk", key), w, 1, slice(256, 512), 256, open_=False)
                    release()
                    pend.append(key)
                    if len(pend) > 1:
                        mean_of(pend.pop(0))
                for c in range(2):
                    outs = [open_group(("v2", g, c, t), closes_next=False) for t in range(2)]
                    for h in range(2):
                        wh, wl = halves(weights(("a_in", g, 2, 2 * c + h)), 4)
                        for t, o in enumerate(outs):
                            cs = slice(256 + t * P, 256 + (t + 1) * P)
                            for k in range(4):
                                last = product(o[:, :], (HH[:, 4 * h + k, cs], HL[:, 4 * h + k, cs]), (wh[:, k, :], wl[:, k, :]),
                                               h == 0 and k == 0, h == 1 and k == 3)
                            if h == 1:
                                last.then_inc(full, closed(("v2", g, c, t)))
                        release(last if h == 0 else None)
                        if pend:
                            mean_of(pend.pop(0))
            for j in range(4):
                w = weights(("a_in", "z", 0, j))
                t_out(("z2", j), w, 0, slice(256, 512), close_=False)
                t_out(("z2", j), w, 1, slice(256, 512), 256, open_=False)
                release()
            pe.wait_ge(q_done.sem, q_done.after(QKEYS[-1]))
            for g in range(NG):
                for c in range(2):
                    for t in range(2):
                        pe.wait_ge(*taken_after(("v2", g, c, t)))
            U = len(BU)
            for st in range(U + 2):
                if st < U:
                    h, t = BU[st]
                    r = slice(64 * (h % 2), 64 * (h % 2) + 64)
                    n = (t + 1) * P
                    for part_, gs in enumerate(((0, 1), (2,))):
                        o = open_group(("s2", st, part_))
                        for g in gs:
                            last = pe.matmul(o[:, g % 2 * 256:g % 2 * 256 + n], QK2[r, g, 0, h // 2, cols_of(t)],
                                             QK2[r, g, 1, h // 2, 0:n], start=True, stop=True)
                        last.then_inc(full, 1)
                if 0 <= st - 1 < U:
                    u = st - 1
                    h, t = BU[u]
                    pe.wait_ge(b_exp.sem, b_exp.after(BU[u]))
                    for part_, gs in enumerate(((0, 1), (2,))):
                        o = open_group(("eT", u, part_))
                        for g in gs:
                            for kt in range(t + 1):
                                c = (g % 2 * 2 + kt) * P
                                last = pe.transpose(o[:, c:c + P], LG[:, u % 2, g, kt * P:(kt + 1) * P], ident)
                        last.then_inc(full, 1)
                if 0 <= st - 2 < U:
                    u = st - 2
                    h, t = BU[u]
                    o = open_group(("o2", u))
                    for part_ in range(2):
                        pe.wait_ge(*taken_after(("eT", u, part_)))
                    blocks = [(g, kt) for g in range(NG) for kt in range(t + 1)]
                    for j, (g, kt) in enumerate(blocks):
                        c = (g * 2 + kt) * P
                        last = pe.matmul(o[:, 0:64], E3[:, u % 2, c:c + P], V2[:, g, kt, h * 64:(h + 1) * 64],
                                         start=(j == 0), stop=(j == len(blocks) - 1))
                    last.then_inc(full, 1)
            for u in range(U - 8, U):
                pe.wait_ge(*taken_after(("o2", u)))
            for k in range(KT):
                o = open_group(("yT", k))
                for t in range(2):
                    last = pe.matmul(o[:, t * P:(t + 1) * P], Y2[:, t, k * P:(k + 1) * P], flip, start=True, stop=True)
                last.then_inc(full, 1)
            for k in range(KT):
                pe.wait_ge(*taken_after(("yT", k)))
            for c in range(2):
                outs = [open_group(("a_out", c, t)) for t in range(2)]
                for h in range(2):
                    w = weights(("a_out", c, h)).rearrange("p (k n) -> p k n", k=4)
                    for t, o in enumerate(outs):
                        for k in range(4):
                            last = pe.matmul(o[:, :], YT2[:, 4 * h + k, t * P:(t + 1) * P], w[:, k, :],
                                             start=(h == 0 and k == 0), stop=(h == 1 and k == 3))
                        if h == 1:
                            last.then_inc(full, 1)
                    release(last if h == 0 else None)
            assert read[0] == len(plan)

        @block.sync
        def _(sp):
            sp.dma_start(wide[:, :], wide_c).then_inc(s_const, 16)
            sp.dma_start(arena[:, 0:2 * LEVELS * P], mask_c).then_inc(s_const, 16)
            for dst, src in small_ins:
                sp.dma_start(dst, src).then_inc(s_small, 16)
            sp.dma_start(RES[:, 0:2, :], A["ctx"].rearrange("a (t p) n -> p (a t) n", p=P)).then_inc(s_in, 16)
            sp.dma_start(RES[:, 2:4, :], A["x"].rearrange("a (t p) n -> p (a t) n", p=P)).then_inc(s_in, 16)
            for n, (key, split, src) in enumerate(plan):
                if n >= SLOTS:
                    sp.wait_ge(*read_at[n - SLOTS])
                _, k, m = src.shape
                sp.dma_start(slot(n)[:, 0:k * m].rearrange("p (k n) -> p k n", k=k), src).then_inc(slot_in[n % SLOTS], 16)
            for c in range(2):
                for t in range(2):
                    sp.wait_ge(*taken_after(("a_out", c, t)))
                    sp.dma_start(out[0, t * P:(t + 1) * P, c * 512:(c + 1) * 512],
                                 RES[:, 2 + t, c * 512:(c + 1) * 512]).then_inc(s_out, 16)
            sp.wait_ge(s_out, 64)

        @block.gpsimd
        def _(pool):
            line = Line()

            def root(dst, mean):
                pool.tensor_scalar(dst, mean, EPS, None, ALU.add).then_inc(pool_step, line.one())
                pool.wait_ge(pool_step, line.n)
                return pool.tensor_tensor(dst, dst, minus_half[:, 0:mean.shape[1]], ALU.pow)

            def pow_norm(N):
                for t in norm_tiles(N):
                    pool.wait_ge(squared.sem, squared.after((N, t)))
                    root(rstd[:, t:t + 1], ssq[:, t:t + 1]).then_inc(row_scale.sem, 1)

            def hgrn_roots(li):
                for t in (range(NT) if li == 0 else range(2, NT)):
                    pool.wait_ge(rec_sum.sem, rec_sum.after((li, t)))
                    root(hrstd[:, t, :], hssq[:, t, :]).then_inc(og_exp.sem, 1)

            def att_roots(li):
                for u in range(len(att_units(li))):
                    pool.wait_ge(o_sq.sem, o_sq.after((li, u)))
                    b = slice(u % 2, u % 2 + 1)
                    root(orstd[:, b], ossq[:, b]).then_inc(o_rs.sem, 1)

            def gate_bias(li, g):
                row = A["b_ada"][li, (2 + 3 * g) * DM:(3 + 3 * g) * DM]
                for s in range(2 if li == 0 else 1):
                    pool.dma_start(GB[:, s, :], row.partition_broadcast(P)).then_inc(s_gb, 16)

            pool.memset(minus_half, -0.5).then_inc(s_half, 1)
            pool.wait_ge(s_half, 1)
            gate_bias(0, 0)
            pool.wait_ge(c_ready, 1)
            pool.wait_ge(full, full_after(("cols", 4)))
            pool.dma_start(wf, A["w_fnet"][0, :, :].rearrange("(f p) n -> p f n", p=P)).then_inc(s_wf, 16)
            for li in range(DEPTH):
                pow_norm(("n1", li))
                hgrn_roots(li)
                att_roots(li)
                pool.wait_ge(res_new.sem, res_new.after(("w_out", li)))
                gate_bias(li, 1)
                pow_norm(("n2", li))
                pool.wait_ge(res_new.sem, res_new.after(("w_down", li)))
                if li == 0:
                    gate_bias(1, 0)
                    pool.dma_start(lb_rows, A["lb_param"].rearrange("l d n -> l (d n)").partition_broadcast(P)).then_inc(s_lb, 16)
                    pool.dma_start(wf, A["w_fnet"][1, :, :].rearrange("(f p) n -> p f n", p=P)).then_inc(s_wf, 16)
            pool.dma_start(GB[:, 0, :], A["final_norm_w"].partition_broadcast(P)).then_inc(s_fw, 16)
            pow_norm(("fn", 0))
            pool.dma_start(hot, hot_c).then_inc(s_hot, 16)
            pool.dma_start(tabx[0:32, :], A["rel_bias_2"]).then_inc(s_hot, 16)
            pool.dma_start(tabx[32:32 + NG, :], tab_c).then_inc(s_hot, 16)
            pow_norm(("cn", 0))
            pool.wait_ge(*taken_after("vec"))
            pool.dma_start(vec_d, vec).then_inc(s_vec, 16)
            pool.wait_ge(s_vec, 16)
            pow_norm(("an", 0))
            for h in range(NH):
                if h >= 3:
                    pool.wait_ge(b_max.sem, b_max.after((h - 3, 1)))
                src = bass.AP(tensor=vec_d.tensor, offset=h * 384, ap=[[1, P], [NH * 384, NG], [1, 256]])
                pool.dma_start(BIAS[:, h % 3, :, :], src).then_inc(s_bias[h % 3], 16)
            for b in range(3):
                pool.wait_ge(s_bias[b], 16 * len(range(b, NH, 3)))

        @block.scalar
        def _(act):
            line = Line()
            act.wait_ge(s_eps, 1)

            def evict(key, dst, n):
                act.wait_ge(full, full_after(key))
                act.activation(dst, bank(key, n), ACT.Copy).then_inc(taken_of(key), 1)

            def split(key):
                n, m = item[key], split_no[key]
                act.wait_ge(slot_in[n % SLOTS], 16 * (n // SLOTS + 1))
                if m >= HIGH:
                    act.wait_ge(*read_at[item[split_keys[m - HIGH]]])
                used = plan[n][2].shape[1] * plan[n][2].shape[2]
                act.activation(hi_slot(key)[:, 0:used], slot(n)[:, 0:used], ACT.Copy).then_inc(hi_in.sem, 1)

            def splits(stage):
                keys = stage_keys(stage)
                split(keys[0])
                for key in keys[1:]:
                    yield split(key)
                while True:
                    yield

            def norm(N):
                for t in norm_tiles(N):
                    if N == ("n1", 0):
                        if t == 0:
                            act.wait_ge(s_in, 32)
                    elif N == ("an", 0):
                        act.wait_ge(*taken_after(("c_out", 1, 3)))
                        act.wait_ge(*taken_after(("c_out", 0, 3)))
                    elif t == norm_tiles(N)[0]:
                        act.wait_ge(res_new.sem, res_new.after({("n2", 0): ("w_out", 0), ("n1", 1): ("w_down", 0), ("n2", 1): ("w_out", 1),
                                           ("fn", 0): ("w_down", 1), ("cn", 0): ("final", 0)}[N]))
                    act.activation(XS[:, t, :], RES[:, t, :], ACT.Square, scale=1.0 / 32.0,
                                   accum_out=ssq[:, t:t + 1]).then_inc(squared.sem, 1)
                if N == ("fn", 0):
                    return
                for k in range(KT):
                    act.wait_ge(full, full_after((N, k)))
                    if k >= 2:
                        act.wait_ge(ht_done.sem, ht_done.after((N, k - 2)))
                    x, v = bank((N, k)), n_t[:, k % 2, :]
                    if N[0] in ("n1", "n2"):
                        m = 0 if N[0] == "n1" else 2
                        if 0 in norm_tiles(N):
                            act.activation(v[:, 0:256], x[:, 0:256], ACT.Identity, scale=nscale[:, k, 1:2],
                                           bias=modt[:, N[1], m, k, 1:2]).then_inc(scalar_step, line.one())
                        act.activation(v[:, 256:512], x[:, 256:512], ACT.Identity, scale=nscale[:, k, 0:1],
                                       bias=modt[:, N[1], m, k, 0:1]).then_inc(taken_of((N, k)), 1)
                    else:
                        act.activation(v[:, 256:512], x[:, 256:512], ACT.Copy, scale=pcol(N, k)).then_inc(taken_of((N, k)), 1)

            def ada(li, n):
                if n // 4 in GATES:
                    key = ("ada", li, n)
                    act.wait_ge(full, full_after(key))
                    act.activation(grow, bank(key)[0:2, 0:256], ACT.Copy).then_inc(taken_of(key), 1)

            def w_in(li):
                lo = 0 if li == 0 else 256
                ahead = splits(("w_in", li))
                if li:
                    act.wait_ge(lb_abs, 1)
                    act.activation(lb_rows[:, 1, :], lb_rows[:, 0, :], ACT.Abs).then_inc(scalar_step, line.one())
                    act.wait_ge(scalar_step, line.n)
                    act.activation(lb_rows[:, 1, :], lb_rows[:, 1, :], ACT.Exp, scale=-1.0).then_inc(scalar_step, line.one())
                    act.wait_ge(scalar_step, line.n)
                    act.activation(lb_rows[:, 1, :], lb_rows[:, 1, :], ACT.Ln, bias=1.0).then_inc(lb_exp, 1)
                next(ahead)
                for n, (name, h, _) in enumerate(W_IN):
                    if name in ("qa", "ka"):
                        X, l0 = (QA, lo) if name == "qa" else (KA, 0)
                        for m in range(2):
                            evict((name, li, 2 * h + m), X[:, 2 * h + m, l0:512], 512 - l0)
                    elif name == "va" and h:
                        for t in range(NT):
                            evict(("va", li, t), VA[:, t, :], 512)
                    elif name == "ihgh" and h:
                        for t in range(NT):
                            key = ("ihgh", li, t)
                            act.wait_ge(full, full_after(key))
                            if li == 0 or t >= 2:
                                act.activation(GH[:, t, :], bank(key)[:, 256:512], ACT.Silu).then_inc(scalar_step, line.one())
                            act.activation(IH[:, t, :], bank(key)[:, 0:256], ACT.Copy).then_inc(taken_of(key), 1)
                    elif name == "qh":
                        for p in range(2):
                            evict(("qh", li, p), QH[:, p, lo:512], 512 - lo)
                    elif name == "uf":
                        for t in (range(NT) if li == 0 else range(2, NT)):
                            evict(("uf", li, t), UF[:, t, :], 256)
                    for lj in fill(("w_in", li), n):
                        ada(*lj)
                    next(ahead)
                for t in range(NT):
                    act.wait_ge(full, full_after(("zz", li, t)))
                    act.activation(SP[:, t, :], bank(("zz", li, t)), ACT.Abs).then_inc(scalar_step, line.one())
                act.wait_ge(scalar_step, line.n)
                for t in range(NT):
                    act.activation(SP[:, t, :], SP[:, t, :], ACT.Exp, scale=-1.0).then_inc(scalar_step, line.one())
                act.wait_ge(scalar_step, line.n)
                for t in range(NT):
                    act.activation(SP[:, t, :], SP[:, t, :], ACT.Ln, bias=1.0).then_inc(z_soft.sem, 1)
                if li:
                    for t in range(NT):
                        act.wait_ge(b_gap.sem, b_gap.after((li, t)))
                        act.activation(BG[:, t, :], BG[:, t, :], ACT.Abs).then_inc(scalar_step, line.one())
                    act.wait_ge(scalar_step, line.n)
                    for t in range(NT):
                        act.activation(BG[:, t, :], BG[:, t, :], ACT.Exp, scale=-1.0).then_inc(scalar_step, line.one())
                    act.wait_ge(scalar_step, line.n)
                    for t in range(NT):
                        act.activation(BG[:, t, :], BG[:, t, :], ACT.Ln, bias=1.0).then_inc(b_soft.sem, 1)
                for t in range(NT):
                    act.wait_ge(*taken_after(("zz", li, t)))
                    act.activation(KTOK[:, t, :], KTOK[:, t, :], ACT.Exp).then_inc(k_ready.sem, 1)

            def fourier(li):
                act.wait_ge(g_ready.sem, g_ready.after((li, NT - 1)))
                for s in ((0, 1) if li == 0 else (1,)):
                    for f in range(2):
                        evict(("f1", li, s, f), FS[:, f, :], 512)
                    evict(("f2", li, s), YT4, 512)
                    key = ("f3", li, s)
                    act.wait_ge(full, full_after(key))
                    act.activation(MT[:, 6:8, s * 256:(s + 1) * 256],
                                   bank(key).rearrange("p (c n) -> p c n", c=2), ACT.Copy).then_inc(taken_of(key), 1)

            def hgrn(li):

                def gates(i):
                    b = i % 2
                    if is_full(li, i):
                        for p in range(2):
                            for hf in range(2):
                                key = ("E", li, i, p, hf)
                                act.wait_ge(full, full_after(key))
                                if i >= 2 and is_full(li, i - 2):
                                    act.wait_ge(full, full_after(("O", li, i - 2, 1)))
                                act.activation(XE[b][:, p, 4 * hf:4 * hf + 4, :],
                                                         bank(key).rearrange("p (l n) -> p l n", l=4), ACT.Exp).then_inc(taken_of(key), 1)
                    if i < 6:
                        key = ("suf", li, i)
                        act.wait_ge(full, full_after(key))
                        if i >= 2:
                            act.wait_ge(*taken_after(("SU", li, i - 2)))
                        act.activation(SE[:, b, 0:258], bank(key, 258), ACT.Exp).then_inc(taken_of(key), 1)

                gates(0)
                for i in range(8):
                    if i + 1 < 8:
                        gates(i + 1)
                for p in range(2):
                    key = ("rec", li, p)
                    lo = 0 if li == 0 else 256
                    act.wait_ge(full, full_after(("rec", li, 1)))
                    act.activation(MT[:, 4 + p, lo:512], bank(key)[:, lo:512], ACT.Copy).then_inc(taken_of(key), 1)

            def attention(li):
                au = att_units(li)
                U = len(au)
                lam_init = 0.8 - 0.6 * math.exp(-0.3 * li)
                for st in range(U + 3):
                    if st < U:
                        u = st
                        t, h = au[u]
                        n = 256 if t < 2 else 512
                        act.wait_ge(a_max.sem, a_max.after((li, u)))
                        if u >= 2:
                            act.wait_ge(full, full_after(("aT", li, u - 2)))
                        if u >= 2:
                            act.wait_ge(a_ready.sem, a_ready.after((li, u - 2)))
                        for c in range(2):
                            ins = act.activation(E2[:, u % 2, c, 0:n], bank(("s", li, u, c), n), ACT.Exp, scale=0.125,
                                                 bias=amax[:, u % 2, c:c + 1], accum_out=asum[:, u % 2, c:c + 1])
                            ins.then_inc(taken_of(("s", li, u, c)), 1)
                    if 0 <= st - 1 < U:
                        u = st - 1
                        t, h = au[u]
                        n = 256 if t < 2 else 512
                        if u >= 2:
                            act.wait_ge(full, full_after(("av", li, u - 2)))
                        evict(("aT", li, u), AT[:, u % 2, 0:n], n)
                    if 0 <= st - 2 < U:
                        u = st - 2
                        act.wait_ge(full, full_after(("av", li, u)))
                        if u >= 2:
                            act.wait_ge(full, full_after(("oT", li, u - 2)))
                        b = slice(u % 2, u % 2 + 1)
                        if u >= 2:
                            act.wait_ge(o_rs.sem, o_rs.after((li, u - 2)))
                        act.activation(ON[:, u % 2, :], bank(("av", li, u), P), ACT.Square,
                                       scale=1.0 / math.sqrt(128.0), accum_out=ossq[:, b]).then_inc(o_sq.sem, 1)
                    if 0 <= st - 3 < U:
                        u = st - 3
                        t, h = au[u]
                        act.wait_ge(full, full_after(("oT", li, u)))
                        act.activation(MT[:, h, cols_of(t)], bank(("oT", li, u), P), ACT.Copy,
                                                           scale=pcol(("subln", li))).then_inc(taken_of(("oT", li, u)), 1)

            def split_rows(X, key, n, r0, nrow, lo, last_read):
                b = 4 * (n % 2)
                if n == 0:
                    act.wait_ge(full, full_after(last_read))
                elif n >= 2:
                    act.wait_ge(*read_at[item[FS_KEYS[FS_KEYS.index(key) - 2]]])
                act.activation(HH[:, b:b + nrow, lo:lo + X.shape[2]], X[:, r0:r0 + nrow, :], ACT.Copy).then_inc(part_hi.sem, 1)

            def ffn(li):
                norm(("n2", li))
                lo = 0 if li == 0 else 256
                w = 512 - lo
                ahead = splits(("w_up", li))
                next(ahead)
                for f2 in range(FT // 2):
                    for a in range(2):
                        for j in range(2):
                            f = 2 * f2 + j
                            if f2:
                                act.wait_ge(f_out.sem, f_out.after((li, f - 2)))
                            key = ("u", li, f, a)
                            act.wait_ge(full, full_after(key))
                            act.activation(FC[:, j, a, 0:w], bank(key, w), ACT.Identity, scale=pcol(("cw", li, 1), a * FT + f),
                                           bias=pcol(("cb", li), a * FT + f)).then_inc(f_mid.sem, 1)
                        for lj in fill(("w_up", li), 2 * f2 + a):
                            ada(*lj)
                        next(ahead)
                    for j in range(2):
                        f = 2 * f2 + j
                        act.wait_ge(*taken_after(("u", li, f, 0)))
                        act.activation(FC[:, j, 2, 0:w], FC[:, j, 0, 0:w], ACT.Silu).then_inc(f_exp.sem, 1)
                ahead = splits(("w_down", li))
                keys = [(("w_down", li, c, r0), r0, nrow) for c in range(2) for r0, nrow in DOWN]
                for n, (key, r0, nrow) in enumerate(keys):
                    act.wait_ge(f_out.sem, f_out.after((li, r0 + nrow - 1)))
                    split_rows(HF[:, :, lo:512], key, n, r0, nrow, lo, ("u", li, FT - 1, 1))
                    next(ahead)

            for c in range((NCOL + P - 1) // P):
                n = min(P, NCOL - c * P)
                evict(("cols", c), cols[:, c * P:c * P + n], n)
            act.wait_ge(*taken_after(("cols", 0)))
            act.activation(csil.rearrange("p s k -> p (s k)"), cols[:, 0:16], ACT.Silu).then_inc(c_ready, 1)
            act.wait_ge(lam_sum, 2 * DEPTH)
            act.activation(lam2, lam2, ACT.Exp).then_inc(lam_exp, 1)
            for li in range(DEPTH):
                norm(("n1", li))
                w_in(li)
                fourier(li)
                hgrn(li)
                attention(li)
                ffn(li)
            norm(("fn", 0))
            norm(("cn", 0))
            ahead = splits(("c_in",))
            next(ahead)
            for e2 in range(ET // 2):
                for q in C_IN:
                    for j in range(2):
                        e = 2 * e2 + j
                        key = ("c", e, q)
                        if q in (1, 3):
                            act.wait_ge(full, full_after(key))
                        if q == 1:
                            if e >= 2:
                                act.wait_ge(c_out.sem, c_out.after(e - 2))
                            act.activation(CC[:, j, 0, :], bank(key, 256), ACT.Copy).then_inc(taken_of(key), 1)
                        if q == 3:
                            act.activation(CC[:, j, 1, :], bank(key, 256), ACT.Silu).then_inc(taken_of(key), 1)
                    next(ahead)
            ahead = splits(("c_out",))
            for n, (c, (r0, nrow)) in enumerate([(c, part) for c in range(2) for part in C_OUT]):
                act.wait_ge(c_out.sem, c_out.after(r0 + nrow - 1))
                split_rows(YC, ("c_out", c, r0), n, r0, nrow, 256, ("c", ET - 1, 0))
                next(ahead)
            norm(("an", 0))
            ahead = splits(("a_in",))
            next(ahead)
            pend = []

            def scales_of(four):
                for key in four:
                    n = QKEYS.index(key)
                    act.wait_ge(full, full_after(("ms", key)))
                    if n >= 4:
                        act.wait_ge(q_done.sem, q_done.after(QKEYS[n - 4]))
                    act.activation(RQ[:, n % 4, :], bank(("ms", key)), ACT.Ln, bias=EPS_COL).then_inc(taken_of(("ms", key)), 1)
                for key in four:
                    n = QKEYS.index(key)
                    act.wait_ge(*taken_after(("ms", key)))
                    act.activation(RQ[:, n % 4, :], RQ[:, n % 4, :], ACT.Exp, scale=-0.5).then_inc(q_rs.sem, 1)

            for g, a, j in A_IN:
                if g == "z":
                    key = ("z2", j)
                    act.wait_ge(full, full_after(key))
                    act.wait_ge(s_vec, 16)
                    act.activation(ZS[:, 2 * j:2 * j + 2, :], bank(key).rearrange("p (m n) -> p m n", m=2),
                                   ACT.Silu).then_inc(taken_of(key), 1)
                elif a < 2:
                    key = (g, a, j)
                    n = QKEYS.index(key)
                    act.wait_ge(full, full_after(("qk", key)))
                    if n >= 2:
                        act.wait_ge(full, full_after(("ms", QKEYS[n - 2])))
                    act.activation(SQ[:, n % 2, :], bank(("qk", key)), ACT.Square, scale=0.125).then_inc(q_sq.sem, 1)
                    pend.append(key)
                    if len(pend) == 5:
                        scales_of(pend[:4])
                        pend = pend[4:]
                elif j == 0 and pend:
                    scales_of(pend)
                    pend = []
                elif j % 2:
                    for t in range(2):
                        evict(("v2", g, j // 2, t), V2[:, g, t, j // 2 * 512:(j // 2 + 1) * 512], 512)
                next(ahead)
            for st in range(len(BU) + 1):
                if st < len(BU):
                    u = st
                    h, t = BU[u]
                    n = (t + 1) * P
                    act.wait_ge(b_max.sem, b_max.after(BU[u]))
                    act.activation(LG[:, u % 2, :, 0:n], LG[:, u % 2, :, 0:n], ACT.Exp,
                                                     bias=bmax[:, u % 2:u % 2 + 1], accum_out=bsum[:, u % 2:u % 2 + 1]).then_inc(b_exp.sem, 1)
                if 0 <= st - 1:
                    u = st - 1
                    h, t = BU[u]
                    n = (t + 1) * P
                    key = ("eT", u, 0)
                    act.wait_ge(full, full_after(key))
                    if u >= 2:
                        act.wait_ge(full, full_after(("o2", u - 2)))
                    act.activation(E3[:, u % 2, 0:512].rearrange("p (g n) -> p g n", g=2)[:, :, 0:n],
                                             bank(key).rearrange("p (g n) -> p g n", g=2)[:, :, 0:n], ACT.Copy).then_inc(taken_of(key), 1)

        @block.vector
        def _(dve):
            line = Line()

            def split(key):
                dve.wait_ge(hi_in.sem, hi_in.after(key))
                n = item[key]
                used = plan[n][2].shape[1] * plan[n][2].shape[2]
                dve.tensor_tensor(slot(n, ring_lo)[:, 0:used], slot(n)[:, 0:used], hi_slot(key)[:, 0:used], ALU.subtract).then_inc(lo_in.sem, 1)

            def splits(stage):
                keys = stage_keys(stage)
                split(keys[0])
                for key in keys[1:]:
                    yield split(key)
                while True:
                    yield

            def norm(N):
                m = {"n1": 0, "n2": 2}.get(N[0])
                if m is not None:
                    dve.tensor_scalar(nscale, modt[:, N[1], m + 1, :, :], 1.0, None, ALU.add).then_inc(vector_step, line.one())
                    dve.wait_ge(vector_step, line.n)
                    w8 = cols[:, col[N]:col[N] + 8].unsqueeze(2).to_broadcast([P, KT, 2])
                    dve.tensor_tensor(nscale, nscale, w8, ALU.mult).then_inc(vector_step, line.one())
                    dve.wait_ge(vector_step, line.n)
                for t in norm_tiles(N):
                    dve.wait_ge(row_scale.sem, row_scale.after((N, t)))
                    if N == ("fn", 0):
                        if t == 2:
                            dve.wait_ge(s_fw, 16)
                        done = vector_step if t == 2 else res_new.sem
                        dve.scalar_tensor_tensor(RES[:, t, :], RES[:, t, :], rstd[:, t:t + 1], GB[:, 0, :],
                                                 ALU.mult, ALU.mult).then_inc(done, line.one() if t == 2 else 1)
                    else:
                        dve.tensor_scalar(XS[:, t, :], RES[:, t, :], rstd[:, t:t + 1], None, ALU.mult).then_inc(scaled.sem, 1)
                if N == ("fn", 0):
                    return
                lo = 0 if 0 in norm_tiles(N) else 256
                for k in range(KT):
                    v = n_t[:, k % 2, lo:512]
                    dve.wait_ge(*taken_after((N, k)))
                    dve.tensor_copy(HH[:, k, lo:512], v).then_inc(vector_step, line.one())
                    dve.wait_ge(vector_step, line.n)
                    dve.tensor_tensor(HL[:, k, lo:512], v, HH[:, k, lo:512], ALU.subtract).then_inc(ht_done.sem, 1)

            seen_gb = [0]

            def ada(li, n):
                key, sec, q = ("ada", li, n), n // 4, n % 4
                if sec in GATES:
                    if q == 0:
                        seen_gb[0] += 32 if li == 0 else 16
                        dve.wait_ge(s_gb, seen_gb[0])
                    for s in range(2 if li == 0 else 1):
                        k2 = ("gb", li, n, s)
                        dve.wait_ge(full, full_after(k2))
                        d = GB[:, s, q * 256:(q + 1) * 256]
                        dve.tensor_tensor(d, bank(k2, 256), d, ALU.add).then_inc(taken_of(k2), 1)
                else:
                    m = {0: 0, 1: 1, 3: 2, 4: 3}[sec]
                    dve.wait_ge(full, full_after(key))
                    c0 = col["b_ada", li] + 2 * n
                    bb = cols[:, c0:c0 + 2].unsqueeze(2).to_broadcast([P, 2, 2])
                    dve.tensor_tensor(modt[:, li, m, 2 * q:2 * q + 2, :], bank(key, 4).rearrange("p (k s) -> p k s", s=2), bb,
                                      ALU.add).then_inc(taken_of(key), 1)
                    dve.wait_ge(*taken_after(key))

            def w_in(li):
                ahead = splits(("w_in", li))
                if li:
                    dve.wait_ge(s_lb, 16)
                    dve.tensor_tensor(lb_rows[:, 0, :], lb_rows[:, 1, :], lb_rows[:, 0, :], ALU.subtract).then_inc(lb_abs, 1)
                    dve.wait_ge(lb_exp, 1)
                    dve.scalar_tensor_tensor(lb_rows[:, 1, :], lb_rows[:, 0, :], 0.0, lb_rows[:, 1, :], ALU.min,
                                             ALU.subtract).then_inc(vector_step, line.one())
                    dve.wait_ge(vector_step, line.n)
                    dve.tensor_tensor(lb_rows[:, 0, :], lb_rows[:, 1, :], lb_rows[:, 0, :], ALU.subtract).then_inc(vector_step, line.one())
                    dve.wait_ge(vector_step, line.n)
                next(ahead)
                for n, (name, h, _) in enumerate(W_IN):
                    if name == "va" and h == 0:
                        for name2, X in (("qa", QA), ("ka", KA)):
                            for hd in range(NH_A):
                                key = ("rot", name2, li, hd)
                                dve.wait_ge(full, full_after(key))
                                b = hd % 2
                                dve.tensor_tensor(rope_t[:, b, :], bank(key, 256), sinT, ALU.mult).then_inc(vector_step, line.one())
                                dve.tensor_tensor(X[:, hd, 256:512], X[:, hd, 256:512], cosT, ALU.mult).then_inc(vector_step, line.one())
                                dve.wait_ge(vector_step, line.n)
                                dve.tensor_tensor(X[:, hd, 256:512], X[:, hd, 256:512], rope_t[:, b, :], ALU.add).then_inc(taken_of(key), 1)
                    for lj in fill(("w_in", li), n):
                        ada(*lj)
                    next(ahead)
                dve.wait_ge(full, full_after(("zz", li, NT - 1)))
                for t in range(NT):
                    key = ("zz", li, t)
                    z = bank(key)
                    dve.wait_ge(z_soft.sem, z_soft.after((li, t)))
                    done = vector_step if li else g_ready.sem
                    dve.scalar_tensor_tensor(GL[:, t, :], z, 0.0, SP[:, t, :], ALU.min,
                                             ALU.subtract).then_inc(done, line.one() if li else 1)
                    if li:
                        dve.wait_ge(vector_step, line.n)
                        dve.tensor_tensor(GL[:, t, :], GL[:, t, :], lb_rows[:, 0, :], ALU.add).then_inc(vector_step, line.one())
                        dve.wait_ge(vector_step, line.n)
                        dve.tensor_tensor(BG[:, t, :], GL[:, t, :], lb_rows[:, 1, :], ALU.subtract).then_inc(b_gap.sem, 1)
                    else:
                        dve.wait_ge(g_ready.sem, g_ready.after((li, t)))
                    dve.tensor_tensor(KTOK[:, t, :], GL[:, t, :], z, ALU.subtract).then_inc(taken_of(key), 1)
                    if li:
                        dve.tensor_tensor(GL[:, t, :], GL[:, t, :], lb_rows[:, 1, :], ALU.max).then_inc(vector_step, line.one())
                if li:
                    dve.wait_ge(vector_step, line.n)
                    for t in range(NT):
                        dve.wait_ge(b_soft.sem, b_soft.after((li, t)))
                        dve.tensor_tensor(GL[:, t, :], GL[:, t, :], BG[:, t, :], ALU.add).then_inc(g_ready.sem, 1)

            def hgrn(li):
                un = units(li)

                def gates(i):
                    d, t = un[i]
                    b = i % 2
                    if is_full(li, i):
                        key = ("kT", li, i)
                        dve.wait_ge(full, full_after(key))
                        dve.tensor_copy(KTT[:, b, :, :], bank(key, 256).rearrange("p (q n) -> p q n", q=2)).then_inc(taken_of(key), 1)
                        dve.wait_ge(*taken_after(key))
                        for p in range(2):
                            for hf in range(2):
                                dve.wait_ge(*taken_after(("E", li, i, p, hf)))
                        if i == (0 if li == 0 else 4):
                            for p in range(2):
                                dve.wait_ge(*taken_after(("qh", li, p)))
                        q = QH[:, :, cols_of(t)]
                        for level in range(1, LEVELS):
                            B = level_block(level)
                            for hf in range(2):
                                src = q if hf == 1 - d else KTT[:, b, :, :]
                                for p in range(2):
                                    x = XE[b][:, p, level - 1, :].rearrange("p (m h n) -> p m h n", h=2, n=B)[:, :, hf, :]
                                    y = src[:, p, :].rearrange("p (m h n) -> p m h n", h=2, n=B)[:, :, hf, :]
                                    dve.tensor_tensor(x, x, y, ALU.mult).then_inc(vector_step, line.one())
                        dve.tensor_tensor(XE[b][:, :, 7, :], XE[b][:, :, 7, :], q, ALU.mult).then_inc(z_ready.sem, 1)
                    if i < 6:
                        dve.wait_ge(*taken_after(("suf", li, i)))
                        if i >= 2:
                            dve.wait_ge(full, full_after(("SU", li, i - 2)))
                        dve.tensor_tensor(KD[:, b, :], KTOK[:, t, d * 256:(d + 1) * 256], SE[:, b, 0:256], ALU.mult).then_inc(kd_ready.sem, 1)

                def apply(i):
                    d, t = un[i]
                    b = i % 2
                    if is_full(li, i):
                        for lp in range(4):
                            dve.wait_ge(full, full_after(("S", li, i, lp, 1)))
                            for lv in range(2):
                                m = MASK[:, d, 2 * lp + lv, :].unsqueeze(1).to_broadcast([P, 2, P])
                                for par in range(2):
                                    key = ("S", li, i, lp, par)
                                    ins = dve.copy_predicated(ACC[:, d, par, :, :], m,
                                                              bank(key)[:, lv * 256:(lv + 1) * 256].rearrange("p (h n) -> p h n", h=2))
                                    if lv:
                                        ins.then_inc(taken_of(key), 1)
                                    else:
                                        ins.then_inc(vector_step, line.one())
                                dve.wait_ge(vector_step, line.n)
                            for par in range(2):
                                dve.wait_ge(*taken_after(("S", li, i, lp, par)))
                        for par in range(2):
                            key = ("O", li, i, par)
                            dve.wait_ge(full, full_after(key))
                            o = OREC[:, t, :].rearrange("p (q a n) -> p q a n", q=2, a=2)[:, :, par, :]
                            src = bank(key, P).rearrange("p (q n) -> p q n", q=2)
                            if (d, t) in ((0, 0), (1, 1), (0, 2), (1, 3)):
                                dve.tensor_copy(o, src).then_inc(taken_of(key), 1)
                            else:
                                dve.tensor_tensor(o, src, o, ALU.add).then_inc(taken_of(key), 1)
                    if i < 6:
                        key = ("SU", li, i)
                        dve.wait_ge(full, full_after(key))
                        for p in range(2):
                            for hh in range(2):
                                r = slice(64 * hh, 64 * hh + 64)
                                dst = ST[r, d, p, :]
                                new = bank(key)[r, p * P + hh * 64:p * P + hh * 64 + 64]
                                if i < 2:
                                    ins = dve.tensor_copy(dst, new)
                                else:
                                    ins = dve.scalar_tensor_tensor(dst, dst, SE[r, b, 256 + p:257 + p], new, ALU.mult, ALU.add)
                                if p == 1 and hh == 1:
                                    ins.then_inc(taken_of(key), 1)
                                else:
                                    ins.then_inc(vector_step, line.one())
                        dve.wait_ge(*taken_after(key))

                dve.wait_ge(s_mask, 1)
                for s in ((0, 1) if li == 0 else (1,)):
                    dve.wait_ge(full, full_after(("f3", li, s)))
                dve.memset(scr[:, 2560:3584], 0.0).then_inc(vector_step, line.one())
                dve.wait_ge(vector_step, line.n)
                gates(0)
                for i in range(8):
                    if i + 1 < 8:
                        gates(i + 1)
                    apply(i)
                live = range(NT) if li == 0 else range(2, NT)
                for par in range(2):
                    dve.wait_ge(*taken_after(("O", li, 7, par)))
                for t in live:
                    o = OREC[:, t, :]
                    o4 = o.rearrange("p (h n) -> p h n", h=4)
                    tf = scr[:, 0:256]
                    dve.scalar_tensor_tensor(tf, o, 1.0 / 64.0, o, ALU.mult, ALU.mult).then_inc(vector_step, line.one())
                    dve.wait_ge(vector_step, line.n)
                    dve.tensor_reduce(hssq[:, t, :], tf.rearrange("p (h n) -> p h n", h=4), AX.X, ALU.add).then_inc(rec_sum.sem, 1)
                    dve.wait_ge(rec_sum.sem, rec_sum.after((li, t)))
                for t in live:
                    o = OREC[:, t, :]
                    o4 = o.rearrange("p (h n) -> p h n", h=4)
                    dve.wait_ge(og_exp.sem, og_exp.after((li, t)))
                    dve.tensor_tensor(o4, o4, hrstd[:, t, :].unsqueeze(2).to_broadcast([P, 4, 64]), ALU.mult).then_inc(vector_step, line.one())
                    dve.wait_ge(vector_step, line.n)
                    dve.tensor_tensor(o4, o4, hw[:, li, :].unsqueeze(1).to_broadcast([P, 4, 64]), ALU.mult).then_inc(vector_step, line.one())
                    dve.wait_ge(vector_step, line.n)
                    dve.tensor_tensor(o, o, GH[:, t, :], ALU.mult).then_inc(rec_ready.sem, 1)

            def attention(li):
                au = att_units(li)
                U = len(au)
                lam_init = 0.8 - 0.6 * math.exp(-0.3 * li)
                for st in range(U + 3):
                    if st < U:
                        u = st
                        t, h = au[u]
                        n = 256 if t < 2 else 512
                        b = u % 2
                        for c in range(2):
                            dve.wait_ge(full, full_after(("s", li, u, c)))
                            dve.tensor_reduce(arec[:, b, c:c + 1], bank(("s", li, u, c), n), AX.X, ALU.max).then_inc(vector_step, line.one())
                        dve.wait_ge(vector_step, line.n)
                        dve.tensor_scalar(amax[:, b, :], arec[:, b, :], -0.125, None, ALU.mult).then_inc(a_max.sem, 1)
                        dve.wait_ge(a_max.sem, a_max.after((li, u)))
                        for c in range(2):
                            dve.wait_ge(*taken_after(("s", li, u, c)))
                        dve.reciprocal(arec[:, b, :], asum[:, b, :]).then_inc(vector_step, line.one())
                        dve.wait_ge(vector_step, line.n)
                        dve.tensor_tensor(arec[:, b, 1:2], arec[:, b, 1:2], neglam[:, li:li + 1], ALU.mult).then_inc(vector_step, line.one())
                        dve.tensor_scalar(E2[:, b, 0, 0:n], E2[:, b, 0, 0:n], arec[:, b, 0:1], None, ALU.mult).then_inc(vector_step, line.one())
                        dve.wait_ge(vector_step, line.n)
                        dve.scalar_tensor_tensor(E2[:, b, 0, 0:n], E2[:, b, 1, 0:n], arec[:, b, 1:2],
                                                                       E2[:, b, 0, 0:n], ALU.mult, ALU.add).then_inc(a_ready.sem, 1)
                    if 0 <= st - 2 < U:
                        u = st - 2
                        b = u % 2
                        dve.wait_ge(o_rs.sem, o_rs.after((li, u)))
                        dve.tensor_scalar(ON[:, b, :], bank(("av", li, u), P), orstd[:, b:b + 1],
                                                              1.0 - lam_init, ALU.mult, ALU.mult).then_inc(taken_of(("av", li, u)), 1)

            def add_out(name, live, c, gated, signal=None):
                for i, t in enumerate(live):
                    key = (*name, c, t)
                    dve.wait_ge(full, full_after(key))
                    r = RES[:, t, c * 512:(c + 1) * 512]
                    if not gated:
                        dve.tensor_tensor(r, bank(key), r, ALU.add).then_inc(taken_of(key), 1)
                        continue
                    if i >= 2:
                        dve.wait_ge(vector_step, line.n)
                    tmp = wo_t[:, i % 2, :]
                    dve.tensor_tensor(tmp, bank(key), GB[:, stream_of(t), c * 512:(c + 1) * 512], ALU.mult).then_inc(taken_of(key), 1)
                    dve.wait_ge(*taken_after(key))
                    if signal is not None and t == NT - 1:
                        dve.tensor_tensor(r, r, tmp, ALU.add).then_inc(signal.sem, 1)
                    else:
                        dve.tensor_tensor(r, r, tmp, ALU.add).then_inc(vector_step, line.one())

            def split_rows(X, key, n, r0, nrow, lo):
                b = 4 * (n % 2)
                dve.wait_ge(part_hi.sem, part_hi.after(key))
                c = slice(lo, lo + X.shape[2])
                dve.tensor_tensor(HL[:, b:b + nrow, c], X[:, r0:r0 + nrow, :], HH[:, b:b + nrow, c], ALU.subtract).then_inc(part_lo.sem, 1)

            def ffn(li):
                norm(("n2", li))
                lo = 0 if li == 0 else 256
                live = range(NT) if li == 0 else range(2, NT)
                w = 512 - lo
                ns = w // 256

                def conv(f, a):
                    key, j = ("u", li, f, a), f % 2
                    dve.wait_ge(f_mid.sem, f_mid.after((li, f, a)))
                    u3 = bank(key, w).rearrange("p (s n) -> p s n", s=ns)
                    o3 = FC[:, j, a, 0:w].rearrange("p (s n) -> p s n", s=ns)
                    dve.scalar_tensor_tensor(o3[:, :, 1:256], u3[:, :, 0:255], pcol(("cw", li, 0), a * FT + f),
                                             o3[:, :, 1:256], ALU.mult, ALU.add).then_inc(vector_step, line.one())
                    dve.wait_ge(vector_step, line.n)
                    dve.scalar_tensor_tensor(o3[:, :, 0:255], u3[:, :, 1:256], pcol(("cw", li, 2), a * FT + f),
                                             o3[:, :, 0:255], ALU.mult, ALU.add).then_inc(taken_of(key), 1)
                    dve.wait_ge(*taken_after(key))

                ahead = splits(("w_up", li))
                next(ahead)
                for f2 in range(FT // 2):
                    for a in range(2):
                        for j in range(2):
                            conv(2 * f2 + j, a)
                        for lj in fill(("w_up", li), 2 * f2 + a):
                            ada(*lj)
                        next(ahead)
                    for j in range(2):
                        f = 2 * f2 + j
                        dve.wait_ge(f_exp.sem, f_exp.after((li, f)))
                        dve.tensor_tensor(HF[:, f, lo:512], FC[:, j, 2, 0:w], FC[:, j, 1, 0:w], ALU.mult).then_inc(f_out.sem, 1)
                ahead = splits(("w_down", li))
                keys = [(("w_down", li, c, r0), r0, nrow) for c in range(2) for r0, nrow in DOWN]
                for n, (key, r0, nrow) in enumerate(keys):
                    split_rows(HF[:, :, lo:512], key, n, r0, nrow, lo)
                    next(ahead)
                    if n == len(DOWN) + 2:
                        add_out(("w_down", li), live, 0, True)
                add_out(("w_down", li), live, 1, True, res_new)

            dve.wait_ge(s_const, 32)
            dve.tensor_copy(masks[:, :], arena[:, 0:2 * LEVELS * P]).then_inc(s_mask, 1)
            dve.memset(EPS_COL, EPS).then_inc(s_eps, 1)
            dve.wait_ge(s_small, 16 * len(small_ins))
            for li in range(DEPTH):
                for a in range(2):
                    dve.tensor_tensor_reduce(out=lam_tmp, in0=lam_rows[:, li, 2 * a, :], in1=lam_rows[:, li, 2 * a + 1, :],
                                             scale=1.0, scalar=0.0, op0=ALU.mult, op1=ALU.add,
                                             accum_out=lam2[:, li, a:a + 1]).then_inc(lam_sum, 1)
                    dve.wait_ge(lam_sum, 2 * li + a + 1)
            dve.wait_ge(lam_exp, 1)
            for li in range(DEPTH):
                dve.tensor_tensor(neglam[:, li:li + 1], lam2[:, li, 1:2], lam2[:, li, 0:1], ALU.subtract).then_inc(vector_step, line.one())
                dve.wait_ge(vector_step, line.n)
                dve.tensor_scalar(neglam[:, li:li + 1], neglam[:, li:li + 1], -(0.8 - 0.6 * math.exp(-0.3 * li)), None, ALU.add).then_inc(vector_step, line.one())
            for c in range((NCOL + P - 1) // P):
                dve.wait_ge(*taken_after(("cols", c)))
            for n in range(8):
                ada(0, n)
            for li in range(DEPTH):
                norm(("n1", li))
                w_in(li)
                hgrn(li)
                attention(li)
                live = range(NT) if li == 0 else range(2, NT)
                add_out(("w_out", li), live, 0, True)
                add_out(("w_out", li), live, 1, True, res_new)
                ffn(li)
            norm(("fn", 0))
            norm(("cn", 0))
            ahead = splits(("c_in",))
            next(ahead)
            for e2 in range(ET // 2):
                for q in C_IN:
                    for j in range(2):
                        e = 2 * e2 + j
                        key = ("c", e, q)
                        v, s_, cv = CC[:, j, 0, :], CC[:, j, 1, :], CC[:, j, 2, :]
                        if q == 2:
                            dve.wait_ge(*taken_after(("c", e, 1)))
                            dve.wait_ge(full, full_after(key))
                            dve.tensor_tensor(v, bank(key, 256), v, ALU.mult).then_inc(taken_of(key), 1)
                            dve.wait_ge(*taken_after(key))
                            dve.tensor_scalar(cv, v, pcol(("cw2", 2), e), None, ALU.mult).then_inc(vector_step, line.one())
                            for d, tap in ((1, 1), (2, 0)):
                                dve.wait_ge(vector_step, line.n)
                                dve.scalar_tensor_tensor(cv[:, d:256], v[:, 0:256 - d], pcol(("cw2", tap), e), cv[:, d:256],
                                                         ALU.mult, ALU.add).then_inc(vector_step, line.one())
                        if q == 0:
                            dve.wait_ge(*taken_after(("c", e, 3)))
                            dve.wait_ge(full, full_after(key))
                            dve.tensor_tensor(s_, bank(key, 256), s_, ALU.mult).then_inc(taken_of(key), 1)
                            dve.wait_ge(*taken_after(key))
                            dve.tensor_tensor(YC[:, e, :], s_, cv, ALU.mult).then_inc(c_out.sem, 1)
                    next(ahead)
            ahead = splits(("c_out",))
            for n, (c, (r0, nrow)) in enumerate([(c, part) for c in range(2) for part in C_OUT]):
                split_rows(YC, ("c_out", c, r0), n, r0, nrow, 256)
                next(ahead)
                if n == len(C_OUT) + 2:
                    add_out(("c_out",), (2, 3), 0, False)
            add_out(("c_out",), (2, 3), 1, False)
            dve.wait_ge(full, full_after("vec"))
            dve.tensor_copy(vec, bank("vec")[0:NG * NH, 0:384]).then_inc(taken_of("vec"), 1)
            norm(("an", 0))
            ahead = splits(("a_in",))
            next(ahead)
            pend = []

            def q_place(key):
                g, a, j = key
                d = QK2[:, g, a, 2 * j:2 * j + 2, :].rearrange("p m (t n) -> p (m t) n", t=2)
                return backwards(d) if a == 0 else d

            def scale(four):
                for key in four:
                    r = RQ[:, QKEYS.index(key) % 4, :].rearrange("p (m n) -> p m n", m=4)
                    dve.wait_ge(q_rs.sem, q_rs.after(key))
                    dve.tensor_tensor(q_place(key), q_place(key), r, ALU.mult).then_inc(q_done.sem, 1)

            for g, a, j in A_IN:
                if g != "z" and a < 2:
                    key = (g, a, j)
                    dve.wait_ge(q_sq.sem, q_sq.after(key))
                    dve.tensor_scalar(q_place(key), bank(("qk", key)).rearrange("p (m n) -> p m n", m=4), pcol(("gain", a), g), None,
                                      ALU.mult).then_inc(taken_of(("qk", key)), 1)
                    dve.wait_ge(*taken_after(("qk", key)))
                    pend.append(key)
                    if len(pend) == 5:
                        scale(pend[:4])
                        pend = pend[4:]
                elif a == 2 and j == 0:
                    scale(pend)
                    pend = []
                next(ahead)
            for st in range(len(BU) + 2):
                if st < len(BU):
                    u = st
                    h, t = BU[u]
                    b = u % 2
                    n = (t + 1) * P
                    if t == 0:
                        dve.wait_ge(s_bias[h % 3], 16 * (h // 3 + 1))
                    if u >= 2:
                        dve.wait_ge(full, full_after(("eT", u - 2, 1)))
                    for part_, gs in enumerate(((0, 1), (2,))):
                        key = ("s2", u, part_)
                        dve.wait_ge(full, full_after(key))
                        g0, ng = gs[0], len(gs)
                        src = bank(key).rearrange("p (g n) -> p g n", g=2)[:, 0:ng, 0:n]
                        dve.scalar_tensor_tensor(LG[:, b, g0:g0 + ng, 0:n], src, 0.125,
                                                           BIAS[:, h % 3, g0:g0 + ng, 256 - n:256], ALU.mult, ALU.add).then_inc(taken_of(key), 1)
                        dve.wait_ge(*taken_after(key))
                    dve.tensor_reduce(bred[:, b:b + 1], LG[:, b, :, 0:n], AX.XY, ALU.max).then_inc(vector_step, line.one())
                    dve.wait_ge(vector_step, line.n)
                    dve.tensor_scalar(bmax[:, b:b + 1], bred[:, b:b + 1], -1.0, None, ALU.mult).then_inc(b_max.sem, 1)
                if 0 <= st - 1 < len(BU):
                    u = st - 1
                    h, t = BU[u]
                    n = (t + 1) * P
                    key = ("eT", u, 1)
                    dve.wait_ge(full, full_after(key))
                    if u >= 2:
                        dve.wait_ge(full, full_after(("o2", u - 2)))
                    dve.tensor_copy(E3[:, u % 2, 512:512 + n], bank(key, n)).then_inc(taken_of(key), 1)
                    b = u % 2
                    dve.wait_ge(b_exp.sem, b_exp.after(BU[u]))
                    if u >= 2:
                        dve.wait_ge(*taken_after(("o2", u - 2)))
                    dve.reciprocal(brec[:, b:b + 1], bsum[:, b:b + 1]).then_inc(vector_step, line.one())
                    dve.wait_ge(vector_step, line.n)
                if 0 <= st - 2:
                    u = st - 2
                    h, t = BU[u]
                    b = u % 2
                    dve.wait_ge(full, full_after(("o2", u)))
                    dve.tensor_scalar(Y2[:, t, h * 64:(h + 1) * 64], bank(("o2", u), 64), brec[:, b:b + 1], None,
                                                      ALU.mult).then_inc(taken_of(("o2", u)), 1)
            for k in range(KT):
                dve.wait_ge(full, full_after(("yT", k)))
                dve.tensor_tensor(YT2[:, k, :], bank(("yT", k), 256), ZS[:, k, :], ALU.mult).then_inc(taken_of(("yT", k)), 1)
            for c in range(2):
                for t in range(2):
                    key = ("a_out", c, t)
                    dve.wait_ge(full, full_after(key))
                    r = RES[:, 2 + t, c * 512:(c + 1) * 512]
                    dve.tensor_tensor(r, bank(key), r, ALU.add).then_inc(taken_of(key), 1)


_INS = ["x", "c", "ctx", "c_ctx", "w_ada", "b_ada", "norm1_w", "norm2_w", "w_in", "lam_qk", "subln_w", "lb_param",
        "hgrn_norm_w", "w_fnet", "w_out", "w_up", "conv_w", "conv_b", "w_down", "final_norm_w", "conv_norm_2",
        "conv_w_in_2", "conv_w_2", "conv_w_out_2", "attn_norm_2", "attn_w_in_2", "attn_q_gain_2", "attn_k_gain_2",
        "attn_w_out_2", "rel_bias_2"]


def kernel(**inputs):
    import numpy as _np
    import concourse.bacc as _bacc
    from concourse import mybir as _mybir
    from concourse.bass_utils import run_bass_kernel_spmd as _run

    nc = _bacc.Bacc("TRN2", target_bir_lowering=False, num_devices=1)
    arrays, args = {}, {}
    for name in _INS:
        a = _np.ascontiguousarray(inputs[name])
        arrays[f"in_{name}_dram"] = a
        args[name] = nc.dram_tensor(f"in_{name}_dram", a.shape, _mybir.dt.from_np(a.dtype), kind="ExternalInput").ap()
    consts = []
    for name, a in zip(("wide", "masks", "hot", "tab"), constants()):
        arrays[f"const_{name}_dram"] = a
        consts.append(nc.dram_tensor(f"const_{name}_dram", a.shape, _mybir.dt.from_np(a.dtype), kind="ExternalInput").ap())
    out = nc.dram_tensor("out_0_dram", (1, SEQ, DM), F32, kind="ExternalOutput").ap()
    program(nc, args, *consts, out)
    r = _run(nc, [arrays], core_ids=[0])
    return r.results[0]["out_0_dram"]
```

```python
import math
from contextlib import ExitStack

import numpy as np

import concourse.bass as bass
from concourse import mybir

F32 = mybir.dt.float32
F32R = mybir.dt.float32r
U8 = mybir.dt.uint8
ALU = mybir.AluOpType
ACT = mybir.ActivationFunctionType
AX = mybir.AxisListType

P = 128
DM = 1024
KT = DM // P
SEQ = 256
NT = 4
DEPTH = 2
EPS = 1e-6
NH_A = 4
DFF = 2816
FT = DFF // P
CEXP = 2048
ET = CEXP // P
NG = 3
NH = 16
LEVELS = 8
BANKS = 8
SLOTS = 3
SLOT = KT * 256
SMALL = 368
HIGH = 3
NEG = -1.0e30


def level_block(level):
    return 2 ** (level - 1)


def scan_matrices():
    u, tau = np.arange(P)[:, None], np.arange(P)[None, :]
    out = np.zeros((P, 2, 9, P), np.float32)
    for level in range(1, LEVELS):
        b = level_block(level)
        mid = tau // (2 * b) * 2 * b + b
        out[:, 0, level - 1] = np.where(tau >= mid, (u >= mid) & (u <= tau), (u > tau) & (u < mid))
        out[:, 1, level - 1] = np.where(tau < mid, (u >= tau) & (u < mid), (u >= mid) & (u < tau))
    out[:, 0, 7], out[:, 1, 7] = u <= tau, u >= tau
    out[:, 0, 8], out[:, 1, 8] = u > tau, u < tau
    return out.reshape(P, -1)


def level_masks():
    s, t = np.arange(P)[:, None], np.arange(P)[None, :]
    out = np.zeros((P, 2, LEVELS, P), np.float32)
    out[:, 0, 0] = out[:, 1, 0] = s == t
    for level in range(1, LEVELS):
        b = level_block(level)
        same = s // (2 * b) == t // (2 * b)
        out[:, 0, level] = same & (s // b % 2 == 0) & (t // b % 2 == 1)
        out[:, 1, level] = same & (s // b % 2 == 1) & (t // b % 2 == 0)
    return out.reshape(P, -1)


def rope_tables():
    pos = np.arange(SEQ)
    half = 32
    inv = (np.float32(10000.0) ** (-np.arange(0, half, 2, dtype=np.float32) / half)).astype(np.float32)
    ar = (pos // 64).astype(np.float32)[:, None] * inv
    ac = (pos % 64).astype(np.float32)[:, None] * inv
    ang = np.concatenate([ar, ar, ac, ac], axis=-1).T
    ang = np.concatenate([ang, ang], axis=0)
    return np.cos(ang).astype(np.float32), np.sin(ang).astype(np.float32)


def rotate_matrix():
    r = np.zeros((P, P), np.float32)
    for base in range(0, P, 32):
        for m in range(16):
            r[base + m + 16, base + m] = -1.0
            r[base + m, base + m + 16] = 1.0
    return r


def t5_bucket(dist):
    d = np.maximum(dist, 1).astype(np.float32)
    large = 16 + (np.log(d / np.float32(16)) / np.float32(math.log(2048 / 16)) * np.float32(16)).astype(np.int32)
    return np.where(dist < 16, dist, np.minimum(large, 31))


def constants():
    ident = np.eye(P, dtype=np.float32)
    k = np.arange(SEQ, dtype=np.float64)
    ang = 2 * np.pi * (np.outer(k, k) % SEQ) / SEQ
    scale = 1.0 / math.sqrt(SEQ * 64)
    both = np.concatenate([np.cos(ang), np.sin(ang)], axis=1) * scale
    dft_seq = both.reshape(2, P, 512).transpose(1, 0, 2).reshape(P, -1).astype(np.float32)
    d = np.arange(64, dtype=np.float64)
    ang = 2 * np.pi * (np.outer(d, d) % 64) / 64
    two = np.eye(2)
    dft_cos = np.kron(two, np.cos(ang)).astype(np.float32)
    dft_sin = np.kron(two, -np.sin(ang)).astype(np.float32)
    cos, sin = rope_tables()
    sel = np.zeros((P, 2, P), np.float32)
    sel[0:4:2, 0], sel[1:4:2, 1] = 1.0, 1.0
    means = np.kron(two, np.ones((64, 64))).astype(np.float32)
    wide = np.concatenate([ident, ident[::-1], sel.reshape(P, -1), means, dft_seq, dft_cos, dft_sin, rotate_matrix(), cos, sin,
                           scan_matrices()], axis=1)
    dist = 255 - np.arange(384)
    hot = np.zeros((32 + NG, 384), np.float32)
    tab = np.zeros((NG, NG * NH), np.float32)
    bucket = t5_bucket(np.maximum(dist, 0))
    for m in range(384):
        hot[bucket[m], m] = 1.0
    for g, dil in enumerate((1, 4, 16)):
        hot[32 + g] = ~((dist >= 0) & (dist % dil == 0) & (dist // dil <= 128))
        tab[g, g * NH:(g + 1) * NH] = NEG
    return np.ascontiguousarray(wide), level_masks(), hot, tab


class Signal:

    def __init__(self, sem, keys):
        self.sem = sem
        self.count = {k: i + 1 for i, k in enumerate(keys)}

    def after(self, key):
        return self.count[key]


class Line:

    def __init__(self):
        self.n = 0

    def one(self):
        self.n += 1
        return 1


def program(nc, A, wide_c, mask_c, hot_c, tab_c, out):
    ctx = ExitStack()

    def sb(name, cols, dt=F32, rows=P):
        return ctx.enter_context(nc.sbuf_tensor(name, [rows, cols], dt))

    def sem(name):
        return ctx.enter_context(nc.semaphore(name))

    with ctx:
        def at_top(name, cols, dt, above):
            return nc.alloc_sbuf_tensor_at(name, [P, cols], dt, offset=top + 4 * above)

        top = (nc.sbuf_top - 4 * (SLOTS * SLOT + 2 * KT * 512)) // 32 * 32
        ring = at_top("weights", SLOTS * SLOT, F32, 0)
        ring_lo = at_top("weights_low", SLOTS * SLOT, F32R, 0)
        ht_hi = at_top("normed_t_high", KT * 512, F32R, SLOTS * SLOT)
        ht_lo = at_top("normed_t_low", KT * 512, F32R, SLOTS * SLOT + KT * 512)
        ht_r = at_top("mixer_scratch", KT * 512, F32, SLOTS * SLOT)
        ht_b = at_top("mixer_scratch_2", KT * 512, F32, SLOTS * SLOT + KT * 512)
        ring_hi = sb("weights_high", HIGH * SLOT, F32R)
        res = sb("residual", NT * DM)
        arena = sb("arena", 12288)
        mg = sb("merge_and_gates", 6144)
        scr = sb("scratch", 3840)
        wide = sb("wide_consts", 128 * 4 + 128 + 1024 + 256 + 128 + 512 + 2304)
        masks = sb("level_masks_sb", 2 * LEVELS * P, U8)
        cols = sb("param_columns", 568)
        small = sb("small", SMALL)
        cond_t = sb("conditioning_split", 4 * KT, F32R)
        assert nc.sbuf_base <= top
        ps = ctx.enter_context(nc.psum_tensor("acc", [P, BANKS, 512], F32))

        RES = res[:, :].rearrange("p (t n) -> p t n", t=NT)
        HH = ht_hi[:, :].rearrange("p (k n) -> p k n", k=KT)
        HL = ht_lo[:, :].rearrange("p (k n) -> p k n", k=KT)
        MT = mg[:, 0:4096].rearrange("p (k n) -> p k n", k=8)
        XS = mg[:, 0:4096].rearrange("p (t n) -> p t n", t=NT)
        GB = mg[:, 4096:6144].rearrange("p (s n) -> p s n", s=2)
        SP = mg[:, 0:2048].rearrange("p (t n) -> p t n", t=NT)
        BG = mg[:, 2048:4096].rearrange("p (t n) -> p t n", t=NT)
        KTOK = ht_b[:, 0:2048].rearrange("p (t n) -> p t n", t=NT)
        OREC = mg[:, 2048:3072].rearrange("p (t n) -> p t n", t=NT)
        V2 = mg[:, 0:6144].rearrange("p (g t n) -> p g t n", g=NG, t=2)
        ZS = res[:, 0:2048].rearrange("p (k n) -> p k n", k=KT)
        VA = arena[:, 0:2048].rearrange("p (t n) -> p t n", t=NT)
        GL = arena[:, 2048:4096].rearrange("p (t n) -> p t n", t=NT)
        IH = arena[:, 4096:5120].rearrange("p (t n) -> p t n", t=NT)
        GH = arena[:, 5120:6144].rearrange("p (t n) -> p t n", t=NT)
        UF = arena[:, 6144:7168].rearrange("p (t n) -> p t n", t=NT)
        QA = arena[:, 7168:9216].rearrange("p (h n) -> p h n", h=NH_A)
        KA = arena[:, 9216:11264].rearrange("p (h n) -> p h n", h=NH_A)
        QH = arena[:, 11264:12288].rearrange("p (k n) -> p k n", k=2)
        HF = arena[:, 0:FT * 512].rearrange("p (f n) -> p f n", f=FT)
        YC = arena[:, 0:ET * SEQ].rearrange("p (f n) -> p f n", f=ET)
        QK2 = arena[:, :].rearrange("p (g a h n) -> p g a h n", g=NG, a=2, h=8)
        at = [0]

        def part(t, n, pos=at):
            pos[0] += n
            return t[:, pos[0] - n:pos[0]]

        FIRST = 4 * 128
        ident = part(wide, 128)
        flip = part(wide, 128)
        sel = part(wide, 256).rearrange("p (s n) -> p s n", s=2)
        means = part(wide, 128)
        dft_seq = part(wide, 1024).rearrange("p (k n) -> p k n", k=2)
        dft_cos, dft_sin, rot = part(wide, 128), part(wide, 128), part(wide, 128)
        cosT, sinT = part(wide, 256), part(wide, 256)
        m0 = at[0]
        SM = part(wide, 2304).rearrange("p (d l n) -> p d l n", d=2, l=9)
        BIAS = wide[:, m0:m0 + 2304].rearrange("p (b g n) -> p b g n", b=3, g=NG)
        MASK = masks[:, :].rearrange("p (d l n) -> p d l n", d=2, l=LEVELS)
        pos = [0]

        def sm(n):
            return part(small, n, pos)

        ssq, rstd, EPS_COL = sm(4), sm(4), sm(1)
        modt = sm(128).rearrange("p (l m k s) -> p l m k s", l=2, m=4, k=KT)
        csil = sm(16).rearrange("p (s k) -> p s k", s=2)
        nscale = sm(16).rearrange("p (k s) -> p k s", k=KT)
        hw = sm(128).rearrange("p (l n) -> p l n", l=2)
        lam2 = sm(4).rearrange("p (l a) -> p l a", l=2)
        neglam = sm(2)
        amax = sm(4).rearrange("p (b c) -> p b c", b=2)
        asum = sm(4).rearrange("p (b c) -> p b c", b=2)
        arec = sm(4).rearrange("p (b c) -> p b c", b=2)
        ossq, orstd = sm(2), sm(2)
        hssq, hrstd = sm(16).rearrange("p (t h) -> p t h", t=4), sm(16).rearrange("p (t h) -> p t h", t=4)
        minus_half = sm(4)
        bred, bmax, bsum, brec = sm(3), sm(3), sm(3), sm(3)
        rows = scr[:, 0:640].rearrange("p (c n) -> p c n", c=5)
        lam_rows = scr[:, 640:1152].rearrange("p (l a n) -> p l a n", l=2, a=4)
        lam_tmp = scr[:, 1152:1216]
        lb_rows = scr[:, 2048:3072].rearrange("p (l n) -> p l n", l=2)
        XE = [scr[:, 0:2048].rearrange("p (q l n) -> p q l n", q=2, l=8),
              ht_r[:, 0:2048].rearrange("p (q l n) -> p q l n", q=2, l=8)]
        KTT = scr[:, 2048:2560].rearrange("p (b q n) -> p b q n", b=2, q=2)
        ACC = scr[:, 2560:3584].rearrange("p (d a h n) -> p d a h n", d=2, a=2, h=2)
        ST = scr[:, 3584:3840].rearrange("p (d q n) -> p d q n", d=2, q=2)
        SE = ht_r[:, 2048:2568].rearrange("p (b n) -> p b n", b=2)
        KD = ht_r[:, 2568:3080].rearrange("p (b n) -> p b n", b=2)
        rope_t = scr[:, 1536:2048].rearrange("p (b n) -> p b n", b=2)
        FS = ht_r[:, 0:1024].rearrange("p (f n) -> p f n", f=2)
        YT4 = ht_r[:, 1024:1536].rearrange("p (f n) -> p f n", f=2)
        wf = scr[:, 3072:3584].rearrange("p (f n) -> p f n", f=2)
        E2 = ht_b[:, 2048:4096].rearrange("p (b c n) -> p b c n", b=2, c=2)
        AT = arena[:, 6144:7168].rearrange("p (b n) -> p b n", b=2)
        ON = ht_r[:, 3080:3336].rearrange("p (b n) -> p b n", b=2)
        wo_t = scr[:, 0:1024].rearrange("p (b n) -> p b n", b=2)
        grow = mg[0:4, 3584:4096].rearrange("p (b n) -> p b n", b=2)
        cond = cond_t[:, :].rearrange("p (k s) -> p k s", k=KT)
        n_t = scr[:, 1024:2048].rearrange("p (b n) -> p b n", b=2)
        FC = scr[:, 0:3072].rearrange("p (b a n) -> p b a n", b=2, a=3)
        CC = scr[:, 0:2048].rearrange("p (b a n) -> p b a n", b=2, a=4)
        SQ = scr[:, 0:1024].rearrange("p (b n) -> p b n", b=2)
        RQ = scr[:, 1024:3072].rearrange("p (b n) -> p b n", b=4)
        LG = scr[:, 0:2304].rearrange("p (b g n) -> p b g n", b=3, g=NG)
        E3 = scr[:, 2304:3840].rearrange("p (b n) -> p b n", b=2)
        Y2 = ht_r[:, 0:2048].rearrange("p (t n) -> p t n", t=2)
        YT2 = mg[:, 0:2048].rearrange("p (k n) -> p k n", k=KT)
        hot = res[0:32 + NG, 0:384]
        tabx = res[0:32 + NG, 384:384 + NG * NH]
        vec = res[0:NG * NH, 512:512 + 384]
        vec_d = nc.dram_tensor("bias_rows", [NG * NH, 384], F32, kind="Internal").ap()

        slot_in = [sem(f"slot_in{i}") for i in range(SLOTS)]
        slot_part = sem("slot_read_part_way")
        read_at, parts_read = [], [0]
        full = sem("psum_full")
        taken = [sem(f"psum_taken{i}") for i in range(BANKS)]
        s_in, s_const = sem("residual_in"), sem("constants_in")
        s_first = sem("first_constants_in")
        s_small, s_eps, s_mask = sem("small_in"), sem("eps_ready"), sem("masks_ready")
        s_half = sem("minus_half_ready")
        s_lb = sem("bounds_in")
        s_wf = sem("fnet_in")
        s_gb = sem("gate_bias_in")
        s_fw = sem("final_weight_in")
        s_vec = sem("bias_rows_out")
        s_hot = sem("hot_in")
        s_bias = [sem(f"bias_in{i}") for i in range(3)]
        s_out = sem("result_out")
        vector_step, scalar_step, pool_step = sem("vector_step"), sem("scalar_step"), sem("pool_step")

        def S(name, keys):
            return Signal(sem(name), keys)

        NORMS = [("n1", 0), ("n2", 0), ("n1", 1), ("n2", 1), ("fn", 0), ("cn", 0), ("an", 0)]

        BEFORE = {("n2", 0): ("w_out", 0), ("n1", 1): ("w_down", 0), ("n2", 1): ("w_out", 1),
                  ("fn", 0): ("w_down", 1), ("cn", 0): ("final", 0)}

        def norm_tiles(N):
            return range(NT) if N in (("n1", 0), ("n2", 0), ("n1", 1)) else range(2, NT)

        nk = [(N, t) for N in NORMS for t in norm_tiles(N)]
        squared = S("row_squares", nk)
        row_scale = S("row_scale", nk)
        scaled = S("scaled", [k for k in nk if k[0] != ("fn", 0)])
        res_new = S("residual_new", [(*st, t) for st, first in ((("w_out", 0), 0), (("w_down", 0), 0), (("w_out", 1), 2), (("w_down", 1), 2), (("final", 0), 2))
                                     for t in range(first, NT)])
        s_silu, c_ready = sem("silu_of_c"), sem("c_ready")
        lam_sum, lam_exp = sem("lam_sum"), sem("lam_exp")
        lb_abs, lb_exp = sem("lb_difference"), sem("lb_logs")
        gate_keys = [(li, t) for li in range(DEPTH) for t in range(NT)]
        z_soft = S("z_softplus", gate_keys)
        b_gap = S("bound_gap", [k for k in gate_keys if k[0]])
        b_soft = S("bound_softplus", [k for k in gate_keys if k[0]])
        g_ready = S("g_ready", gate_keys)
        k_ready = S("k_ready", gate_keys)

        def units(li):
            out_ = []
            for f, b in ((0, 1), (1, 0), (2, 3), (3, 2)):
                out_ += [(0, f), (1, b)]
            return out_

        HGRN_STEPS = 20
        UN = [(li, i) for li in range(DEPTH) for i in range(8)]

        def is_full(li, i):
            return li == 0 or i >= 4

        z_ready = S("z_ready", [u for u in UN if is_full(*u)])
        kd_ready = S("kd_ready", [u for u in UN if u[1] < 6])
        rec_keys = [(li, t) for li in range(DEPTH) for t in (range(NT) if li == 0 else range(2, NT))]
        rec_sum = S("rec_sum", rec_keys)
        og_exp = S("og_exp", rec_keys)
        rec_ready = S("rec_ready", rec_keys)

        def att_units(li):
            return [(t, h) for t in (range(NT) if li == 0 else range(2, NT)) for h in range(NH_A)]

        AU = [(li, u) for li in range(DEPTH) for u in range(len(att_units(li)))]
        a_max = S("a_max", AU)
        a_exp = S("a_exp", AU)
        a_ready = S("a_ready", AU)
        o_sq = S("o_squared", AU)
        o_rs = S("o_scale", AU)
        FK = [(li, f) for li in range(DEPTH) for f in range(FT)]
        f_mid = S("ff_centre", [(li, 2 * f2 + j, a) for li in range(DEPTH) for f2 in range(FT // 2) for a in range(2) for j in range(2)])
        f_exp = S("ff_silu", FK)
        f_out = S("ff_product", FK)
        CK = list(range(ET))
        c_out = S("conv_product", CK)
        QKEYS = [(g, a, j) for g in range(NG) for a in range(2) for j in range(4)]
        q_sq = S("qk_squared", QKEYS)
        q_rs = S("qk_scale", QKEYS)
        q_done = S("qk_scaled", QKEYS)
        zk = [(c, t) for c in range(2) for t in range(2)]
        BU = [(h, t) for h in range(NH) for t in range(2)]
        b_max = S("b_max", BU)
        b_exp = S("b_exp", BU)

        CONV_J = [(e, j) for e in range(ET // 2) for j in range(2)]
        col_loads = []
        ncol = [0]

        def column(rows_ap, n, halves=False):
            c0 = ncol[0]
            ncol[0] += n
            done = 0
            while done < n:
                c, r = divmod(c0 + done, P)
                m = min(n - done, P - r)
                col_loads.append((rows_ap[done:done + m, :], c, r, m, halves))
                done += m
            return c0

        def as_rows(ap):
            return ap.rearrange("(r n) -> r n", n=P)

        col = {"c": column(as_rows(A["c"].rearrange("a n -> (a n)")), 8), "cc": column(as_rows(A["c_ctx"]), 8)}
        for li in range(DEPTH):
            col["b_ada", li] = column(as_rows(A["b_ada"][li, :]), 48)
            col["n1", li] = column(as_rows(A["norm1_w"][li, :]), 8)
            col["n2", li] = column(as_rows(A["norm2_w"][li, :]), 8)
            col["subln", li] = column(A["subln_w"][li:li + 1, :], 1)
            for j in range(3):
                col["cw", li, j] = column(as_rows(A["conv_w"][li, j, :]), 2 * FT)
            col["cb", li] = column(as_rows(A["conv_b"][li, :]), 2 * FT)
        col["cn", 0] = column(as_rows(A["conv_norm_2"][0, :]), 8)
        col["an", 0] = column(as_rows(A["attn_norm_2"][0, :]), 8)
        for j in range(3):
            col["cw2", j] = column(as_rows(A["conv_w_2"][0, j, :]), ET)
        col["gain", 0] = column(A["attn_q_gain_2"][0, :, :], NG, True)
        col["gain", 1] = column(A["attn_k_gain_2"][0, :, :], NG, True)
        NCOL = ncol[0]
        assert NCOL <= 568
        small_ins = [(lam_rows.rearrange("p l a n -> p (l a n)"), A["lam_qk"].rearrange("l a n -> (l a n)").partition_broadcast(P)),
                     (hw.rearrange("p l n -> p (l n)"), A["hgrn_norm_w"].rearrange("l n -> (l n)").partition_broadcast(P))]
        for src, c, r, m, halves in col_loads:
            if halves:
                small_ins += [(rows[r:r + m, c, 0:64], src), (rows[r:r + m, c, 64:128], src)]
            else:
                small_ins.append((rows[r:r + m, c, :], src))

        def pcol(key, j=0):
            return cols[:, col[key] + j:col[key] + j + 1]

        def slot(n, t=None):
            return (ring if t is None else t)[:, (n % SLOTS) * SLOT:(n % SLOTS + 1) * SLOT]

        plan = []

        def by_columns(key, w, c0):
            plan.append((key, w[:, c0:c0 + 256].rearrange("(k p) n -> p k n", p=P)))

        def by_rows(key, w, r0, nrow, c0):
            plan.append((key, w[r0:r0 + nrow * P, c0:c0 + 512].rearrange("(k p) n -> p k n", p=P)))

        GATES = {2: 0, 5: 1}
        ADA_NO = {(li, n): 24 * li + n for li in range(DEPTH) for n in range(24)}
        FILL = {"start": ([(0, n) for n in (*range(8), 18, 19)], [1] * 10),
                ("w_in", 0): ([(0, n) for n in range(8, 18)], [1] * 10),
                ("w_up", 0): ([(0, n) for n in range(20, 24)] + [(1, n) for n in (*range(8), *range(12, 20))], [1] * 20),
                ("w_in", 1): ([(1, n) for n in range(8, 12)], [0, 0, 1, 1, 1, 1]),
                ("w_up", 1): ([(1, n) for n in range(20, 24)], [1] * 4)}

        def fill(stage, n):
            slots, each = FILL[stage]
            return slots[sum(each[:n]):sum(each[:n + 1])]

        def spread(stage, lj):
            slots, _ = FILL[stage]
            return slots[slots.index(lj) - 1:slots.index(lj)] if lj != slots[0] else []

        def last_spread(stage, n):
            slots, each = FILL[stage]
            return slots[-1:] if n == len(each) - 1 else []

        def owed(N):
            return {"n1": 2 * N[1], "n2": 2, "cn": 2, "an": 2}[N[0]]

        def plan_ada(li, n):
            by_columns(("ada", li, n), A["w_ada"][li, :, :], 256 * n)

        W_IN = [("qa", 0, 0), ("qa", 1, 256), ("ka", 0, 512), ("ka", 1, 768), ("va", 0, 1024), ("va", 1, 1024),
                ("ihgh", 0, 2304), ("ihgh", 1, 2304), ("qh", 0, 1536), ("uf", 0, 2816), ("zz", 0, 1792), ("zz", 1, 1792)]
        DOWN = [(4 * i, min(4, FT - 4 * i)) for i in range((FT + 3) // 4)]
        for lj in FILL["start"][0]:
            plan_ada(*lj)
        for li in range(DEPTH):
            W = A["w_in"][li, :, :]
            for n, (name, h, c0) in enumerate(W_IN):
                if name in ("va", "ihgh", "zz"):
                    by_rows(("w_in", li, name, h), W, 512 * h, 4, c0)
                else:
                    by_columns(("w_in", li, name, h), W, c0)
                for lj in fill(("w_in", li), n):
                    plan_ada(*lj)
            for c in range(2):
                for h in range(2):
                    by_rows(("w_out", li, c, h), A["w_out"][li, :, :], 512 * h, 4, 512 * c)
            for f2 in range(FT // 2):
                for a in range(2):
                    by_columns(("w_up", li, f2, a), A["w_up"][li, :, :], DFF * a + 256 * f2)
                    for lj in fill(("w_up", li), 2 * f2 + a):
                        plan_ada(*lj)
            for c in range(2):
                for r0, nrow in DOWN:
                    by_rows(("w_down", li, c, r0), A["w_down"][li, :, :], P * r0, nrow, 512 * c)
        C_IN = (1, 2, 3, 0)
        for e in range(ET // 2):
            for q in C_IN:
                by_columns(("c_in", e, q), A["conv_w_in_2"][0, :, :], CEXP * q + 256 * e)
        C_OUT = [(4 * i, 4) for i in range(ET // 4)]
        for c in range(2):
            for r0, nrow in C_OUT:
                by_rows(("c_out", c, r0), A["conv_w_out_2"][0, :, :], P * r0, nrow, 512 * c)
        W = A["attn_w_in_2"][0, :, :]
        A_IN = []
        for g in range(NG):
            A_IN += [(g, a, j) for a in range(2) for j in range(4)] + [(g, 2, j) for j in range(4)]
        A_IN += [("z", 0, j) for j in range(4)]
        for g, a, j in A_IN:
            if a == 2:
                by_rows(("a_in", g, a, j), W, 512 * (j % 2), 4, g * 3072 + 2048 + 512 * (j // 2))
            else:
                by_columns(("a_in", g, a, j), W, (NG * 3072 if g == "z" else g * 3072 + a * 1024) + 256 * j)
        for c in range(2):
            for h in range(2):
                by_rows(("a_out", c, h), A["attn_w_out_2"][0, :, :], 512 * h, 4, 512 * c)
        item = {key: n for n, (key, _) in enumerate(plan)}
        split_keys = list(item)
        hi_in = S("weights_high_ready", split_keys)
        lo_in = S("weights_split", split_keys)
        FS_KEYS = []
        for li in range(DEPTH):
            FS_KEYS += [("w_out", li, 0, r) for r in (0, 4)]
            FS_KEYS += [("w_down", li, c, r) for c in range(2) for r, _ in DOWN]
        FS_KEYS += [("c_out", c, r) for c in range(2) for r, _ in C_OUT]
        FS_KEYS += [("a_out", 0, r) for r in (0, 4)]
        part_rows_of = {key: 2 if key[0] == "w_down" and key[-1] == DOWN[-1][0] and DOWN[-1][1] == 2 else 4 for key in FS_KEYS}
        PAIRS = [(key, k) for key in FS_KEYS for k in range(0, part_rows_of[key], 2)]
        part_hi = S("products_high_ready", PAIRS)
        part_lo = S("products_split", PAIRS)
        ht_done = S("normed_split", [(N, k) for N in NORMS if N[0] != "fn" for k in range(KT)])

        def hi_slot(n):
            return ring_hi[:, n % HIGH * SLOT:(n % HIGH + 1) * SLOT]

        group = {}
        finished = {}

        def bank(key, n=512):
            return ps[:, group[key] % BANKS, 0:n]

        def full_after(key):
            return finished[key]

        def taken_of(key):
            return taken[group[key] % BANKS]

        def taken_after(key):
            return taken_of(key), group[key] // BANKS + 1

        def backwards(ap):
            *dims, (step, count) = ap.ap
            return bass.AP(tensor=ap.tensor, offset=ap.offset + step * (count - 1), ap=[*[list(d) for d in dims], [-step, count]])

        def weave(hgrn_steps, att_steps, total, late_steps=()):
            n = done = 0
            late = iter(late_steps)
            late_done = 0
            for early_point in hgrn_steps:
                while late_done < done:
                    next(late, None)
                    late_done += 1
                if early_point:
                    continue
                n += 1
                while done < total * n // HGRN_STEPS:
                    while late_done < done:
                        next(late, None)
                        late_done += 1
                    next(att_steps)
                    done += 1
            assert n == HGRN_STEPS and done == total

        def mixer_steps(li):
            return len(att_units(li)) + 3

        def cols_of(t):
            return slice(t * P, (t + 1) * P)

        def stream_of(t):
            return 0 if t >= 2 else 1

        block = ctx.enter_context(nc.Block())

        @block.tensor
        def _(pe):
            read = [0]

            def closed(key):
                finished[key] = len(finished) + 1
                return 1

            def open_group(key, closes_next=True):
                n = len(group)
                group[key] = n
                if closes_next:
                    closed(key)
                if n >= BANKS:
                    pe.wait_ge(taken[n % BANKS], n // BANKS)
                return ps[:, n % BANKS, :]

            def weights(key):
                n = read[0]
                assert plan[n][0] == key, (plan[n][0], key)
                read[0] += 1
                pe.wait_ge(lo_in.sem, lo_in.after(key))
                return hi_slot(n), slot(n, ring_lo)

            def halves(w, k):
                return [x.rearrange("p (k n) -> p k n", k=k) for x in w]

            def product(o, a, b, start, stop):
                (ah, al), (bh, bl) = a, b
                pe.matmul(o, ah, bh, start=start, stop=False)
                pe.matmul(o, ah, bl, start=False, stop=False)
                return pe.matmul(o, al, bh, start=False, stop=stop)

            def release(part_way=None):
                if part_way is None:
                    read_at.append((full, len(finished)))
                else:
                    part_way.then_inc(slot_part, 1)
                    parts_read[0] += 1
                    read_at.append((slot_part, parts_read[0]))

            def norm(N):
                first = True
                for k in range(KT):
                    o = open_group((N, k))
                    for t in norm_tiles(N):
                        if first:
                            pe.wait_ge(scaled.sem, scaled.after((N, t)))
                        last = pe.transpose(o[:, cols_of(t)], XS[:, t, k * P:(k + 1) * P], ident)
                    first = False
                    last.then_inc(full, 1)

            def ada(li, n):
                wh, wl = halves(weights(("ada", li, n)), KT)
                o = open_group(("ada", li, n))
                for k in range(KT):
                    pe.matmul(o[0:4, 0:256], cond[:, k, :], wh[:, k, :], start=(k == 0), stop=False)
                    last = pe.matmul(o[0:4, 0:256], cond[:, k, :], wl[:, k, :], start=False, stop=(k == KT - 1))
                last.then_inc(full, 1)
                release()

            def ada_spread(li, n):
                pe.wait_ge(*taken_after(("ada", li, n)))
                row = grow[:, ADA_NO[li, n] % 2, :]
                if n // 4 in GATES:
                    for s in range(2 if li == 0 else 1):
                        o = open_group(("gb", li, n, s))
                        pe.matmul(o[:, 0:256], sel[0:4, s, :], row, start=True, stop=True).then_inc(full, 1)
                else:
                    o = open_group(("mc", li, n))
                    for m in range(2):
                        last = pe.matmul(o[:, 2 * m:2 * m + 2], row[:, m * P:(m + 1) * P], sel[0:4, :, 0], start=True, stop=True)
                    last.then_inc(full, 1)

            def t_out(key, w, m, cs, c0=0, open_=True, close_=True, normed=None):
                o = open_group(key) if open_ else ps[:, group[key] % BANKS, :]
                wh, wl = halves(w, KT)
                for k in range(KT):
                    if normed is not None:
                        pe.wait_ge(ht_done.sem, ht_done.after((normed, k)))
                    last = product(o[:, c0:c0 + cs.stop - cs.start], (wh[:, k, m * P:(m + 1) * P], wl[:, k, m * P:(m + 1) * P]),
                                   (HH[:, k, cs], HL[:, k, cs]), k == 0, k == KT - 1)
                if close_:
                    last.then_inc(full, 1)

            def tok_out(key_of, name, tiles, n_of, c_of=cols_of):
                outs = {}
                for h in range(2):
                    wh, wl = halves(weights((*name, h)), 4)
                    for t in tiles:
                        if h == 0:
                            outs[t] = open_group(key_of(t), closes_next=False)
                        n = n_of(t)
                        for k in range(4):
                            last = product(outs[t][:, 0:n], (HH[:, 4 * h + k, c_of(t)], HL[:, 4 * h + k, c_of(t)]),
                                           (wh[:, k, 0:n], wl[:, k, 0:n]), h == 0 and k == 0, h == 1 and k == 3)
                        if h == 1:
                            last.then_inc(full, closed(key_of(t)))
                    release(last if h == 0 else None)
                    yield

            def w_in(li):
                live = range(NT) if li == 0 else range(2, NT)
                xcols = slice(0, 512) if li == 0 else slice(256, 512)
                n = 0

                def after():
                    for lj in fill(("w_in", li), n):
                        ada(*lj)
                        for before in spread(("w_in", li), lj):
                            ada_spread(*before)
                    for lj in last_spread(("w_in", li), n):
                        ada_spread(*lj)

                for name, cs in (("qa", xcols), ("ka", slice(0, 512))):
                    for h in range(2):
                        w = weights(("w_in", li, name, h))
                        for m in range(2):
                            t_out((name, li, 2 * h + m), w, m, cs, normed=("n1", li) if (name, h, m) == ("qa", 0, 0) else None)
                        release()
                        after()
                        n += 1
                if li == 0:
                    pe.wait_ge(s_const, 32)
                for name, X in (("qa", QA), ("ka", KA)):
                    for h in range(NH_A):
                        pe.wait_ge(*taken_after((name, li, h)))
                        o = open_group(("rot", name, li, h))
                        pe.matmul(o[:, 0:256], rot, X[:, h, 256:512], start=True, stop=True).then_inc(full, 1)
                for name in ("va", "ihgh"):
                    for _ in tok_out(lambda t: (name, li, t), ("w_in", li, name), range(NT),
                                     lambda t: 256 if name == "ihgh" and t not in live else 512):
                        after()
                        n += 1
                w = weights(("w_in", li, "qh", 0))
                for p in range(2):
                    t_out(("qh", li, p), w, p, xcols)
                release()
                after()
                n += 1
                wh, wl = halves(weights(("w_in", li, "uf", 0)), KT)
                for t in live:
                    o = open_group(("uf", li, t))
                    for k in range(KT):
                        last = product(o[:, 0:256], (HH[:, k, cols_of(t)], HL[:, k, cols_of(t)]), (wh[:, k, :], wl[:, k, :]),
                                       k == 0, k == KT - 1)
                    last.then_inc(full, 1)
                release()
                after()
                n += 1
                for _ in tok_out(lambda t: ("zz", li, t), ("w_in", li, "zz"), range(NT), lambda t: 512):
                    after()
                    n += 1

            def fourier(li):
                streams = (0, 1) if li == 0 else (1,)
                pe.wait_ge(s_wf, 16 * (li + 1))
                for s in streams:
                    for f in range(2):
                        o = open_group(("f1", li, s, f))
                        for k in range(2):
                            t = 2 * s + k
                            pe.wait_ge(*taken_after(("uf", li, t)))
                            last = pe.matmul(o[:, :], UF[:, t, f * P:(f + 1) * P], dft_seq[:, k, :],
                                             start=(k == 0), stop=(k == 1))
                        last.then_inc(full, 1)
                    o = open_group(("f2", li, s))
                    for f in range(2):
                        pe.wait_ge(*taken_after(("f1", li, s, f)))
                        pe.matmul(o[:, f * 256:(f + 1) * 256], dft_cos, FS[:, f, 0:256], start=True, stop=False)
                        last = pe.matmul(o[:, f * 256:(f + 1) * 256], dft_sin, FS[:, f, 256:512], start=False, stop=True)
                    last.then_inc(full, 1)
                    pe.wait_ge(*taken_after(("f2", li, s)))
                    o = open_group(("f3", li, s))
                    for c in range(2):
                        for f in range(2):
                            last = pe.matmul(o[:, c * 256:(c + 1) * 256], wf[:, f, c * P:(c + 1) * P], YT4[:, f, :],
                                             start=(f == 0), stop=(f == 1))
                    last.then_inc(full, 1)

            def hgrn(li):
                un = units(li)

                def gates(i):
                    d, t = un[i]
                    pe.wait_ge(g_ready.sem, g_ready.after((li, t)))
                    pe.wait_ge(k_ready.sem, k_ready.after((li, t)))
                    if is_full(li, i):
                        o = open_group(("kT", li, i))
                        for p in range(2):
                            last = pe.transpose(o[:, p * P:(p + 1) * P], KTOK[:, t, d * 256 + p * P:d * 256 + (p + 1) * P], ident)
                        last.then_inc(full, 1)
                        for p in range(2):
                            for hf in range(2):
                                o = open_group(("E", li, i, p, hf))
                                pe.matmul(o[:, :], GL[:, t, d * 256 + p * P:d * 256 + (p + 1) * P],
                                                SM[:, d, 4 * hf:4 * hf + 4, :], start=True, stop=True).then_inc(full, 1)
                    if i < 6:
                        o = open_group(("suf", li, i))
                        pe.matmul(o[:, 0:256], SM[:, d, 8, :], GL[:, t, d * 256:(d + 1) * 256], start=True, stop=True)
                        end = (P - 1) * (1 - d)
                        for p in range(2):
                            last = pe.matmul(o[:, 256 + p:257 + p], GL[:, t, d * 256 + p * P:d * 256 + (p + 1) * P],
                                             SM[:, d, 7, end:end + 1], start=True, stop=True)
                        last.then_inc(full, 1)

                def apply(i):
                    d, t = un[i]
                    b = i % 2
                    if is_full(li, i):
                        pe.wait_ge(z_ready.sem, z_ready.after((li, i)))
                        pe.wait_ge(*taken_after(("kT", li, i)))
                        if i == (0 if li == 0 else 4):
                            for p in range(2):
                                pe.wait_ge(*taken_after(("qh", li, p)))
                        for lp in range(4):
                            for par in range(2):
                                o = open_group(("S", li, i, lp, par))
                                r = slice(64 * par, 64 * par + 64)
                                for lv in range(2):
                                    level = 2 * lp + lv
                                    for p in range(2):
                                        c = (lv * 2 + p) * P
                                        if level == 0:
                                            zk_, zq_ = KTT[r, b, p, :], QH[r, p, cols_of(t)]
                                        else:
                                            zk_ = zq_ = XE[b][r, p, level - 1, :]
                                        last = pe.matmul(o[:, c:c + P], zk_, zq_, start=True, stop=True)
                                last.then_inc(full, 1)
                    yield
                    if is_full(li, i):
                        for par in range(2):
                            o = open_group(("O", li, i, par))
                            r = slice(64 * par, 64 * par + 64)
                            r = slice(64 * par, 64 * par + 64)
                            pe.wait_ge(*taken_after(("S", li, i, 3, par)))
                            if i >= 2:
                                pe.wait_ge(*taken_after(("SU", li, i - 2)))
                            for p in range(2):
                                h = 2 * p + par
                                last = pe.matmul(o[:, p * 64:(p + 1) * 64], ACC[:, d, par, p, :], IH[:, t, h * 64:(h + 1) * 64],
                                                 start=True, stop=(i < 2))
                                if i >= 2:
                                    last = pe.matmul(o[:, p * 64:(p + 1) * 64], XE[b][r, p, 7, :], ST[r, d, p, :],
                                                     start=False, stop=True)
                            last.then_inc(full, 1)
                    if i < 6:
                        pe.wait_ge(kd_ready.sem, kd_ready.after((li, i)))
                        o = open_group(("SU", li, i))
                        for p in range(2):
                            last = pe.matmul(o[:, p * P:(p + 1) * P], KD[:, b, p * P:(p + 1) * P], IH[:, t, p * P:(p + 1) * P],
                                             start=True, stop=True)
                        last.then_inc(full, 1)

                for t in range(NT):
                    pe.wait_ge(*taken_after(("ihgh", li, t)))
                gates(0)
                for i in range(8):
                    if i + 1 < 8:
                        gates(i + 1)
                    yield from apply(i)
                    yield
                for _ in range(4):
                    yield

            def merge_rec(li):
                for p in range(2):
                    o = open_group(("rec", li, p))
                    for t in (range(NT) if li == 0 else range(2, NT)):
                        pe.wait_ge(rec_ready.sem, rec_ready.after((li, t)))
                        last = pe.transpose(o[:, cols_of(t)], OREC[:, t, p * P:(p + 1) * P], ident)
                    last.then_inc(full, 1)

            def attention(li):
                au = att_units(li)
                for name in ("qa", "ka"):
                    for h in range(NH_A):
                        pe.wait_ge(*taken_after(("rot", name, li, h)))
                for t in range(NT):
                    pe.wait_ge(*taken_after(("va", li, t)))
                U = len(au)
                for st in range(U + 3):
                    if st < U:
                        t, h = au[st]
                        nk_ = 256 if t < 2 else 512
                        for c in range(2):
                            o = open_group(("s", li, st, c))
                            r = slice(64 * c, 64 * c + 64)
                            pe.matmul(o[:, 0:nk_], QA[r, h, cols_of(t)], KA[r, h, 0:nk_], start=True, stop=True).then_inc(full, 1)
                    if 0 <= st - 1 < U:
                        u = st - 1
                        t, h = au[u]
                        o = open_group(("aT", li, u))
                        pe.wait_ge(a_ready.sem, a_ready.after((li, u)))
                        for j in range(2 if t < 2 else 4):
                            last = pe.transpose(o[:, j * P:(j + 1) * P], E2[:, u % 2, 0, j * P:(j + 1) * P], ident)
                        last.then_inc(full, 1)
                    if 0 <= st - 2 < U:
                        u = st - 2
                        t, h = au[u]
                        o = open_group(("av", li, u))
                        pe.wait_ge(*taken_after(("aT", li, u)))
                        nj = 2 if t < 2 else 4
                        for j in range(nj):
                            last = pe.matmul(o[:, 0:P], AT[:, u % 2, j * P:(j + 1) * P], VA[:, j, h * P:(h + 1) * P],
                                             start=(j == 0), stop=(j == nj - 1))
                        last.then_inc(full, 1)
                    if 0 <= st - 3 < U:
                        u = st - 3
                        pe.wait_ge(*taken_after(("av", li, u)))
                        o = open_group(("oT", li, u))
                        pe.transpose(o[:, 0:P], ON[:, u % 2, :], ident).then_inc(full, 1)
                    yield

            def w_out(li):
                live = range(NT) if li == 0 else range(2, NT)
                for u in range(len(att_units(li))):
                    pe.wait_ge(*taken_after(("oT", li, u)))
                for p in range(2):
                    pe.wait_ge(*taken_after(("rec", li, p)))
                for s in ((0, 1) if li == 0 else (1,)):
                    pe.wait_ge(*taken_after(("f3", li, s)))
                rows_twice(("w_out", li), live, cols_of)

            def rows_twice(name, live, c_of):
                for c in range(2):
                    outs = [open_group((*name, c, t)) for t in live]
                    for h in range(2):
                        wh, wl = halves(weights((*name, c, h)), 4)
                        for t, o in zip(live, outs):
                            for k in range(4):
                                if c == 0 and t == live[0] and k % 2 == 0:
                                    pe.wait_ge(part_lo.sem, part_lo.after(((*name, 0, 4 * h), k)))
                                last = product(o[:, :], (HH[:, 4 * h + k, c_of(t)], HL[:, 4 * h + k, c_of(t)]),
                                               (wh[:, k, :], wl[:, k, :]), h == 0 and k == 0, h == 1 and k == 3)
                            if h == 1:
                                last.then_inc(full, 1)
                        release(last if h == 0 else None)

            def rows_out(name, parts, live, c_of, total):
                for c in range(2):
                    outs = [open_group((*name, c, t)) for t in live]
                    for r0, nrow in parts:
                        key = (*name, c, r0)
                        wh, wl = halves(weights(key), 4)
                        b = 4 * (FS_KEYS.index(key) % 2)
                        for t, o in zip(live, outs):
                            for k in range(nrow):
                                f = r0 + k
                                if t == live[0] and k % 2 == 0:
                                    pe.wait_ge(part_lo.sem, part_lo.after((key, k)))
                                last = product(o[:, :], (HH[:, b + k, c_of(t)], HL[:, b + k, c_of(t)]),
                                               (wh[:, k, :], wl[:, k, :]), f == 0, f == total - 1)
                                if f == total - 1:
                                    last.then_inc(full, 1)
                        release(last if r0 + nrow < total else None)

            def ffn(li):
                xcols = slice(0, 512) if li == 0 else slice(256, 512)
                live = range(NT) if li == 0 else range(2, NT)
                norm(("n2", li))
                for f2 in range(FT // 2):
                    for a in range(2):
                        w = weights(("w_up", li, f2, a))
                        for j in range(2):
                            t_out(("u", li, 2 * f2 + j, a), w, j, xcols, normed=("n2", li) if (f2, a, j) == (0, 0, 0) else None)
                        release()
                        for lj in fill(("w_up", li), 2 * f2 + a):
                            ada(*lj)
                            for before in spread(("w_up", li), lj):
                                ada_spread(*before)
                        for lj in last_spread(("w_up", li), 2 * f2 + a):
                            ada_spread(*lj)
                rows_out(("w_down", li), DOWN, live, cols_of, FT)

            pe.wait_ge(s_first, 16)
            pe.wait_ge(s_small, 16 * len(small_ins))
            for c in range((NCOL + P - 1) // P):
                n = min(P, NCOL - c * P)
                o = open_group(("cols", c))
                pe.transpose(o[:, 0:n], rows[0:n, c, :], ident[0:n, 0:n]).then_inc(full, 1)
            pe.wait_ge(c_ready, 1)
            for n in range(len(FILL["start"][0])):
                for lj in fill("start", n):
                    ada(*lj)
                    for before in spread("start", lj):
                        ada_spread(*before)
                for lj in last_spread("start", n):
                    ada_spread(*lj)
            for li in range(DEPTH):
                norm(("n1", li))
                w_in(li)
                fourier(li)
                weave(hgrn(li), attention(li), mixer_steps(li))
                merge_rec(li)
                w_out(li)
                ffn(li)

            norm(("cn", 0))
            for e in range(ET // 2):
                for q in C_IN:
                    w = weights(("c_in", e, q))
                    for j in range(2):
                        t_out(("c", 2 * e + j, q), w, j, slice(256, 512), normed=("cn", 0) if (e, q, j) == (0, C_IN[0], 0) else None)
                    release()
            rows_out(("c_out",), C_OUT, (2, 3), lambda t: slice(t * P, (t + 1) * P), ET)
            o = open_group("vec")
            pe.wait_ge(s_hot, 48)
            pe.matmul(o[0:NG * NH, 0:384], tabx, hot, start=True, stop=True).then_inc(full, 1)
            norm(("an", 0))
            pend = []

            def mean_of(key):
                pe.wait_ge(q_sq.sem, q_sq.after(key))
                o = open_group(("ms", key))
                pe.matmul(o[:, :], means, SQ[:, QKEYS.index(key) % 2, :], start=True, stop=True).then_inc(full, 1)

            for g in range(NG):
                for key in [(g, a, j) for a in range(2) for j in range(4)]:
                    w = weights(("a_in", *key))
                    t_out(("qk", key), w, 0, slice(256, 512), close_=False, normed=("an", 0) if key == (0, 0, 0) else None)
                    t_out(("qk", key), w, 1, slice(256, 512), 256, open_=False)
                    release()
                    pend.append(key)
                    if len(pend) > 1:
                        mean_of(pend.pop(0))
                for c in range(2):
                    outs = [open_group(("v2", g, c, t), closes_next=False) for t in range(2)]
                    for h in range(2):
                        wh, wl = halves(weights(("a_in", g, 2, 2 * c + h)), 4)
                        for t, o in enumerate(outs):
                            cs = slice(256 + t * P, 256 + (t + 1) * P)
                            for k in range(4):
                                last = product(o[:, :], (HH[:, 4 * h + k, cs], HL[:, 4 * h + k, cs]), (wh[:, k, :], wl[:, k, :]),
                                               h == 0 and k == 0, h == 1 and k == 3)
                            if h == 1:
                                last.then_inc(full, closed(("v2", g, c, t)))
                        release(last if h == 0 else None)
                        if pend:
                            mean_of(pend.pop(0))
            for j in range(4):
                w = weights(("a_in", "z", 0, j))
                t_out(("z2", j), w, 0, slice(256, 512), close_=False)
                t_out(("z2", j), w, 1, slice(256, 512), 256, open_=False)
                release()
            pe.wait_ge(q_done.sem, q_done.after(QKEYS[-1]))
            for g in range(NG):
                for c in range(2):
                    for t in range(2):
                        pe.wait_ge(*taken_after(("v2", g, c, t)))
            U = len(BU)
            for st in range(U + 3):
                if st < U:
                    h, t = BU[st]
                    r = slice(64 * (h % 2), 64 * (h % 2) + 64)
                    n = (t + 1) * P
                    for part_, gs in enumerate(((0, 1), (2,))):
                        o = open_group(("s2", st, part_))
                        for g in gs:
                            last = pe.matmul(o[:, g % 2 * 256:g % 2 * 256 + n], QK2[r, g, 0, h // 2, cols_of(t)],
                                             QK2[r, g, 1, h // 2, 0:n], start=True, stop=True)
                        last.then_inc(full, 1)
                if 0 <= st - 2 < U:
                    u = st - 2
                    h, t = BU[u]
                    pe.wait_ge(b_exp.sem, b_exp.after(BU[u]))
                    for part_, gs in enumerate(((0, 1), (2,))):
                        o = open_group(("eT", u, part_))
                        for g in gs:
                            for kt in range(t + 1):
                                c = (g % 2 * 2 + kt) * P
                                last = pe.transpose(o[:, c:c + P], LG[:, u % 3, g, kt * P:(kt + 1) * P], ident)
                        last.then_inc(full, 1)
                if 0 <= st - 3 < U:
                    u = st - 3
                    h, t = BU[u]
                    o = open_group(("o2", u))
                    for part_ in range(2):
                        pe.wait_ge(*taken_after(("eT", u, part_)))
                    blocks = [(g, kt) for g in range(NG) for kt in range(t + 1)]
                    for j, (g, kt) in enumerate(blocks):
                        c = (g * 2 + kt) * P
                        last = pe.matmul(o[:, 0:64], E3[:, u % 2, c:c + P], V2[:, g, kt, h * 64:(h + 1) * 64],
                                         start=(j == 0), stop=(j == len(blocks) - 1))
                    last.then_inc(full, 1)
            for u in range(U - 8, U):
                pe.wait_ge(*taken_after(("o2", u)))
            for k in range(KT):
                o = open_group(("yT", k))
                for t in range(2):
                    last = pe.matmul(o[:, t * P:(t + 1) * P], Y2[:, t, k * P:(k + 1) * P], flip, start=True, stop=True)
                last.then_inc(full, 1)
            rows_twice(("a_out",), (2, 3), cols_of)
            assert read[0] == len(plan)

        @block.sync
        def _(sp):
            sp.dma_start(wide[:, 0:FIRST], wide_c[:, 0:FIRST]).then_inc(s_first, 16)
            for dst, src in small_ins[0::2]:
                sp.dma_start(dst, src).then_inc(s_small, 16)
            for n, (key, src) in enumerate(plan):
                if n == SLOTS:
                    sp.dma_start(RES[:, 0:2, :], A["ctx"].rearrange("a (t p) n -> p (a t) n", p=P)).then_inc(s_in, 16)
                    sp.dma_start(RES[:, 2:4, :], A["x"].rearrange("a (t p) n -> p (a t) n", p=P)).then_inc(s_in, 16)
                if n == 13:
                    sp.dma_start(wide[:, FIRST:], wide_c[:, FIRST:]).then_inc(s_const, 16)
                    sp.dma_start(arena[:, 0:2 * LEVELS * P], mask_c).then_inc(s_const, 16)
                if n >= SLOTS:
                    sp.wait_ge(*read_at[n - SLOTS])
                _, k, m = src.shape
                sp.dma_start(slot(n)[:, 0:k * m].rearrange("p (k n) -> p k n", k=k), src).then_inc(slot_in[n % SLOTS], 16)
            for c in range(2):
                for t in range(2):
                    sp.wait_ge(*taken_after(("a_out", c, 2 + t)))
                    sp.dma_start(out[0, t * P:(t + 1) * P, c * 512:(c + 1) * 512],
                                 RES[:, 2 + t, c * 512:(c + 1) * 512]).then_inc(s_out, 16)
            sp.wait_ge(s_out, 64)

        @block.gpsimd
        def _(pool):
            line = Line()

            def root(dst, mean):
                pool.tensor_scalar(dst, mean, EPS, None, ALU.add).then_inc(pool_step, line.one())
                pool.wait_ge(pool_step, line.n)
                return pool.tensor_tensor(dst, dst, minus_half[:, 0:mean.shape[1]], ALU.pow)

            def pow_norm(N):
                for t in norm_tiles(N):
                    pool.wait_ge(squared.sem, squared.after((N, t)))
                    root(rstd[:, t:t + 1], ssq[:, t:t + 1]).then_inc(row_scale.sem, 1)

            def hgrn_roots(li):
                for _ in range(16):
                    yield
                for t in (range(NT) if li == 0 else range(2, NT)):
                    pool.wait_ge(rec_sum.sem, rec_sum.after((li, t)))
                    root(hrstd[:, t, :], hssq[:, t, :]).then_inc(og_exp.sem, 1)
                for _ in range(4):
                    yield

            def att_roots(li):
                U = len(att_units(li))
                for st in range(U + 3):
                    u = st - 2
                    if not 0 <= u < U:
                        yield
                        continue
                    pool.wait_ge(o_sq.sem, o_sq.after((li, u)))
                    b = slice(u % 2, u % 2 + 1)
                    root(orstd[:, b], ossq[:, b]).then_inc(o_rs.sem, 1)
                    yield

            def gate_bias(li, g):
                row = A["b_ada"][li, (2 + 3 * g) * DM:(3 + 3 * g) * DM]
                for s in range(2 if li == 0 else 1):
                    pool.dma_start(GB[:, s, :], row.partition_broadcast(P)).then_inc(s_gb, 16)

            pool.memset(minus_half, -0.5).then_inc(s_half, 1)
            pool.wait_ge(s_half, 1)
            gate_bias(0, 0)
            pool.wait_ge(full, full_after(("cols", 4)))
            pool.dma_start(wf, A["w_fnet"][0, :, :].rearrange("(f p) n -> p f n", p=P)).then_inc(s_wf, 16)
            for li in range(DEPTH):
                pow_norm(("n1", li))
                weave(hgrn_roots(li), att_roots(li), mixer_steps(li))
                pool.wait_ge(res_new.sem, res_new.after(("w_out", li, NT - 1)))
                gate_bias(li, 1)
                pow_norm(("n2", li))
                pool.wait_ge(res_new.sem, res_new.after(("w_down", li, NT - 1)))
                if li == 0:
                    gate_bias(1, 0)
                    pool.dma_start(lb_rows, A["lb_param"].rearrange("l d n -> l (d n)").partition_broadcast(P)).then_inc(s_lb, 16)
                    pool.dma_start(wf, A["w_fnet"][1, :, :].rearrange("(f p) n -> p f n", p=P)).then_inc(s_wf, 16)
            pool.dma_start(GB[:, 0, :], A["final_norm_w"].partition_broadcast(P)).then_inc(s_fw, 16)
            pow_norm(("fn", 0))
            pool.dma_start(hot, hot_c).then_inc(s_hot, 16)
            pool.dma_start(tabx[0:32, :], A["rel_bias_2"]).then_inc(s_hot, 16)
            pool.dma_start(tabx[32:32 + NG, :], tab_c).then_inc(s_hot, 16)
            pow_norm(("cn", 0))
            pool.wait_ge(*taken_after("vec"))
            pool.dma_start(vec_d, vec).then_inc(s_vec, 16)
            pool.wait_ge(s_vec, 16)
            pow_norm(("an", 0))
            for h in range(NH):
                if h >= 3:
                    pool.wait_ge(b_max.sem, b_max.after((h - 3, 1)))
                src = bass.AP(tensor=vec_d.tensor, offset=h * 384, ap=[[1, P], [NH * 384, NG], [1, 256]])
                pool.dma_start(BIAS[:, h % 3, :, :], src).then_inc(s_bias[h % 3], 16)
            for b in range(3):
                pool.wait_ge(s_bias[b], 16 * len(range(b, NH, 3)))

        @block.scalar
        def _(act):
            line = Line()
            for dst, src in small_ins[1::2]:
                act.dma_start(dst, src).then_inc(s_small, 16)
            act.wait_ge(s_eps, 1)

            def evict(key, dst, n):
                act.wait_ge(full, full_after(key))
                act.activation(dst, bank(key, n), ACT.Copy).then_inc(taken_of(key), 1)

            next_slot = [0]

            def split_next():
                n = next_slot[0]
                if n == len(plan):
                    return
                next_slot[0] += 1
                used = plan[n][1].shape[1] * plan[n][1].shape[2]
                act.wait_ge(slot_in[n % SLOTS], 16 * (n // SLOTS + 1))
                if n >= HIGH:
                    act.wait_ge(*read_at[n - HIGH])
                act.activation(hi_slot(n)[:, 0:used], slot(n)[:, 0:used], ACT.Copy).then_inc(hi_in.sem, 1)

            def squares(N, tiles=None):
                for t in norm_tiles(N) if tiles is None else tiles:
                    if N == ("n1", 0):
                        if t == 0:
                            act.wait_ge(s_in, 32)
                    elif N == ("an", 0):
                        act.wait_ge(*taken_after(("c_out", 0, t)))
                        act.wait_ge(*taken_after(("c_out", 1, t)))
                    else:
                        act.wait_ge(res_new.sem, res_new.after((*BEFORE[N], t)))
                    place = t
                    if N == ("n1", 0) and t == NT - 1:
                        place = 2
                        act.wait_ge(squared.sem, squared.after((N, t - 1)))
                    act.activation(XS[:, place, :], RES[:, t, :], ACT.Square, scale=1.0 / 32.0,
                                   accum_out=ssq[:, t:t + 1]).then_inc(squared.sem, 1)

            def norm(N):
                if N != ("n1", 0):
                    squares(N)
                if N == ("fn", 0):
                    return
                for k in range(KT):
                    act.wait_ge(full, full_after((N, k)))
                    if k >= 2:
                        act.wait_ge(ht_done.sem, ht_done.after((N, k - 2)))
                    x, v = bank((N, k)), n_t[:, k % 2, :]
                    if N[0] in ("n1", "n2"):
                        m = 0 if N[0] == "n1" else 2
                        if 0 in norm_tiles(N):
                            act.activation(v[:, 0:256], x[:, 0:256], ACT.Identity, scale=nscale[:, k, 1:2],
                                           bias=modt[:, N[1], m, k, 1:2]).then_inc(scalar_step, line.one())
                        act.activation(v[:, 256:512], x[:, 256:512], ACT.Identity, scale=nscale[:, k, 0:1],
                                       bias=modt[:, N[1], m, k, 0:1]).then_inc(taken_of((N, k)), 1)
                    else:
                        act.activation(v[:, 256:512], x[:, 256:512], ACT.Copy, scale=pcol(N, k)).then_inc(taken_of((N, k)), 1)
                for n in range(owed(N)):
                    split_next()

            def ada(li, n):
                key = ("ada", li, n)
                act.wait_ge(full, full_after(key))
                act.activation(grow[:, ADA_NO[li, n] % 2, :], bank(key)[0:4, 0:256], ACT.Copy).then_inc(taken_of(key), 1)

            def w_in(li):
                lo = 0 if li == 0 else 256
                if li:
                    act.wait_ge(lb_abs, 1)
                    act.activation(lb_rows[:, 1, :], lb_rows[:, 0, :], ACT.Abs).then_inc(scalar_step, line.one())
                    act.wait_ge(scalar_step, line.n)
                    act.activation(lb_rows[:, 1, :], lb_rows[:, 1, :], ACT.Exp, scale=-1.0).then_inc(scalar_step, line.one())
                    act.wait_ge(scalar_step, line.n)
                    act.activation(lb_rows[:, 1, :], lb_rows[:, 1, :], ACT.Ln, bias=1.0).then_inc(lb_exp, 1)
                for n, (name, h, _) in enumerate(W_IN):
                    if name in ("qa", "ka"):
                        X, l0 = (QA, lo) if name == "qa" else (KA, 0)
                        for m in range(2):
                            evict((name, li, 2 * h + m), X[:, 2 * h + m, l0:512], 512 - l0)
                    elif name == "va" and h:
                        if li == 0:
                            act.wait_ge(s_mask, 1)
                        for t in range(NT):
                            evict(("va", li, t), VA[:, t, :], 512)
                    elif name == "ihgh" and h:
                        for t in range(NT):
                            key = ("ihgh", li, t)
                            act.wait_ge(full, full_after(key))
                            if li == 0 or t >= 2:
                                act.activation(GH[:, t, :], bank(key)[:, 256:512], ACT.Silu).then_inc(scalar_step, line.one())
                            act.activation(IH[:, t, :], bank(key)[:, 0:256], ACT.Copy).then_inc(taken_of(key), 1)
                    elif name == "qh":
                        for p in range(2):
                            evict(("qh", li, p), QH[:, p, lo:512], 512 - lo)
                    elif name == "uf":
                        for t in (range(NT) if li == 0 else range(2, NT)):
                            evict(("uf", li, t), UF[:, t, :], 256)
                    for lj in fill(("w_in", li), n):
                        ada(*lj)
                        split_next()
                    if n < len(W_IN) - 1:
                        split_next()
                first = 0 if li == 0 else 1
                for t in range(NT):
                    act.wait_ge(full, full_after(("zz", li, t)))
                    act.activation(SP[:, t, :], bank(("zz", li, t)), ACT.Abs).then_inc(scalar_step, line.one())
                act.wait_ge(scalar_step, line.n)
                for t in range(NT):
                    act.activation(SP[:, t, :], SP[:, t, :], ACT.Exp, scale=-1.0).then_inc(scalar_step, line.one())
                act.wait_ge(scalar_step, line.n)
                for t in range(NT):
                    act.activation(SP[:, t, :], SP[:, t, :], ACT.Ln, bias=1.0).then_inc(z_soft.sem, 1)
                for f in range(2):
                    evict(("f1", li, first, f), FS[:, f, :], 512)
                if li:
                    for t in range(NT):
                        act.wait_ge(b_gap.sem, b_gap.after((li, t)))
                        act.activation(BG[:, t, :], BG[:, t, :], ACT.Abs).then_inc(scalar_step, line.one())
                evict(("f2", li, first), YT4, 512)
                if li:
                    act.wait_ge(scalar_step, line.n)
                    for t in range(NT):
                        act.activation(BG[:, t, :], BG[:, t, :], ACT.Exp, scale=-1.0).then_inc(scalar_step, line.one())
                    act.wait_ge(scalar_step, line.n)
                    for t in range(NT):
                        act.activation(BG[:, t, :], BG[:, t, :], ACT.Ln, bias=1.0).then_inc(b_soft.sem, 1)
                for t in range(NT):
                    act.wait_ge(*taken_after(("zz", li, t)))
                    act.activation(KTOK[:, t, :], KTOK[:, t, :], ACT.Exp).then_inc(k_ready.sem, 1)
                split_next()

            def fourier(li):
                act.wait_ge(g_ready.sem, g_ready.after((li, NT - 1)))
                for s in ((0, 1) if li == 0 else (1,)):
                    if li == 0 and s:
                        for f in range(2):
                            evict(("f1", li, s, f), FS[:, f, :], 512)
                        evict(("f2", li, s), YT4, 512)
                    key = ("f3", li, s)
                    act.wait_ge(full, full_after(key))
                    act.activation(MT[:, 6:8, s * 256:(s + 1) * 256],
                                   bank(key).rearrange("p (c n) -> p c n", c=2), ACT.Copy).then_inc(taken_of(key), 1)

            def hgrn(li):

                def gates(i):
                    b = i % 2
                    if is_full(li, i):
                        for p in range(2):
                            for hf in range(2):
                                key = ("E", li, i, p, hf)
                                act.wait_ge(full, full_after(key))
                                if i >= 2 and is_full(li, i - 2):
                                    act.wait_ge(full, full_after(("O", li, i - 2, 1)))
                                act.activation(XE[b][:, p, 4 * hf:4 * hf + 4, :],
                                                         bank(key).rearrange("p (l n) -> p l n", l=4), ACT.Exp).then_inc(taken_of(key), 1)
                    if i < 6:
                        key = ("suf", li, i)
                        act.wait_ge(full, full_after(key))
                        if i >= 2:
                            act.wait_ge(*taken_after(("SU", li, i - 2)))
                        act.activation(SE[:, b, 0:258], bank(key, 258), ACT.Exp).then_inc(taken_of(key), 1)

                gates(0)
                for i in range(8):
                    if i + 1 < 8:
                        gates(i + 1)
                    yield
                    yield
                for _ in range(4):
                    yield

            def merge_rec(li):
                for p in range(2):
                    key = ("rec", li, p)
                    lo = 0 if li == 0 else 256
                    act.wait_ge(full, full_after(("rec", li, 1)))
                    act.activation(MT[:, 4 + p, lo:512], bank(key)[:, lo:512], ACT.Copy).then_inc(taken_of(key), 1)
                act.wait_ge(*taken_after(("rec", li, 1)))

            def attention(li):
                au = att_units(li)
                U = len(au)
                lam_init = 0.8 - 0.6 * math.exp(-0.3 * li)
                for st in range(U + 3):
                    if st < U:
                        u = st
                        t, h = au[u]
                        n = 256 if t < 2 else 512
                        act.wait_ge(a_max.sem, a_max.after((li, u)))
                        if u >= 2:
                            act.wait_ge(full, full_after(("aT", li, u - 2)))
                        if u >= 2:
                            act.wait_ge(a_ready.sem, a_ready.after((li, u - 2)))
                        for c in range(2):
                            ins = act.activation(E2[:, u % 2, c, 0:n], bank(("s", li, u, c), n), ACT.Exp, scale=0.125,
                                                 bias=amax[:, u % 2, c:c + 1], accum_out=asum[:, u % 2, c:c + 1])
                            ins.then_inc(taken_of(("s", li, u, c)), 1)
                    if 0 <= st - 1 < U:
                        u = st - 1
                        t, h = au[u]
                        n = 256 if t < 2 else 512
                        if u >= 2:
                            act.wait_ge(full, full_after(("av", li, u - 2)))
                        evict(("aT", li, u), AT[:, u % 2, 0:n], n)
                    if 0 <= st - 2 < U:
                        u = st - 2
                        act.wait_ge(full, full_after(("av", li, u)))
                        if u >= 2:
                            act.wait_ge(full, full_after(("oT", li, u - 2)))
                        b = slice(u % 2, u % 2 + 1)
                        if u >= 2:
                            act.wait_ge(o_rs.sem, o_rs.after((li, u - 2)))
                        act.activation(ON[:, u % 2, :], bank(("av", li, u), P), ACT.Square,
                                       scale=1.0 / math.sqrt(128.0), accum_out=ossq[:, b]).then_inc(o_sq.sem, 1)
                    if 0 <= st - 3 < U:
                        u = st - 3
                        t, h = au[u]
                        act.wait_ge(full, full_after(("oT", li, u)))
                        act.activation(MT[:, h, cols_of(t)], bank(("oT", li, u), P), ACT.Copy,
                                                           scale=pcol(("subln", li))).then_inc(taken_of(("oT", li, u)), 1)
                    yield

            def split_rows(X, key, n, r0, nrow, lo, last_read=None):
                b = 4 * (n % 2)
                if n == 0 and last_read is not None:
                    act.wait_ge(full, full_after(last_read))
                elif n >= 2:
                    act.wait_ge(*read_at[item[FS_KEYS[FS_KEYS.index(key) - 2]]])
                for k in range(0, nrow, 2):
                    act.activation(HH[:, b + k:b + k + 2, lo:lo + X.shape[2]], X[:, r0 + k:r0 + k + 2, :], ACT.Copy).then_inc(part_hi.sem, 1)

            def ffn(li):
                norm(("n2", li))
                lo = 0 if li == 0 else 256
                w = 512 - lo
                keys = [(("w_down", li, c, r0), r0, nrow) for c in range(2) for r0, nrow in DOWN]

                def part_rows(n):
                    key, r0, nrow = keys[n]
                    act.wait_ge(f_out.sem, f_out.after((li, r0 + nrow - 1)))
                    split_rows(HF[:, :, lo:512], key, n, r0, nrow, lo, ("u", li, FT - 1, 1))

                for f2 in range(FT // 2):
                    for a in range(2):
                        for j in range(2):
                            f = 2 * f2 + j
                            if f2:
                                act.wait_ge(f_out.sem, f_out.after((li, f - 2)))
                            key = ("u", li, f, a)
                            act.wait_ge(full, full_after(key))
                            act.activation(FC[:, j, a, 0:w], bank(key, w), ACT.Identity, scale=pcol(("cw", li, 1), a * FT + f),
                                           bias=pcol(("cb", li), a * FT + f)).then_inc(f_mid.sem, 1)
                        for lj in fill(("w_up", li), 2 * f2 + a):
                            ada(*lj)
                            split_next()
                        if 2 * f2 + a < FT - 1:
                            split_next()
                    if 2 * f2 + 2 == FT:
                        for n in range(2):
                            part_rows(n)
                    for j in range(2):
                        f = 2 * f2 + j
                        act.wait_ge(*taken_after(("u", li, f, 0)))
                        act.activation(FC[:, j, 2, 0:w], FC[:, j, 0, 0:w], ACT.Silu).then_inc(f_exp.sem, 1)
                split_next()
                for n in range(2, 2 * len(DOWN)):
                    part_rows(n)
                    split_next()

            for c in range((NCOL + P - 1) // P):
                n = min(P, NCOL - c * P)
                evict(("cols", c), cols[:, c * P:c * P + n], n)
                if c == 0:
                    act.wait_ge(*taken_after(("cols", 0)))
                    act.activation(csil.rearrange("p s k -> p (s k)"), cols[:, 0:16], ACT.Silu).then_inc(s_silu, 1)
            act.wait_ge(lam_sum, 2 * DEPTH)
            act.activation(lam2, lam2, ACT.Exp).then_inc(lam_exp, 1)
            for n in range(HIGH):
                split_next()
            for n, lj in enumerate(FILL["start"][0]):
                ada(*lj)
                split_next()
                if 4 <= n < 8:
                    squares(("n1", 0), [n - 4])
            for li in range(DEPTH):
                norm(("n1", li))
                w_in(li)
                fourier(li)
                weave(hgrn(li), attention(li), mixer_steps(li))
                merge_rec(li)
                act.wait_ge(*taken_after(("oT", li, len(att_units(li)) - 1)))
                for n, r0 in enumerate((0, 4)):
                    lo = 0 if li == 0 else 256
                    split_rows(MT[:, :, lo:512], ("w_out", li, 0, r0), n, r0, 4, lo)
                for n in range(2):
                    split_next()
                ffn(li)
            norm(("fn", 0))
            norm(("cn", 0))
            for e2 in range(ET // 2):
                for q in C_IN:
                    for j in range(2):
                        e = 2 * e2 + j
                        key = ("c", e, q)
                        if q in (1, 3):
                            act.wait_ge(full, full_after(key))
                        if q == 1:
                            if e >= 2:
                                act.wait_ge(c_out.sem, c_out.after(e - 2))
                            act.activation(CC[:, j, 0, :], bank(key, 256), ACT.Copy).then_inc(taken_of(key), 1)
                        if q == 3:
                            act.activation(CC[:, j, 1, :], bank(key, 256), ACT.Silu).then_inc(taken_of(key), 1)
                    if (e2, q) != (ET // 2 - 1, C_IN[-1]):
                        split_next()
            for n, (c, (r0, nrow)) in enumerate([(c, part) for c in range(2) for part in C_OUT]):
                act.wait_ge(c_out.sem, c_out.after(r0 + nrow - 1))
                split_rows(YC, ("c_out", c, r0), n, r0, nrow, 256, ("c", ET - 1, 0))
                if n:
                    split_next()
            norm(("an", 0))
            pend = []

            def scales_of(four):
                for key in four:
                    n = QKEYS.index(key)
                    act.wait_ge(full, full_after(("ms", key)))
                    if n >= 4:
                        act.wait_ge(q_done.sem, q_done.after(QKEYS[n - 4]))
                    act.activation(RQ[:, n % 4, :], bank(("ms", key)), ACT.Ln, bias=EPS_COL).then_inc(taken_of(("ms", key)), 1)
                for key in four:
                    n = QKEYS.index(key)
                    act.wait_ge(*taken_after(("ms", key)))
                    act.activation(RQ[:, n % 4, :], RQ[:, n % 4, :], ACT.Exp, scale=-0.5).then_inc(q_rs.sem, 1)

            for g, a, j in A_IN:
                if g == "z":
                    key = ("z2", j)
                    act.wait_ge(full, full_after(key))
                    act.wait_ge(s_vec, 16)
                    act.activation(ZS[:, 2 * j:2 * j + 2, :], bank(key).rearrange("p (m n) -> p m n", m=2),
                                   ACT.Silu).then_inc(taken_of(key), 1)
                elif a < 2:
                    key = (g, a, j)
                    n = QKEYS.index(key)
                    act.wait_ge(full, full_after(("qk", key)))
                    if n >= 2:
                        act.wait_ge(full, full_after(("ms", QKEYS[n - 2])))
                    act.activation(SQ[:, n % 2, :], bank(("qk", key)), ACT.Square, scale=0.125).then_inc(q_sq.sem, 1)
                    pend.append(key)
                    if len(pend) == 5:
                        scales_of(pend[:4])
                        pend = pend[4:]
                elif j == 0 and pend:
                    scales_of(pend)
                    pend = []
                elif j % 2:
                    for t in range(2):
                        evict(("v2", g, j // 2, t), V2[:, g, t, j // 2 * 512:(j // 2 + 1) * 512], 512)
                if (g, j) != ("z", 3):
                    split_next()
            for st in range(len(BU) + 2):
                if st < len(BU):
                    u = st
                    h, t = BU[u]
                    n = (t + 1) * P
                    act.wait_ge(b_max.sem, b_max.after(BU[u]))
                    act.activation(LG[:, u % 3, :, 0:n], LG[:, u % 3, :, 0:n], ACT.Exp,
                                                     bias=bmax[:, u % 3:u % 3 + 1], accum_out=bsum[:, u % 3:u % 3 + 1]).then_inc(b_exp.sem, 1)
                if 0 <= st - 2:
                    u = st - 2
                    h, t = BU[u]
                    n = (t + 1) * P
                    key = ("eT", u, 0)
                    act.wait_ge(full, full_after(key))
                    if u >= 2:
                        act.wait_ge(full, full_after(("o2", u - 2)))
                    act.activation(E3[:, u % 2, 0:512].rearrange("p (g n) -> p g n", g=2)[:, :, 0:n],
                                             bank(key).rearrange("p (g n) -> p g n", g=2)[:, :, 0:n], ACT.Copy).then_inc(taken_of(key), 1)
            for n, r0 in enumerate((0, 4)):
                act.wait_ge(*taken_after(("yT", KT - 1)))
                split_rows(YT2, ("a_out", 0, r0), n, r0, 4, 256)
            for n in range(2):
                split_next()

        @block.vector
        def _(dve):
            line = Line()

            next_slot = [0]

            def split_next():
                n = next_slot[0]
                if n == len(plan):
                    return
                next_slot[0] += 1
                used = plan[n][1].shape[1] * plan[n][1].shape[2]
                dve.wait_ge(hi_in.sem, hi_in.after(split_keys[n]))
                dve.tensor_tensor(slot(n, ring_lo)[:, 0:used], slot(n)[:, 0:used], hi_slot(n)[:, 0:used], ALU.subtract).then_inc(lo_in.sem, 1)

            def scale_rows(N, t):
                dve.wait_ge(row_scale.sem, row_scale.after((N, t)))
                if N == ("n1", 0) and t == 2:
                    dve.wait_ge(squared.sem, squared.after((N, NT - 1)))
                if N == ("fn", 0):
                    if t == 2:
                        dve.wait_ge(s_fw, 16)
                    dve.scalar_tensor_tensor(RES[:, t, :], RES[:, t, :], rstd[:, t:t + 1], GB[:, 0, :],
                                             ALU.mult, ALU.mult).then_inc(res_new.sem, 1)
                else:
                    dve.tensor_scalar(XS[:, t, :], RES[:, t, :], rstd[:, t:t + 1], None, ALU.mult).then_inc(scaled.sem, 1)

            def norm(N):
                m = {"n1": 0, "n2": 2}.get(N[0])
                if m is not None:
                    dve.tensor_scalar(nscale, modt[:, N[1], m + 1, :, :], 1.0, None, ALU.add).then_inc(vector_step, line.one())
                    dve.wait_ge(vector_step, line.n)
                    w8 = cols[:, col[N]:col[N] + 8].unsqueeze(2).to_broadcast([P, KT, 2])
                    dve.tensor_tensor(nscale, nscale, w8, ALU.mult).then_inc(vector_step, line.one())
                    dve.wait_ge(vector_step, line.n)
                for t in norm_tiles(N):
                    if N != ("n1", 0) or t == NT - 1:
                        scale_rows(N, t)
                if N == ("fn", 0):
                    return
                lo = 0 if 0 in norm_tiles(N) else 256
                for k in range(KT):
                    v = n_t[:, k % 2, lo:512]
                    dve.wait_ge(*taken_after((N, k)))
                    dve.tensor_copy(HH[:, k, lo:512], v).then_inc(vector_step, line.one())
                    dve.wait_ge(vector_step, line.n)
                    dve.tensor_tensor(HL[:, k, lo:512], v, HH[:, k, lo:512], ALU.subtract).then_inc(ht_done.sem, 1)
                for n in range(owed(N)):
                    split_next()

            seen_gb = [0]

            def ada(li, n):
                key, sec, q = ("ada", li, n), n // 4, n % 4
                if sec in GATES:
                    if q == 0:
                        seen_gb[0] += 32 if li == 0 else 16
                        dve.wait_ge(s_gb, seen_gb[0])
                    for s in range(2 if li == 0 else 1):
                        k2 = ("gb", li, n, s)
                        dve.wait_ge(full, full_after(k2))
                        d = GB[:, s, q * 256:(q + 1) * 256]
                        dve.tensor_tensor(d, bank(k2, 256), d, ALU.add).then_inc(taken_of(k2), 1)
                else:
                    m = {0: 0, 1: 1, 3: 2, 4: 3}[sec]
                    key = ("mc", li, n)
                    dve.wait_ge(full, full_after(key))
                    c0 = col["b_ada", li] + 2 * n
                    bb = cols[:, c0:c0 + 2].unsqueeze(2).to_broadcast([P, 2, 2])
                    dve.tensor_tensor(modt[:, li, m, 2 * q:2 * q + 2, :], bank(key, 4).rearrange("p (k s) -> p k s", s=2), bb,
                                      ALU.add).then_inc(taken_of(key), 1)
                    dve.wait_ge(*taken_after(key))

            def w_in(li):
                if li:
                    dve.wait_ge(s_lb, 16)
                    dve.tensor_tensor(lb_rows[:, 0, :], lb_rows[:, 1, :], lb_rows[:, 0, :], ALU.subtract).then_inc(lb_abs, 1)
                    dve.wait_ge(lb_exp, 1)
                    dve.scalar_tensor_tensor(lb_rows[:, 1, :], lb_rows[:, 0, :], 0.0, lb_rows[:, 1, :], ALU.min,
                                             ALU.subtract).then_inc(vector_step, line.one())
                    dve.wait_ge(vector_step, line.n)
                    dve.tensor_tensor(lb_rows[:, 0, :], lb_rows[:, 1, :], lb_rows[:, 0, :], ALU.subtract).then_inc(vector_step, line.one())
                    dve.wait_ge(vector_step, line.n)
                for n, (name, h, _) in enumerate(W_IN):
                    for lj in fill(("w_in", li), n):
                        for before in spread(("w_in", li), lj):
                            ada(*before)
                    for lj in last_spread(("w_in", li), n):
                        ada(*lj)
                    if n == 3 and li == 0:
                        dve.wait_ge(s_const, 32)
                        dve.tensor_copy(masks[:, :], arena[:, 0:2 * LEVELS * P]).then_inc(s_mask, 1)
                    if n == 3:
                        for name2, X in (("qa", QA), ("ka", KA)):
                            for hd in range(NH_A):
                                key = ("rot", name2, li, hd)
                                dve.wait_ge(full, full_after(key))
                                b = hd % 2
                                dve.tensor_tensor(rope_t[:, b, :], bank(key, 256), sinT, ALU.mult).then_inc(vector_step, line.one())
                                dve.tensor_tensor(X[:, hd, 256:512], X[:, hd, 256:512], cosT, ALU.mult).then_inc(vector_step, line.one())
                                dve.wait_ge(vector_step, line.n)
                                dve.tensor_tensor(X[:, hd, 256:512], X[:, hd, 256:512], rope_t[:, b, :], ALU.add).then_inc(taken_of(key), 1)
                    for _ in range(len(fill(("w_in", li), n)) + (n < len(W_IN) - 1)):
                        split_next()
                dve.wait_ge(full, full_after(("zz", li, NT - 1)))
                for t in range(NT):
                    key = ("zz", li, t)
                    z = bank(key)
                    dve.wait_ge(z_soft.sem, z_soft.after((li, t)))
                    done = vector_step if li else g_ready.sem
                    dve.scalar_tensor_tensor(GL[:, t, :], z, 0.0, SP[:, t, :], ALU.min,
                                             ALU.subtract).then_inc(done, line.one() if li else 1)
                    if li:
                        dve.wait_ge(vector_step, line.n)
                        dve.tensor_tensor(GL[:, t, :], GL[:, t, :], lb_rows[:, 0, :], ALU.add).then_inc(vector_step, line.one())
                        dve.wait_ge(vector_step, line.n)
                        dve.tensor_tensor(BG[:, t, :], GL[:, t, :], lb_rows[:, 1, :], ALU.subtract).then_inc(b_gap.sem, 1)
                    else:
                        dve.wait_ge(g_ready.sem, g_ready.after((li, t)))
                    dve.tensor_tensor(KTOK[:, t, :], GL[:, t, :], z, ALU.subtract).then_inc(taken_of(key), 1)
                    if li:
                        dve.tensor_tensor(GL[:, t, :], GL[:, t, :], lb_rows[:, 1, :], ALU.max).then_inc(vector_step, line.one())
                if li:
                    dve.wait_ge(vector_step, line.n)
                    for t in range(NT):
                        dve.wait_ge(b_soft.sem, b_soft.after((li, t)))
                        dve.tensor_tensor(GL[:, t, :], GL[:, t, :], BG[:, t, :], ALU.add).then_inc(g_ready.sem, 1)
                split_next()

            def hgrn(li):
                un = units(li)

                def gates(i):
                    d, t = un[i]
                    b = i % 2
                    if is_full(li, i):
                        key = ("kT", li, i)
                        dve.wait_ge(full, full_after(key))
                        dve.tensor_copy(KTT[:, b, :, :], bank(key, 256).rearrange("p (q n) -> p q n", q=2)).then_inc(taken_of(key), 1)
                        dve.wait_ge(*taken_after(key))
                        for p in range(2):
                            for hf in range(2):
                                dve.wait_ge(*taken_after(("E", li, i, p, hf)))
                        if i == (0 if li == 0 else 4):
                            for p in range(2):
                                dve.wait_ge(*taken_after(("qh", li, p)))
                        q = QH[:, :, cols_of(t)]
                        for level in range(1, LEVELS):
                            B = level_block(level)
                            for hf in range(2):
                                src = q if hf == 1 - d else KTT[:, b, :, :]
                                for p in range(2):
                                    x = XE[b][:, p, level - 1, :].rearrange("p (m h n) -> p m h n", h=2, n=B)[:, :, hf, :]
                                    y = src[:, p, :].rearrange("p (m h n) -> p m h n", h=2, n=B)[:, :, hf, :]
                                    dve.tensor_tensor(x, x, y, ALU.mult).then_inc(vector_step, line.one())
                        dve.tensor_tensor(XE[b][:, :, 7, :], XE[b][:, :, 7, :], q, ALU.mult).then_inc(z_ready.sem, 1)
                    if i < 6:
                        dve.wait_ge(*taken_after(("suf", li, i)))
                        if i >= 2:
                            dve.wait_ge(full, full_after(("SU", li, i - 2)))
                        dve.tensor_tensor(KD[:, b, :], KTOK[:, t, d * 256:(d + 1) * 256], SE[:, b, 0:256], ALU.mult).then_inc(kd_ready.sem, 1)

                def apply(i):
                    d, t = un[i]
                    b = i % 2
                    yield True
                    if is_full(li, i):
                        for lp in range(4):
                            dve.wait_ge(full, full_after(("S", li, i, lp, 1)))
                            for lv in range(2):
                                m = MASK[:, d, 2 * lp + lv, :].unsqueeze(1).to_broadcast([P, 2, P])
                                for par in range(2):
                                    key = ("S", li, i, lp, par)
                                    ins = dve.copy_predicated(ACC[:, d, par, :, :], m,
                                                              bank(key)[:, lv * 256:(lv + 1) * 256].rearrange("p (h n) -> p h n", h=2))
                                    if lv:
                                        ins.then_inc(taken_of(key), 1)
                                    else:
                                        ins.then_inc(vector_step, line.one())
                                dve.wait_ge(vector_step, line.n)
                            for par in range(2):
                                dve.wait_ge(*taken_after(("S", li, i, lp, par)))
                    yield
                    if is_full(li, i):
                        for par in range(2):
                            key = ("O", li, i, par)
                            dve.wait_ge(full, full_after(key))
                            o = OREC[:, t, :].rearrange("p (q a n) -> p q a n", q=2, a=2)[:, :, par, :]
                            src = bank(key, P).rearrange("p (q n) -> p q n", q=2)
                            if (d, t) in ((0, 0), (1, 1), (0, 2), (1, 3)):
                                dve.tensor_copy(o, src).then_inc(taken_of(key), 1)
                            else:
                                dve.tensor_tensor(o, src, o, ALU.add).then_inc(taken_of(key), 1)
                    if i < 6:
                        key = ("SU", li, i)
                        dve.wait_ge(full, full_after(key))
                        for p in range(2):
                            for hh in range(2):
                                r = slice(64 * hh, 64 * hh + 64)
                                dst = ST[r, d, p, :]
                                new = bank(key)[r, p * P + hh * 64:p * P + hh * 64 + 64]
                                if i < 2:
                                    ins = dve.tensor_copy(dst, new)
                                else:
                                    ins = dve.scalar_tensor_tensor(dst, dst, SE[r, b, 256 + p:257 + p], new, ALU.mult, ALU.add)
                                if p == 1 and hh == 1:
                                    ins.then_inc(taken_of(key), 1)
                                else:
                                    ins.then_inc(vector_step, line.one())
                        dve.wait_ge(*taken_after(key))

                dve.wait_ge(s_mask, 1)
                for s in ((0, 1) if li == 0 else (1,)):
                    dve.wait_ge(full, full_after(("f3", li, s)))
                dve.memset(scr[:, 2560:3584], 0.0).then_inc(vector_step, line.one())
                dve.wait_ge(vector_step, line.n)
                gates(0)
                for i in range(8):
                    if i + 1 < 8:
                        gates(i + 1)
                    yield from apply(i)
                    yield
                live = range(NT) if li == 0 else range(2, NT)
                for par in range(2):
                    dve.wait_ge(*taken_after(("O", li, 7, par)))
                for t in live:
                    o = OREC[:, t, :]
                    o4 = o.rearrange("p (h n) -> p h n", h=4)
                    tf = scr[:, 0:256]
                    dve.scalar_tensor_tensor(tf, o, 1.0 / 64.0, o, ALU.mult, ALU.mult).then_inc(vector_step, line.one())
                    dve.wait_ge(vector_step, line.n)
                    dve.tensor_reduce(hssq[:, t, :], tf.rearrange("p (h n) -> p h n", h=4), AX.X, ALU.add).then_inc(rec_sum.sem, 1)
                    dve.wait_ge(rec_sum.sem, rec_sum.after((li, t)))
                yield
                for t in live:
                    o = OREC[:, t, :]
                    o4 = o.rearrange("p (h n) -> p h n", h=4)
                    dve.wait_ge(og_exp.sem, og_exp.after((li, t)))
                    dve.tensor_tensor(o4, o4, hrstd[:, t, :].unsqueeze(2).to_broadcast([P, 4, 64]), ALU.mult).then_inc(vector_step, line.one())
                    dve.wait_ge(vector_step, line.n)
                    dve.tensor_tensor(o4, o4, hw[:, li, :].unsqueeze(1).to_broadcast([P, 4, 64]), ALU.mult).then_inc(vector_step, line.one())
                    dve.wait_ge(vector_step, line.n)
                    dve.tensor_tensor(o, o, GH[:, t, :], ALU.mult).then_inc(rec_ready.sem, 1)
                    if t % 2:
                        yield
                for _ in range(3 - len(live) // 2):
                    yield

            def combine(li):
                for u, (t, h) in enumerate(att_units(li)):
                    n = 256 if t < 2 else 512
                    b = u % 2
                    dve.wait_ge(a_max.sem, a_max.after((li, u)))
                    for c in range(2):
                        dve.wait_ge(*taken_after(("s", li, u, c)))
                    dve.reciprocal(arec[:, b, :], asum[:, b, :]).then_inc(vector_step, line.one())
                    dve.wait_ge(vector_step, line.n)
                    dve.tensor_tensor(arec[:, b, 1:2], arec[:, b, 1:2], neglam[:, li:li + 1], ALU.mult).then_inc(vector_step, line.one())
                    dve.tensor_scalar(E2[:, b, 0, 0:n], E2[:, b, 0, 0:n], arec[:, b, 0:1], None, ALU.mult).then_inc(vector_step, line.one())
                    dve.wait_ge(vector_step, line.n)
                    dve.scalar_tensor_tensor(E2[:, b, 0, 0:n], E2[:, b, 1, 0:n], arec[:, b, 1:2],
                                                                   E2[:, b, 0, 0:n], ALU.mult, ALU.add).then_inc(a_ready.sem, 1)
                    yield

            def attention(li):
                au = att_units(li)
                U = len(au)
                lam_init = 0.8 - 0.6 * math.exp(-0.3 * li)
                for st in range(U + 3):
                    if st < U:
                        u = st
                        t, h = au[u]
                        n = 256 if t < 2 else 512
                        b = u % 2
                        for c in range(2):
                            dve.wait_ge(full, full_after(("s", li, u, c)))
                            dve.tensor_reduce(arec[:, b, c:c + 1], bank(("s", li, u, c), n), AX.X, ALU.max).then_inc(vector_step, line.one())
                        dve.wait_ge(vector_step, line.n)
                        dve.tensor_scalar(amax[:, b, :], arec[:, b, :], -0.125, None, ALU.mult).then_inc(a_max.sem, 1)
                    if 0 <= st - 2 < U:
                        u = st - 2
                        b = u % 2
                        dve.wait_ge(o_rs.sem, o_rs.after((li, u)))
                        dve.tensor_scalar(ON[:, b, :], bank(("av", li, u), P), orstd[:, b:b + 1],
                                                              1.0 - lam_init, ALU.mult, ALU.mult).then_inc(taken_of(("av", li, u)), 1)
                    yield

            def add_out(name, live, c, gated, signal=None):
                for i, t in enumerate(live):
                    key = (*name, c, t)
                    dve.wait_ge(full, full_after(key))
                    r = RES[:, t, c * 512:(c + 1) * 512]
                    if not gated:
                        dve.tensor_tensor(r, bank(key), r, ALU.add).then_inc(taken_of(key), 1)
                        continue
                    if i >= 2:
                        dve.wait_ge(vector_step, line.n)
                    tmp = wo_t[:, i % 2, :]
                    dve.tensor_tensor(tmp, bank(key), GB[:, stream_of(t), c * 512:(c + 1) * 512], ALU.mult).then_inc(taken_of(key), 1)
                    dve.wait_ge(*taken_after(key))
                    if signal is not None:
                        dve.tensor_tensor(r, r, tmp, ALU.add).then_inc(signal.sem, 1)
                    else:
                        dve.tensor_tensor(r, r, tmp, ALU.add).then_inc(vector_step, line.one())

            def split_rows(X, key, n, r0, nrow, lo):
                b = 4 * (n % 2)
                c = slice(lo, lo + X.shape[2])
                for k in range(0, nrow, 2):
                    dve.wait_ge(part_hi.sem, part_hi.after((key, k)))
                    dve.tensor_tensor(HL[:, b + k:b + k + 2, c], X[:, r0 + k:r0 + k + 2, :], HH[:, b + k:b + k + 2, c],
                                      ALU.subtract).then_inc(part_lo.sem, 1)

            def ffn(li):
                norm(("n2", li))
                lo = 0 if li == 0 else 256
                live = range(NT) if li == 0 else range(2, NT)
                w = 512 - lo
                ns = w // 256

                def conv(f, a):
                    key, j = ("u", li, f, a), f % 2
                    dve.wait_ge(f_mid.sem, f_mid.after((li, f, a)))
                    u3 = bank(key, w).rearrange("p (s n) -> p s n", s=ns)
                    o3 = FC[:, j, a, 0:w].rearrange("p (s n) -> p s n", s=ns)
                    dve.scalar_tensor_tensor(o3[:, :, 1:256], u3[:, :, 0:255], pcol(("cw", li, 0), a * FT + f),
                                             o3[:, :, 1:256], ALU.mult, ALU.add).then_inc(vector_step, line.one())
                    dve.wait_ge(vector_step, line.n)
                    dve.scalar_tensor_tensor(o3[:, :, 0:255], u3[:, :, 1:256], pcol(("cw", li, 2), a * FT + f),
                                             o3[:, :, 0:255], ALU.mult, ALU.add).then_inc(taken_of(key), 1)
                    dve.wait_ge(*taken_after(key))

                keys = [(("w_down", li, c, r0), r0, nrow) for c in range(2) for r0, nrow in DOWN]

                def part_rows(n):
                    key, r0, nrow = keys[n]
                    split_rows(HF[:, :, lo:512], key, n, r0, nrow, lo)

                for f2 in range(FT // 2):
                    for a in range(2):
                        for j in range(2):
                            conv(2 * f2 + j, a)
                        for lj in fill(("w_up", li), 2 * f2 + a):
                            for before in spread(("w_up", li), lj):
                                ada(*before)
                            split_next()
                        for lj in last_spread(("w_up", li), 2 * f2 + a):
                            ada(*lj)
                        if 2 * f2 + a < FT - 1:
                            split_next()
                    if 2 * f2 + 2 == FT:
                        for n in range(2):
                            part_rows(n)
                    for j in range(2):
                        f = 2 * f2 + j
                        dve.wait_ge(f_exp.sem, f_exp.after((li, f)))
                        dve.tensor_tensor(HF[:, f, lo:512], FC[:, j, 2, 0:w], FC[:, j, 1, 0:w], ALU.mult).then_inc(f_out.sem, 1)
                split_next()
                for n in range(2, 2 * len(DOWN)):
                    part_rows(n)
                    split_next()
                    if n == len(DOWN) + 2:
                        add_out(("w_down", li), live, 0, True)
                add_out(("w_down", li), live, 1, True, res_new)

            dve.memset(EPS_COL, EPS).then_inc(s_eps, 1)
            dve.wait_ge(s_small, 16 * len(small_ins))
            for li in range(DEPTH):
                for a in range(2):
                    dve.tensor_tensor_reduce(out=lam_tmp, in0=lam_rows[:, li, 2 * a, :], in1=lam_rows[:, li, 2 * a + 1, :],
                                             scale=1.0, scalar=0.0, op0=ALU.mult, op1=ALU.add,
                                             accum_out=lam2[:, li, a:a + 1]).then_inc(lam_sum, 1)
                    dve.wait_ge(lam_sum, 2 * li + a + 1)
            both = csil.rearrange("p s k -> p k s")
            dve.wait_ge(s_silu, 1)
            dve.tensor_copy(cond[:, :, 0:2], both).then_inc(vector_step, line.one())
            dve.wait_ge(vector_step, line.n)
            dve.tensor_tensor(cond[:, :, 2:4], both, cond[:, :, 0:2], ALU.subtract).then_inc(c_ready, 1)
            for n in range(HIGH):
                split_next()
            dve.wait_ge(lam_exp, 1)
            for li in range(DEPTH):
                dve.tensor_tensor(neglam[:, li:li + 1], lam2[:, li, 1:2], lam2[:, li, 0:1], ALU.subtract).then_inc(vector_step, line.one())
                dve.wait_ge(vector_step, line.n)
                dve.tensor_scalar(neglam[:, li:li + 1], neglam[:, li:li + 1], -(0.8 - 0.6 * math.exp(-0.3 * li)), None, ALU.add).then_inc(vector_step, line.one())
            for c in range((NCOL + P - 1) // P):
                dve.wait_ge(*taken_after(("cols", c)))
            for n in range(len(FILL["start"][0])):
                for lj in fill("start", n):
                    split_next()
                    for before in spread("start", lj):
                        ada(*before)
                if n >= 7:
                    scale_rows(("n1", 0), n - 7)
                for lj in last_spread("start", n):
                    ada(*lj)
            for li in range(DEPTH):
                norm(("n1", li))
                w_in(li)
                weave(hgrn(li), attention(li), mixer_steps(li), combine(li))
                live = range(NT) if li == 0 else range(2, NT)
                lo = 0 if li == 0 else 256
                for n, r0 in enumerate((0, 4)):
                    split_rows(MT[:, :, lo:512], ("w_out", li, 0, r0), n, r0, 4, lo)
                for n in range(2):
                    split_next()
                add_out(("w_out", li), live, 0, True)
                add_out(("w_out", li), live, 1, True, res_new)
                ffn(li)
            norm(("fn", 0))
            norm(("cn", 0))
            for e2 in range(ET // 2):
                for q in C_IN:
                    for j in range(2):
                        e = 2 * e2 + j
                        key = ("c", e, q)
                        v, s_, cv = CC[:, j, 0, :], CC[:, j, 1, :], CC[:, j, 2, :]
                        if q == 2:
                            dve.wait_ge(*taken_after(("c", e, 1)))
                            dve.wait_ge(full, full_after(key))
                            dve.tensor_tensor(v, bank(key, 256), v, ALU.mult).then_inc(taken_of(key), 1)
                            dve.wait_ge(*taken_after(key))
                            dve.tensor_scalar(cv, v, pcol(("cw2", 2), e), None, ALU.mult).then_inc(vector_step, line.one())
                            for d, tap in ((1, 1), (2, 0)):
                                dve.wait_ge(vector_step, line.n)
                                dve.scalar_tensor_tensor(cv[:, d:256], v[:, 0:256 - d], pcol(("cw2", tap), e), cv[:, d:256],
                                                         ALU.mult, ALU.add).then_inc(vector_step, line.one())
                        if q == 0:
                            dve.wait_ge(*taken_after(("c", e, 3)))
                            dve.wait_ge(full, full_after(key))
                            dve.tensor_tensor(s_, bank(key, 256), s_, ALU.mult).then_inc(taken_of(key), 1)
                            dve.wait_ge(*taken_after(key))
                            dve.tensor_tensor(YC[:, e, :], s_, cv, ALU.mult).then_inc(c_out.sem, 1)
                    if (e2, q) != (ET // 2 - 1, C_IN[-1]):
                        split_next()
            for n, (c, (r0, nrow)) in enumerate([(c, part) for c in range(2) for part in C_OUT]):
                split_rows(YC, ("c_out", c, r0), n, r0, nrow, 256)
                if n:
                    split_next()
                if n == len(C_OUT) + 2:
                    add_out(("c_out",), (2, 3), 0, False)
            add_out(("c_out",), (2, 3), 1, False)
            dve.wait_ge(full, full_after("vec"))
            dve.tensor_copy(vec, bank("vec")[0:NG * NH, 0:384]).then_inc(taken_of("vec"), 1)
            norm(("an", 0))
            pend = []

            def q_place(key):
                g, a, j = key
                d = QK2[:, g, a, 2 * j:2 * j + 2, :].rearrange("p m (t n) -> p (m t) n", t=2)
                return backwards(d) if a == 0 else d

            def scale(four):
                for key in four:
                    r = RQ[:, QKEYS.index(key) % 4, :].rearrange("p (m n) -> p m n", m=4)
                    dve.wait_ge(q_rs.sem, q_rs.after(key))
                    dve.tensor_tensor(q_place(key), q_place(key), r, ALU.mult).then_inc(q_done.sem, 1)

            for g, a, j in A_IN:
                if g != "z" and a < 2:
                    key = (g, a, j)
                    dve.wait_ge(q_sq.sem, q_sq.after(key))
                    dve.tensor_scalar(q_place(key), bank(("qk", key)).rearrange("p (m n) -> p m n", m=4), pcol(("gain", a), g), None,
                                      ALU.mult).then_inc(taken_of(("qk", key)), 1)
                    dve.wait_ge(*taken_after(("qk", key)))
                    pend.append(key)
                    if len(pend) == 5:
                        scale(pend[:4])
                        pend = pend[4:]
                elif a == 2 and j == 0:
                    scale(pend)
                    pend = []
                if (g, j) != ("z", 3):
                    split_next()
            for st in range(len(BU) + 3):
                if st < len(BU):
                    u = st
                    h, t = BU[u]
                    b = u % 3
                    n = (t + 1) * P
                    if t == 0:
                        dve.wait_ge(s_bias[h % 3], 16 * (h // 3 + 1))
                    if u >= 3:
                        dve.wait_ge(full, full_after(("eT", u - 3, 1)))
                    for part_, gs in enumerate(((0, 1), (2,))):
                        key = ("s2", u, part_)
                        dve.wait_ge(full, full_after(key))
                        g0, ng = gs[0], len(gs)
                        src = bank(key).rearrange("p (g n) -> p g n", g=2)[:, 0:ng, 0:n]
                        dve.scalar_tensor_tensor(LG[:, b, g0:g0 + ng, 0:n], src, 0.125,
                                                           BIAS[:, h % 3, g0:g0 + ng, 256 - n:256], ALU.mult, ALU.add).then_inc(taken_of(key), 1)
                        dve.wait_ge(*taken_after(key))
                    dve.tensor_reduce(bred[:, b:b + 1], LG[:, b, :, 0:n], AX.XY, ALU.max).then_inc(vector_step, line.one())
                    dve.wait_ge(vector_step, line.n)
                    dve.tensor_scalar(bmax[:, b:b + 1], bred[:, b:b + 1], -1.0, None, ALU.mult).then_inc(b_max.sem, 1)
                if 0 <= st - 2 < len(BU):
                    u = st - 2
                    h, t = BU[u]
                    n = (t + 1) * P
                    key = ("eT", u, 1)
                    dve.wait_ge(full, full_after(key))
                    if u >= 2:
                        dve.wait_ge(full, full_after(("o2", u - 2)))
                    dve.tensor_copy(E3[:, u % 2, 512:512 + n], bank(key, n)).then_inc(taken_of(key), 1)
                    b = u % 3
                    dve.wait_ge(b_exp.sem, b_exp.after(BU[u]))
                    if u >= 3:
                        dve.wait_ge(*taken_after(("o2", u - 3)))
                    dve.reciprocal(brec[:, b:b + 1], bsum[:, b:b + 1]).then_inc(vector_step, line.one())
                    dve.wait_ge(vector_step, line.n)
                if 0 <= st - 3:
                    u = st - 3
                    h, t = BU[u]
                    b = u % 3
                    dve.wait_ge(full, full_after(("o2", u)))
                    dve.tensor_scalar(Y2[:, t, h * 64:(h + 1) * 64], bank(("o2", u), 64), brec[:, b:b + 1], None,
                                                      ALU.mult).then_inc(taken_of(("o2", u)), 1)
            for k in range(KT):
                dve.wait_ge(full, full_after(("yT", k)))
                dve.tensor_tensor(YT2[:, k, :], bank(("yT", k), 256), ZS[:, k, :], ALU.mult).then_inc(taken_of(("yT", k)), 1)
            for n, r0 in enumerate((0, 4)):
                split_rows(YT2, ("a_out", 0, r0), n, r0, 4, 256)
            for n in range(2):
                split_next()
            for c in range(2):
                add_out(("a_out",), (2, 3), c, False)


_INS = ["x", "c", "ctx", "c_ctx", "w_ada", "b_ada", "norm1_w", "norm2_w", "w_in", "lam_qk", "subln_w", "lb_param",
        "hgrn_norm_w", "w_fnet", "w_out", "w_up", "conv_w", "conv_b", "w_down", "final_norm_w", "conv_norm_2",
        "conv_w_in_2", "conv_w_2", "conv_w_out_2", "attn_norm_2", "attn_w_in_2", "attn_q_gain_2", "attn_k_gain_2",
        "attn_w_out_2", "rel_bias_2"]


def kernel(**inputs):
    import numpy as _np
    import concourse.bacc as _bacc
    from concourse import mybir as _mybir
    from concourse.bass_utils import run_bass_kernel_spmd as _run

    nc = _bacc.Bacc("TRN2", target_bir_lowering=False, num_devices=1)
    arrays, args = {}, {}
    for name in _INS:
        a = _np.ascontiguousarray(inputs[name])
        arrays[f"in_{name}_dram"] = a
        args[name] = nc.dram_tensor(f"in_{name}_dram", a.shape, _mybir.dt.from_np(a.dtype), kind="ExternalInput").ap()
    consts = []
    for name, a in zip(("wide", "masks", "hot", "tab"), constants()):
        arrays[f"const_{name}_dram"] = a
        consts.append(nc.dram_tensor(f"const_{name}_dram", a.shape, _mybir.dt.from_np(a.dtype), kind="ExternalInput").ap())
    out = nc.dram_tensor("out_0_dram", (1, SEQ, DM), F32, kind="ExternalOutput").ap()
    program(nc, args, *consts, out)
    r = _run(nc, [arrays], core_ids=[0])
    return r.results[0]["out_0_dram"]
```
